# Optimizing a Trainium2 kernel written in Bass

```python
import jax
import jax.numpy as jnp
from jax import lax
import numpy as np
import math
import jax, jax.numpy as jnp

D_MODEL = 1024
BATCH = 1
SEQ = 256
DEPTH = 2

GRID_W = 64
CTX_LEN = 256
N_MIXERS = 3
CHUNK = 64
EPS = 1e-6
ALPHA = (2 * DEPTH) ** 0.25
BETA = (8 * DEPTH) ** -0.25

M_INNER = 2 * D_MODEL
M_HEADS = 4
M_DV = M_INNER // M_HEADS
M_DQK = M_DV // 2
M_CONV = 3

A_HEADS = 8
A_QLORA = 384
A_KVLORA = 256
A_DNOPE = 128
A_DROPE = 64
A_DV = 128
ROPE_BASE = 10000.0
Q_BLOCK = 128

G_HEADS = 4
G_DK = D_MODEL // (2 * G_HEADS)
G_DV = D_MODEL // G_HEADS
G_RANK = 16
G_TAU = 16.0

FFN_DIM = 2816
FFN_CONV = 3


def _count(kind):
    return len(range(kind, DEPTH, N_MIXERS))

def _layer_norm(x, g, b):
    xf = x.astype(jnp.float32)
    mu = jnp.mean(xf, -1, keepdims=True)
    var = jnp.mean(jnp.square(xf - mu), -1, keepdims=True)
    return ((xf - mu) * lax.rsqrt(var + EPS)).astype(x.dtype) * g + b

def _rms_norm(x, g):
    xf = x.astype(jnp.float32)
    return (xf * lax.rsqrt(jnp.mean(jnp.square(xf), -1, keepdims=True) + EPS)).astype(x.dtype) * g

def _head_rms_norm(x, g):
    B, T, H, d = x.shape
    return _rms_norm(x, g.reshape(H, d)).reshape(B, T, H * d)

def _dwconv(x, w, b):
    k = w.shape[0]
    y = lax.conv_general_dilated(x, w[:, None, :].astype(x.dtype), (1,), [(k // 2, k // 2)],
                                 dimension_numbers=("NWC", "WIO", "NWC"),
                                 feature_group_count=x.shape[-1])
    return y + b

def _modulation(cond, w, b):
    m = jax.nn.silu(cond) @ w + b
    return jnp.split(m[:, None, :], 6, axis=-1)

def _modulate(x, shift, scale):
    return x * (1 + scale) + shift

def _axial_angles(n_tokens):
    rows = n_tokens // GRID_W
    row = jnp.repeat(jnp.arange(rows, dtype=jnp.float32), GRID_W)
    col = jnp.tile(jnp.arange(GRID_W, dtype=jnp.float32), rows)
    n_freq = A_DROPE // 4
    inv_freq = ROPE_BASE ** (-jnp.arange(n_freq, dtype=jnp.float32) / n_freq)
    return row[:, None] * inv_freq, col[:, None] * inv_freq

def _rope_half(x, ang):
    x1, x2 = jnp.split(x, 2, axis=-1)
    cos = jnp.cos(ang).astype(x.dtype)
    sin = jnp.sin(ang).astype(x.dtype)
    return jnp.concatenate([x1 * cos - x2 * sin, x2 * cos + x1 * sin], -1)

def _axial_rope(x, ang_row, ang_col):
    xr, xc = jnp.split(x, 2, axis=-1)
    return jnp.concatenate([_rope_half(xr, ang_row), _rope_half(xc, ang_col)], -1)

def _time_flip(a, direction):
    return jnp.flip(a, axis=2) if direction == 1 else a

def _two_way(scan_fn, shared_c, gates_c, shared_l, gates_l, init):
    out_c, out_l = None, None
    for d in range(2):
        args_c = [_time_flip(a, d) for a in shared_c + tuple(g[d] for g in gates_c)]
        hc, state = scan_fn(*args_c, init)
        args_l = [_time_flip(a, d) for a in shared_l + tuple(g[d] for g in gates_l)]
        hl, _ = scan_fn(*args_l, state)
        hc, hl = _time_flip(hc, d), _time_flip(hl, d)
        out_c = hc if out_c is None else out_c + hc
        out_l = hl if out_l is None else out_l + hl
    return out_c, out_l

def _mlstm_chunk_scan(q, k, v, li, lf, state):
    B, H, T, _ = q.shape
    nc = T // CHUNK

    def chunks(a):
        a = a.astype(jnp.float32)
        return jnp.moveaxis(a.reshape(B, H, nc, CHUNK, *a.shape[3:]), 2, 0)

    tril = jnp.tril(jnp.ones((CHUNK, CHUNK), bool))

    def step(carry, inp):
        C, n, m = carry
        qc, kc, vc, ic, fc = inp
        b = jnp.cumsum(fc, axis=-1)
        dmat = jnp.where(tril, b[..., :, None] - b[..., None, :] + ic[..., None, :], -jnp.inf)
        inter = b + m[..., None]
        mj = jnp.maximum(inter, jnp.max(dmat, -1))
        wmat = jnp.exp(dmat - mj[..., None]) * jnp.einsum("bhjd,bhsd->bhjs", qc, kc)
        g = jnp.exp(inter - mj)
        num = g[..., None] * jnp.einsum("bhjd,bhde->bhje", qc, C) + jnp.einsum("bhjs,bhse->bhje", wmat, vc)
        den = g * jnp.einsum("bhjd,bhd->bhj", qc, n) + jnp.sum(wmat, -1)
        h = num / jnp.maximum(jnp.abs(den), jnp.exp(-mj))[..., None]
        bl = b[..., -1]
        ds = bl[..., None] - b + ic
        m_new = jnp.maximum(bl + m, jnp.max(ds, -1))
        kw = kc * jnp.exp(ds - m_new[..., None])[..., None]
        decay = jnp.exp(bl + m - m_new)
        C = decay[..., None, None] * C + jnp.einsum("bhsd,bhse->bhde", kw, vc)
        n = decay[..., None] * n + jnp.sum(kw, axis=2)
        return (C, n, m_new), h

    state, hs = lax.scan(step, state, tuple(chunks(a) for a in (q, k, v, li, lf)))
    return jnp.moveaxis(hs, 0, 2).reshape(B, H, T, -1), state

def _mlstm_inputs(h, w_up, conv_w, conv_b, w_qk, w_v, w_gates, b_gates):
    B, T, _ = h.shape
    x_m = h @ w_up
    x_c = jax.nn.silu(_dwconv(x_m, conv_w, conv_b))
    q, k = jnp.split(x_c @ w_qk, 2, axis=-1)
    q = q.reshape(B, T, M_HEADS, M_DQK).transpose(0, 2, 1, 3)
    k = k.reshape(B, T, M_HEADS, M_DQK).transpose(0, 2, 1, 3) * (M_DQK ** -0.5)
    v = (x_m @ w_v).reshape(B, T, M_HEADS, M_DV).transpose(0, 2, 1, 3)
    gates = jnp.einsum("bti,zig->zbgt", x_c, w_gates) + b_gates[:, None, :, None]
    li = gates[:, :, :M_HEADS].astype(jnp.float32)
    lf = jax.nn.log_sigmoid(gates[:, :, M_HEADS:].astype(jnp.float32))
    return (q, k, v), (li, lf)

def _mlstm_mixer(hl, hc, need_ctx, w_up, conv_w, conv_b, w_qk, w_v, w_gates, b_gates, w_og, norm_g, w_out):
    sh_l, gt_l = _mlstm_inputs(hl, w_up, conv_w, conv_b, w_qk, w_v, w_gates, b_gates)
    sh_c, gt_c = _mlstm_inputs(hc, w_up, conv_w, conv_b, w_qk, w_v, w_gates, b_gates)
    B = hl.shape[0]
    init = (jnp.zeros((B, M_HEADS, M_DQK, M_DV), jnp.float32),
            jnp.zeros((B, M_HEADS, M_DQK), jnp.float32),
            jnp.zeros((B, M_HEADS), jnp.float32))
    s_c, s_l = _two_way(_mlstm_chunk_scan, sh_c, gt_c, sh_l, gt_l, init)

    def out(h_in, s):
        Bq, T, _ = h_in.shape
        o = jax.nn.sigmoid(h_in @ w_og).reshape(Bq, T, M_HEADS, M_DV)
        hsum = o * s.transpose(0, 2, 1, 3).astype(h_in.dtype)
        return _head_rms_norm(hsum, norm_g) @ w_out

    return out(hl, s_l), (out(hc, s_c) if need_ctx else None)

def _mla_q(h, w_dq, q_norm, w_uq, ang):
    B, T, _ = h.shape
    q = (_rms_norm(h @ w_dq, q_norm) @ w_uq).reshape(B, T, A_HEADS, A_DNOPE + A_DROPE)
    if ang is None:
        return q
    q_nope, q_rope = jnp.split(q, [A_DNOPE], axis=-1)
    return jnp.concatenate([q_nope, _axial_rope(q_rope, ang[0][:, None], ang[1][:, None])], -1)

def _mla_kv(h, w_dkv, kv_norm, w_ukv, ang):
    B, T, _ = h.shape
    ckv, k_rope = jnp.split(h @ w_dkv, [A_KVLORA], axis=-1)
    if ang is not None:
        k_rope = _axial_rope(k_rope, ang[0], ang[1])
    kv = (_rms_norm(ckv, kv_norm) @ w_ukv).reshape(B, T, A_HEADS, A_DNOPE + A_DV)
    k_nope, v = jnp.split(kv, [A_DNOPE], axis=-1)
    k = jnp.concatenate([k_nope, jnp.broadcast_to(k_rope[:, :, None], (B, T, A_HEADS, A_DROPE))], -1)
    return k, v

def _attend(q, k, v):
    s = jnp.einsum("bqhd,bkhd->bhqk", q, k).astype(jnp.float32) * ((A_DNOPE + A_DROPE) ** -0.5)
    p = jax.nn.softmax(s, axis=-1).astype(v.dtype)
    return jnp.einsum("bhqk,bkhd->bqhd", p, v)

def _blocked_attend(q, k, v):
    B, T, H, d = q.shape
    qb = q.reshape(B, T // Q_BLOCK, Q_BLOCK, H, d).transpose(1, 0, 2, 3, 4)
    o = lax.map(lambda qi: _attend(qi, k, v), qb)
    return o.transpose(1, 0, 2, 3, 4).reshape(B, T, H, -1)

def _mla_mixer(hl, hc, need_ctx, ang, w_dq, q_norm, w_uq, w_dkv, kv_norm, w_ukv, w_out):
    B, T, _ = hl.shape
    kc, vc = _mla_kv(hc, w_dkv, kv_norm, w_ukv, None)
    kl, vl = _mla_kv(hl, w_dkv, kv_norm, w_ukv, ang)
    ql = _mla_q(hl, w_dq, q_norm, w_uq, ang)
    k_all = jnp.concatenate([kc, kl], axis=1)
    v_all = jnp.concatenate([vc, vl], axis=1)
    yl = _blocked_attend(ql, k_all, v_all).reshape(B, T, -1) @ w_out
    yc = None
    if need_ctx:
        qc = _mla_q(hc, w_dq, q_norm, w_uq, None)
        yc = _attend(qc, kc, vc).reshape(B, hc.shape[1], -1) @ w_out
    return yl, yc

def _gla_chunk_scan(q, k, v, la, S):
    B, H, T, _ = q.shape
    nc = T // CHUNK

    def chunks(a):
        a = a.astype(jnp.float32)
        return jnp.moveaxis(a.reshape(B, H, nc, CHUNK, *a.shape[3:]), 2, 0)

    tril = jnp.tril(jnp.ones((CHUNK, CHUNK), bool))

    def step(S, inp):
        qc, kc, vc, ac = inp
        b = jnp.cumsum(ac, axis=-2)
        inter = jnp.einsum("bhjd,bhde->bhje", qc * jnp.exp(b), S)
        rel = jnp.where(tril[:, :, None], b[:, :, :, None, :] - b[:, :, None, :, :], -jnp.inf)
        att = jnp.sum(qc[:, :, :, None, :] * kc[:, :, None, :, :] * jnp.exp(rel), axis=-1)
        o = inter + jnp.einsum("bhjs,bhse->bhje", att, vc)
        bl = b[:, :, -1:, :]
        S = jnp.exp(bl[:, :, 0, :, None]) * S + jnp.einsum("bhsd,bhse->bhde", kc * jnp.exp(bl - b), vc)
        return S, o

    S, os_ = lax.scan(step, S, tuple(chunks(a) for a in (q, k, v, la)))
    return jnp.moveaxis(os_, 0, 2).reshape(B, H, T, -1), S

def _gla_inputs(h, w_qk, w_v, w_a1, w_a2, b_a):
    B, T, _ = h.shape
    q, k = jnp.split(h @ w_qk, 2, axis=-1)
    q = q.reshape(B, T, G_HEADS, G_DK).transpose(0, 2, 1, 3) * (G_DK ** -0.5)
    k = k.reshape(B, T, G_HEADS, G_DK).transpose(0, 2, 1, 3)
    v = (h @ w_v).reshape(B, T, G_HEADS, G_DV).transpose(0, 2, 1, 3)
    z = jnp.einsum("zbtr,zrk->zbtk", jnp.einsum("btd,zdr->zbtr", h, w_a1), w_a2) + b_a[:, None, None, :]
    la = jax.nn.log_sigmoid(z.astype(jnp.float32)) / G_TAU
    la = la.reshape(2, B, T, G_HEADS, G_DK).transpose(0, 1, 3, 2, 4)
    return (q, k, v), (la,)

def _gla_mixer(hl, hc, need_ctx, w_qk, w_v, w_r, w_a1, w_a2, b_a, norm_g, w_out):
    sh_l, gt_l = _gla_inputs(hl, w_qk, w_v, w_a1, w_a2, b_a)
    sh_c, gt_c = _gla_inputs(hc, w_qk, w_v, w_a1, w_a2, b_a)
    init = jnp.zeros((hl.shape[0], G_HEADS, G_DK, G_DV), jnp.float32)
    s_c, s_l = _two_way(_gla_chunk_scan, sh_c, gt_c, sh_l, gt_l, init)

    def out(h_in, s):
        o = _head_rms_norm(s.transpose(0, 2, 1, 3).astype(h_in.dtype), norm_g)
        return (o * jax.nn.silu(h_in @ w_r)) @ w_out

    return out(hl, s_l), (out(hc, s_c) if need_ctx else None)

def _conv_ffn(h, w_in, conv_w, conv_b, w_out):
    gate, up = jnp.split(h @ w_in, 2, axis=-1)
    return (jax.nn.silu(_dwconv(gate, conv_w, conv_b)) * up) @ w_out

def first_inputs(seed: int = 0) -> dict:
    key = jax.random.key(seed)
    keys = iter(jax.random.split(key, 48))
    D = D_MODEL
    nA, nB, nC = _count(0), _count(1), _count(2)

    def normal(shape):
        return jax.random.normal(next(keys), shape, jnp.float32)

    def dense(shape, fan_in, scale=1.0):
        return normal(shape) * (scale * fan_in ** -0.5)

    def gain(shape):
        return 1.0 + 0.05 * normal(shape)

    def bias(shape, s=0.02):
        return s * normal(shape)

    f_bias = jnp.asarray(np.linspace(3.0, 6.0, M_HEADS), jnp.float32)
    w_ukv = dense((nB, A_KVLORA, A_HEADS, A_DNOPE + A_DV), A_KVLORA)
    w_ukv = w_ukv.at[..., A_DNOPE:].multiply(BETA).reshape(nB, A_KVLORA, A_HEADS * (A_DNOPE + A_DV))
    return {
        "x": normal((BATCH, SEQ, D)),
        "c": normal((BATCH, D)),
        "ctx": normal((BATCH, CTX_LEN, D)),
        "c_ctx": normal((D,)),
        "ada_w": dense((DEPTH, D, 6 * D), D, 0.5),
        "ada_b": bias((DEPTH, 6 * D)),
        "ln_g": gain((DEPTH, 2, D)),
        "ln_b": bias((DEPTH, 2, D)),
        "ffn_w_in": dense((DEPTH, D, 2 * FFN_DIM), D, BETA),
        "ffn_conv_w": dense((DEPTH, FFN_CONV, FFN_DIM), FFN_CONV),
        "ffn_conv_b": bias((DEPTH, FFN_DIM)),
        "ffn_w_out": dense((DEPTH, FFN_DIM, D), FFN_DIM, BETA),
        "m_w_up": dense((nA, D, M_INNER), D),
        "m_conv_w": dense((nA, M_CONV, M_INNER), M_CONV),
        "m_conv_b": bias((nA, M_INNER)),
        "m_w_qk": dense((nA, M_INNER, 2 * M_HEADS * M_DQK), M_INNER),
        "m_w_v": dense((nA, M_INNER, M_HEADS * M_DV), M_INNER, BETA),
        "m_w_gates": dense((nA, 2, M_INNER, 2 * M_HEADS), M_INNER, 0.5),
        "m_b_gates": jnp.concatenate([0.1 * normal((nA, 2, M_HEADS)),
                                      f_bias + 0.1 * normal((nA, 2, M_HEADS))], axis=-1),
        "m_w_og": dense((nA, D, M_HEADS * M_DV), D),
        "m_norm_g": gain((nA, M_HEADS * M_DV)),
        "m_w_out": dense((nA, M_HEADS * M_DV, D), M_HEADS * M_DV, BETA),
        "a_w_dq": dense((nB, D, A_QLORA), D),
        "a_q_norm": gain((nB, A_QLORA)),
        "a_w_uq": dense((nB, A_QLORA, A_HEADS * (A_DNOPE + A_DROPE)), A_QLORA),
        "a_w_dkv": dense((nB, D, A_KVLORA + A_DROPE), D),
        "a_kv_norm": gain((nB, A_KVLORA)),
        "a_w_ukv": w_ukv,
        "a_w_out": dense((nB, A_HEADS * A_DV, D), A_HEADS * A_DV, BETA),
        "g_w_qk": dense((nC, D, 2 * G_HEADS * G_DK), D),
        "g_w_v": dense((nC, D, G_HEADS * G_DV), D, BETA),
        "g_w_r": dense((nC, D, G_HEADS * G_DV), D),
        "g_w_a1": dense((nC, 2, D, G_RANK), D),
        "g_w_a2": dense((nC, 2, G_RANK, G_HEADS * G_DK), G_RANK),
        "g_b_a": bias((nC, 2, G_HEADS * G_DK), 0.1),
        "g_norm_g": gain((nC, G_HEADS * G_DV)),
        "g_w_out": dense((nC, G_HEADS * G_DV, D), G_HEADS * G_DV, BETA),
    }

def first_block(x, c, ctx, c_ctx, ada_w, ada_b, ln_g, ln_b,
              ffn_w_in, ffn_conv_w, ffn_conv_b, ffn_w_out,
              m_w_up, m_conv_w, m_conv_b, m_w_qk, m_w_v, m_w_gates, m_b_gates, m_w_og, m_norm_g, m_w_out,
              a_w_dq, a_q_norm, a_w_uq, a_w_dkv, a_kv_norm, a_w_ukv, a_w_out,
              g_w_qk, g_w_v, g_w_r, g_w_a1, g_w_a2, g_b_a, g_norm_g, g_w_out):
    ang = _axial_angles(x.shape[1])
    xc = ctx
    for i in range(DEPTH):
        need_ctx = i < DEPTH - 1
        kind, j = i % N_MIXERS, i // N_MIXERS
        ml = _modulation(c, ada_w[i], ada_b[i])
        mc = _modulation(c_ctx[None, :], ada_w[i], ada_b[i])
        hl = _modulate(x, ml[0], ml[1])
        hc = _modulate(xc, mc[0], mc[1])
        if kind == 0:
            yl, yc = _mlstm_mixer(hl, hc, need_ctx, m_w_up[j], m_conv_w[j], m_conv_b[j], m_w_qk[j], m_w_v[j],
                                  m_w_gates[j], m_b_gates[j], m_w_og[j], m_norm_g[j], m_w_out[j])
        elif kind == 1:
            yl, yc = _mla_mixer(hl, hc, need_ctx, ang, a_w_dq[j], a_q_norm[j], a_w_uq[j], a_w_dkv[j],
                                a_kv_norm[j], a_w_ukv[j], a_w_out[j])
        else:
            yl, yc = _gla_mixer(hl, hc, need_ctx, g_w_qk[j], g_w_v[j], g_w_r[j], g_w_a1[j], g_w_a2[j],
                                g_b_a[j], g_norm_g[j], g_w_out[j])
        x = _layer_norm(ALPHA * x + ml[2] * yl, ln_g[i, 0], ln_b[i, 0])
        f = _conv_ffn(_modulate(x, ml[3], ml[4]), ffn_w_in[i], ffn_conv_w[i], ffn_conv_b[i], ffn_w_out[i])
        x = _layer_norm(ALPHA * x + ml[5] * f, ln_g[i, 1], ln_b[i, 1])
        if need_ctx:
            xc = _layer_norm(ALPHA * xc + mc[2] * yc, ln_g[i, 0], ln_b[i, 0])
            fc = _conv_ffn(_modulate(xc, mc[3], mc[4]), ffn_w_in[i], ffn_conv_w[i], ffn_conv_b[i], ffn_w_out[i])
            xc = _layer_norm(ALPHA * xc + mc[5] * fc, ln_g[i, 1], ln_b[i, 1])
    return x


D_MIX = D_MODEL
N_MIXERS_2 = 4
GROUP_W = D_MIX // N_MIXERS_2
N_PARTS = 10
D_IN = N_PARTS * GROUP_W
CONV_A_K = 31
DIFF_HEADS = 4
DIFF_DQK = GROUP_W // (2 * DIFF_HEADS)
DIFF_DV = 2 * DIFF_DQK
ROPE_HALF = DIFF_DQK // 2
CHUNK_2 = 128
SG_GROUPS = 4
SG_DIM = GROUP_W // SG_GROUPS
CONV_D_K = 3
D_FF = 4 * D_MODEL


def rms_norm(x, g):
    xf = x.astype(jnp.float32)
    y = xf * lax.rsqrt(jnp.mean(xf * xf, axis=-1, keepdims=True) + EPS)
    return (y * g.astype(jnp.float32)).astype(x.dtype)

def layer_norm(x, g, b):
    xf = x.astype(jnp.float32)
    xc = xf - jnp.mean(xf, axis=-1, keepdims=True)
    y = xc * lax.rsqrt(jnp.mean(xc * xc, axis=-1, keepdims=True) + EPS)
    return (y * g.astype(jnp.float32) + b.astype(jnp.float32)).astype(x.dtype)

def modulate(h, shift, scale):
    return h * (1 + scale) + shift

def depthwise_conv(x, w):
    pad = w.shape[0] // 2
    return lax.conv_general_dilated(
        x, w[:, None, :].astype(x.dtype), window_strides=(1,), padding=[(pad, pad)],
        dimension_numbers=('NWC', 'WIO', 'NWC'), feature_group_count=x.shape[-1])

def axial_rope(rows, dtype):
    row = jnp.repeat(jnp.arange(rows, dtype=jnp.float32), GRID_W)
    col = jnp.tile(jnp.arange(GRID_W, dtype=jnp.float32), rows)
    inv = ROPE_BASE ** (-jnp.arange(0, ROPE_HALF, 2, dtype=jnp.float32) / ROPE_HALF)
    ang_r = row[:, None] * inv
    ang_c = col[:, None] * inv
    return (jnp.cos(ang_r)[:, None, :].astype(dtype), jnp.sin(ang_r)[:, None, :].astype(dtype),
            jnp.cos(ang_c)[:, None, :].astype(dtype), jnp.sin(ang_c)[:, None, :].astype(dtype))

def rotate_pairs(t, cos, sin):
    f = t.shape[-1] // 2
    t1, t2 = t[..., :f], t[..., f:]
    return jnp.concatenate([t1 * cos - t2 * sin, t1 * sin + t2 * cos], axis=-1)

def apply_axial_rope(t, rope):
    cos_r, sin_r, cos_c, sin_c = rope
    return jnp.concatenate([rotate_pairs(t[..., :ROPE_HALF], cos_r, sin_r),
                            rotate_pairs(t[..., ROPE_HALF:], cos_c, sin_c)], axis=-1)

def qk_heads(t, rope):
    b, n, _ = t.shape
    t = t.reshape(b, n, DIFF_HEADS, 2, DIFF_DQK)
    t1, t2 = t[..., 0, :], t[..., 1, :]
    if rope is not None:
        t1, t2 = apply_axial_rope(t1, rope), apply_axial_rope(t2, rope)
    return t1, t2

def v_heads(t):
    b, n, _ = t.shape
    return t.reshape(b, n, DIFF_HEADS, DIFF_DV)

def diff_attention(q1, q2, k1, k2, v, lam, lam_init, subln_g):
    b, n = q1.shape[:2]
    nb = n // Q_BLOCK
    scale = DIFF_DQK ** -0.5

    def blocks(t):
        return t.reshape(b, nb, Q_BLOCK, DIFF_HEADS, DIFF_DQK).transpose(1, 0, 2, 3, 4)

    def one_block(qs):
        qb1, qb2 = qs
        p1 = jax.nn.softmax(jnp.einsum('bqhd,bkhd->bhqk', qb1, k1).astype(jnp.float32) * scale, axis=-1)
        p2 = jax.nn.softmax(jnp.einsum('bqhd,bkhd->bhqk', qb2, k2).astype(jnp.float32) * scale, axis=-1)
        w = (p1 - lam * p2).astype(v.dtype)
        return jnp.einsum('bhqk,bkhd->bqhd', w, v)

    o = lax.map(one_block, (blocks(q1), blocks(q2)))
    o = o.transpose(1, 0, 2, 3, 4).reshape(b, n, DIFF_HEADS, DIFF_DV)
    o = rms_norm(o, subln_g) * (1.0 - lam_init)
    return o.reshape(b, n, GROUP_W)

def conformer_conv(a_val, a_gate, conv_w, conv_b, ln_g, ln_b):
    glu = a_val * jax.nn.sigmoid(a_gate)
    y = depthwise_conv(glu, conv_w) + conv_b
    return jax.nn.silu(layer_norm(y, ln_g, ln_b))

def spatial_gating(u, v, ln_g, ln_b, w_s, b_s):
    u = jax.nn.gelu(u)
    v = layer_norm(jax.nn.gelu(v), ln_g, ln_b)
    b, n, _ = v.shape
    vc = v.reshape(b, n // CHUNK_2, CHUNK_2, SG_GROUPS, SG_DIM)
    s = jnp.einsum('gpq,bcqgd->bcpgd', w_s, vc) + b_s.T[:, :, None]
    return u * s.reshape(b, n, GROUP_W)

def short_conv_mixer(bg, cg, xin, conv_w):
    return bg * depthwise_conv(cg * xin, conv_w)

def token_mixers(z, k1, k2, v, rope, lam, lam_init, conv_a_w, conv_a_b, ln_a_g, ln_a_b, subln_g,
                 sg_ln_g, sg_ln_b, sg_w, sg_b, conv_d_w, w_out):
    a_val, a_gate, q, _, _, u, sv, bg, cg, xin = z
    y_a = conformer_conv(a_val, a_gate, conv_a_w, conv_a_b, ln_a_g, ln_a_b)
    q1, q2 = qk_heads(q, rope)
    y_b = diff_attention(q1, q2, k1, k2, v, lam, lam_init, subln_g)
    y_c = spatial_gating(u, sv, sg_ln_g, sg_ln_b, sg_w, sg_b)
    y_d = short_conv_mixer(bg, cg, xin, conv_d_w)
    return jnp.concatenate([y_a, y_b, y_c, y_d], axis=-1) @ w_out

def channel_mixer(h, w1, w2):
    return jnp.square(jax.nn.relu(h @ w1)) @ w2

def second_inputs(seed: int = 0) -> dict:
    key = jax.random.key(seed)
    ks = jax.random.split(key, 32)

    def nrm(k, shape, scale):
        return jax.random.normal(k, shape, jnp.float32) * scale

    def gain(k, shape):
        return 1.0 + nrm(k, shape, 0.05)

    return {
        'x': nrm(ks[0], (BATCH, SEQ, D_MODEL), 1.0),
        'c': nrm(ks[1], (BATCH, D_MODEL), 1.0),
        'ctx': nrm(ks[2], (BATCH, CTX_LEN, D_MODEL), 1.0),
        'c_ctx': nrm(ks[3], (D_MODEL,), 1.0),
        'ada_w': nrm(ks[4], (DEPTH, D_MODEL, 6 * D_MODEL), 0.5 * D_MODEL ** -0.5),
        'ada_b': nrm(ks[5], (DEPTH, 6 * D_MODEL), 0.01),
        'norm1_g': gain(ks[6], (DEPTH, D_MODEL)),
        'norm2_g': gain(ks[7], (DEPTH, D_MODEL)),
        'w_in': nrm(ks[8], (DEPTH, D_MODEL, D_IN), D_MODEL ** -0.5),
        'conv_a_w': nrm(ks[9], (DEPTH, CONV_A_K, GROUP_W), CONV_A_K ** -0.5),
        'conv_a_b': nrm(ks[10], (DEPTH, GROUP_W), 0.01),
        'ln_a_g': gain(ks[11], (DEPTH, GROUP_W)),
        'ln_a_b': nrm(ks[12], (DEPTH, GROUP_W), 0.01),
        'lam_q1': nrm(ks[13], (DEPTH, DIFF_DQK), 0.1),
        'lam_k1': nrm(ks[14], (DEPTH, DIFF_DQK), 0.1),
        'lam_q2': nrm(ks[15], (DEPTH, DIFF_DQK), 0.1),
        'lam_k2': nrm(ks[16], (DEPTH, DIFF_DQK), 0.1),
        'subln_g': gain(ks[17], (DEPTH, DIFF_DV)),
        'sg_ln_g': gain(ks[18], (DEPTH, GROUP_W)),
        'sg_ln_b': nrm(ks[19], (DEPTH, GROUP_W), 0.01),
        'sg_w': nrm(ks[20], (DEPTH, SG_GROUPS, CHUNK_2, CHUNK_2), CHUNK_2 ** -0.5),
        'sg_b': gain(ks[21], (DEPTH, SG_GROUPS, CHUNK_2)),
        'conv_d_w': nrm(ks[22], (DEPTH, CONV_D_K, GROUP_W), CONV_D_K ** -0.5),
        'w_out': nrm(ks[23], (DEPTH, D_MIX, D_MODEL), D_MIX ** -0.5),
        'mlp_w1': nrm(ks[24], (DEPTH, D_MODEL, D_FF), D_MODEL ** -0.5),
        'mlp_w2': nrm(ks[25], (DEPTH, D_FF, D_MODEL), D_FF ** -0.5),
        'final_g': gain(ks[26], (D_MODEL,)),
    }

def second_block(x, c, ctx, c_ctx, ada_w, ada_b, norm1_g, norm2_g, w_in, conv_a_w, conv_a_b, ln_a_g,
              ln_a_b, lam_q1, lam_k1, lam_q2, lam_k2, subln_g, sg_ln_g, sg_ln_b, sg_w, sg_b, conv_d_w,
              w_out, mlp_w1, mlp_w2, final_g):
    ROWS = x.shape[1] // GRID_W
    rope = axial_rope(ROWS, x.dtype)
    h_ctx = ctx
    for l in range(DEPTH):
        lam_init = 0.8 - 0.6 * math.exp(-0.3 * l)
        lam = (jnp.exp(jnp.sum(lam_q1[l] * lam_k1[l]).astype(jnp.float32))
               - jnp.exp(jnp.sum(lam_q2[l] * lam_k2[l]).astype(jnp.float32)) + lam_init)
        mod_x = jnp.split((jax.nn.silu(c) @ ada_w[l] + ada_b[l])[:, None, :], 6, axis=-1)
        mod_c = jnp.split(jax.nn.silu(c_ctx) @ ada_w[l] + ada_b[l], 6, axis=-1)
        mix_args = (rope, lam, lam_init, conv_a_w[l], conv_a_b[l], ln_a_g[l], ln_a_b[l], subln_g[l],
                    sg_ln_g[l], sg_ln_b[l], sg_w[l], sg_b[l], conv_d_w[l], w_out[l])

        hc = modulate(rms_norm(h_ctx, norm1_g[l]), mod_c[0], mod_c[1])
        zc = jnp.split(hc @ w_in[l], N_PARTS, axis=-1)
        k1c, k2c = qk_heads(zc[3], None)
        vc = v_heads(zc[4])

        hx = modulate(rms_norm(x, norm1_g[l]), mod_x[0], mod_x[1])
        zx = jnp.split(hx @ w_in[l], N_PARTS, axis=-1)
        k1x, k2x = qk_heads(zx[3], rope)
        k1 = jnp.concatenate([k1c, k1x], axis=1)
        k2 = jnp.concatenate([k2c, k2x], axis=1)
        v = jnp.concatenate([vc, v_heads(zx[4])], axis=1)
        x = x + mod_x[2] * token_mixers(zx, k1, k2, v, *mix_args)
        x = x + mod_x[5] * channel_mixer(modulate(rms_norm(x, norm2_g[l]), mod_x[3], mod_x[4]),
                                         mlp_w1[l], mlp_w2[l])

        if l < DEPTH - 1:
            ctx_args = (None,) + mix_args[1:]
            h_ctx = h_ctx + mod_c[2] * token_mixers(zc, k1c, k2c, vc, *ctx_args)
            h_ctx = h_ctx + mod_c[5] * channel_mixer(
                modulate(rms_norm(h_ctx, norm2_g[l]), mod_c[3], mod_c[4]), mlp_w1[l], mlp_w2[l])
    return rms_norm(x, final_g)


def setup_inputs(seed=0):
    out = dict(first_inputs(seed))
    for name, value in second_inputs(seed + 1).items():
        if name != "x":
            out[name + "_2"] = value
    return out


def reference(
    x, c, ctx, c_ctx, ada_w, ada_b, ln_g, ln_b, ffn_w_in, ffn_conv_w, ffn_conv_b, ffn_w_out,
    m_w_up, m_conv_w, m_conv_b, m_w_qk, m_w_v, m_w_gates, m_b_gates, m_w_og, m_norm_g, m_w_out,
    a_w_dq, a_q_norm, a_w_uq, a_w_dkv, a_kv_norm, a_w_ukv, a_w_out, g_w_qk, g_w_v, g_w_r,
    g_w_a1, g_w_a2, g_b_a, g_norm_g, g_w_out, c_2, ctx_2, c_ctx_2, ada_w_2, ada_b_2, norm1_g_2,
    norm2_g_2, w_in_2, conv_a_w_2, conv_a_b_2, ln_a_g_2, ln_a_b_2, lam_q1_2, lam_k1_2, lam_q2_2,
    lam_k2_2, subln_g_2, sg_ln_g_2, sg_ln_b_2, sg_w_2, sg_b_2, conv_d_w_2, w_out_2, mlp_w1_2,
    mlp_w2_2, final_g_2,
):
    x = first_block(
        x, c, ctx, c_ctx, ada_w, ada_b, ln_g, ln_b, ffn_w_in, ffn_conv_w, ffn_conv_b, ffn_w_out,
        m_w_up, m_conv_w, m_conv_b, m_w_qk, m_w_v, m_w_gates, m_b_gates, m_w_og, m_norm_g,
        m_w_out, a_w_dq, a_q_norm, a_w_uq, a_w_dkv, a_kv_norm, a_w_ukv, a_w_out, g_w_qk, g_w_v,
        g_w_r, g_w_a1, g_w_a2, g_b_a, g_norm_g, g_w_out,
    )
    return second_block(
        x, c_2, ctx_2, c_ctx_2, ada_w_2, ada_b_2, norm1_g_2, norm2_g_2, w_in_2, conv_a_w_2,
        conv_a_b_2, ln_a_g_2, ln_a_b_2, lam_q1_2, lam_k1_2, lam_q2_2, lam_k2_2, subln_g_2,
        sg_ln_g_2, sg_ln_b_2, sg_w_2, sg_b_2, conv_d_w_2, w_out_2, mlp_w1_2, mlp_w2_2,
        final_g_2,
    )


_drawn_inputs = setup_inputs


def setup_inputs(seed=0):
    import zlib

    import numpy as np

    out = dict(_drawn_inputs(seed))
    spreads = {}
    factors = {'ada_b': 3.916,
     'ffn_conv_b': 8.0,
     'm_conv_b': 6.625,
     'm_norm_g': 8.0,
     'a_w_dq': 8.0,
     'a_q_norm': 8.0,
     'a_w_uq': 8.0,
     'a_w_dkv': 4.399,
     'a_kv_norm': 8.0,
     'a_w_ukv': 3.143,
     'a_w_out': 4.073,
     'conv_a_b_2': 8.0,
     'ln_a_g_2': 7.239,
     'ln_a_b_2': 64.0,
     'lam_q1_2': 3.938,
     'lam_k1_2': 5.672,
     'lam_q2_2': 8.0,
     'lam_k2_2': 8.0,
     'subln_g_2': 7.194,
     'sg_ln_g_2': 7.737,
     'sg_ln_b_2': 64.0,
     'sg_b_2': 7.562,
     'norm2_g_2': 3.477}
    for name, (base, spread) in spreads.items():
        noise = np.random.default_rng([zlib.crc32(name.encode()), seed]).standard_normal(out[name].shape)
        drawn = base * np.exp(spread * noise) if base else spread * noise
        out[name] = jnp.asarray(drawn.astype(out[name].dtype))
    for name, factor in factors.items():
        out[name] = (out[name] * factor).astype(out[name].dtype)
    return out
```

```python
import math
from contextlib import ExitStack

import numpy as np

import concourse.bass as bass
from concourse import mybir

F32 = mybir.dt.float32
F32R = mybir.dt.float32r
ALU = mybir.AluOpType
ACT = mybir.ActivationFunctionType
AX_X = mybir.AxisListType.X

P = 128
D = 1024
DT = D // P
CTX = 256
T = 512
LAT = slice(CTX, T)
EPS = 1e-6
ALPHA = 4 ** 0.25
NH = 4
FFN_T = 22
MLA_H = 8
RING = 4
BANKS = 4
UNIT = 1024
LEAD = 2
CONV_TAPS = 9
ADA_W = 256
ADA_KS = 4
ADA_LAYER = 6 * D // ADA_W
ADA0 = 2 * D // ADA_W
ADA_RING = 3
MLA_SCALE = 192 ** -0.5
DIFF_SCALE = 32 ** -0.5
ADA_PACE = {"up": (0, 1), "v": (2, 1), "qk": (2, 1), "f1": (1, 4)}



def halves(full):
    return [(slice(0, CTX), 1), (LAT, 0)] if full else [(LAT, 0)]


def rng(full):
    return slice(0, T) if full else LAT



def span(*starts, width=P):
    return np.concatenate([np.arange(s, s + width) for s in starts])


class Linear:

    def __init__(self, name, source, k_tiles, groups, full=True, token_major=False, freed_by="act", row0=0,
                 kc=None):
        self.name, self.source, self.k_tiles, self.groups = name, source, k_tiles, groups
        self.full, self.token_major, self.freed_by, self.row0 = full, token_major, freed_by, row0
        self.width = len(groups[0])
        self.kc = kc or UNIT // self.width
        self.chunks = [list(range(k, min(k + self.kc, k_tiles))) for k in range(0, k_tiles, self.kc)]
        self.nch = len(self.chunks)
        self.tpg = 4 if token_major else self.width // P
        self.n_tiles = self.tpg * len(groups)


def plan():
    g256 = lambda n, at=0: [span(at + i * 256, width=256) for i in range(n)]
    out = []
    out += [Linear("og", "m_w_og", 8, g256(8)),
            Linear("up", "m_w_up", 8, g256(8), freed_by="dve"),
            Linear("v", "m_w_v", 16, [span(i * 512, width=512) for i in range(4)], token_major=True, kc=2),
            Linear("qk", "m_w_qk", 16, g256(8)),
            Linear("mout", "m_w_out", 16, g256(4), freed_by="dve")]

    def ffn(tag, layer, full):
        for half in range(2):
            fs = range(11 * half, 11 * half + 11)
            out.append(Linear(f"{tag}in{half}", ("ffn_w_in", layer), 8,
                              [np.concatenate([span(f * P), span(FFN_T * P + f * P)]) for f in fs],
                              full=full, freed_by="dve"))
            out.append(Linear(f"{tag}out{half}", ("ffn_w_out", layer), 11, g256(4), full=full, freed_by="dve",
                              row0=11 * half))

    ffn("f0", 0, True)
    out += [Linear("dkv", "a_w_dkv", 8, [span(0, width=256)]),
            Linear("dkr", "a_w_dkv", 8, [np.concatenate([span(256, width=64)] * 2)]),
            Linear("dq", "a_w_dq", 8, [span(i * P) for i in range(3)], full=False),
            Linear("uqn", "a_w_uq", 3, [span(384 * i, 384 * i + 192) for i in range(4)], full=False),
            Linear("uqr", "a_w_uq", 3, [np.concatenate([span(192 * h + 128, width=64) for h in range(4 * i, 4 * i + 4)])
                                        for i in range(2)], full=False),
            Linear("ukn", "a_w_ukv", 2, [span(*[256 * h for h in range(4 * i, 4 * i + 4)]) for i in range(2)]),
            Linear("ukv", "a_w_ukv", 2, [span(*[256 * h + 128 for h in range(4 * i, 4 * i + 4)]) for i in range(2)],
                   token_major=True),
            Linear("aout", "a_w_out", 8, g256(4), full=False, freed_by="dve")]
    ffn("f1", 1, False)
    for l in range(2):
        full = l == 0
        out.append(Linear(f"kv{l}", ("w_in_2", l), 8, g256(2, at=768)))
        out.append(Linear(f"z{l}", ("w_in_2", l), 8, g256(3) + g256(5, at=1280), full=full))
        out.append(Linear(f"wo{l}", ("w_out_2", l), 8, g256(4), full=full, freed_by="dve"))
        for half in range(2):
            out.append(Linear(f"g{l}in{half}", ("mlp_w1_2", l), 8, g256(8, at=2048 * half), full=full))
            out.append(Linear(f"g{l}out{half}", ("mlp_w2_2", l), 16, g256(4), full=full, freed_by="dve",
                              row0=16 * half))
    units, tiles, used, done = [], [], 0, 0
    free = {"act": 0, "dve": 0}
    for ph in out:
        ph.u0, ph.t0 = len(units), len(tiles)
        ph.free0 = free[ph.freed_by]
        for g in range(len(ph.groups)):
            for c in range(ph.nch):
                if c < ph.nch - 1:
                    used += 1
                    units.append((ph, g, c, "unit_used", used))
                else:
                    units.append((ph, g, c, "tile_done", done + ph.tpg))
            done += ph.tpg
            for m in range(ph.tpg):
                free[ph.freed_by] += 1
                tiles.append((ph.freed_by, free[ph.freed_by]))
    macs, sums = [], {}
    todo = [(a, k) for a in range(ADA0, 4 * ADA_LAYER) for k in range(ADA_KS)]
    for u, (ph, g, c, _, _) in enumerate(units):
        count, every = ADA_PACE.get(ph.name[:2], (1, 1))
        for _ in range(0 if (u - ph.u0) % every else min(count, len(todo))):
            a, k = todo.pop(0)
            macs.append((u, a, k))
            if k == ADA_KS - 1:
                sums.setdefault(u + 1, []).append(a)
    assert not todo, len(todo)
    return {ph.name: ph for ph in out}, out, units, tiles, macs, sums


LIN, PHASES, UNITS, TILES, ADA_MACS, ADA_SUMS = plan()
hid0 = {"f0": 0, "f1": 22, "g0": 44, "g1": 76}


def ada_conds(a):
    layer, c = divmod(a, ADA_LAYER)
    return 1 if layer % 2 and c >= ADA0 else 2


def ada_steps(n):
    return 2 * sum(ada_conds(a) for _, a, _ in ADA_MACS[:n])


def summed_before(name):
    return ADA0 + sum(len(slices) for u, slices in ADA_SUMS.items() if u < LIN[name].u0)


MOD_READ = {ADA0: 1, summed_before("mout"): 2, summed_before("dkv"): 4, summed_before("kv0"): 5}
assert ADA_LAYER <= summed_before("mout") <= 2 * ADA_LAYER and 2 * ADA_LAYER <= summed_before("dkv") <= 3 * ADA_LAYER
assert 3 * ADA_LAYER <= summed_before("kv0") and summed_before("kv1") == 4 * ADA_LAYER
nsq_after = list(np.cumsum([4] * 4 + [8, 8, 2, 3, 8, 8] + [8, 2, 2, 1, 1, 8] * 2 + [8]).tolist())


def columns(spec):
    at, out = 0, {}
    for name, n in spec:
        out[name] = at
        at += n
    return out, at


VEC1_SPEC = [("ada_b", 96), ("ln_g", 32), ("ln_b", 32), ("ffn_conv_w", 132), ("ffn_conv_b", 44), ("m_conv_w", 48),
             ("m_conv_b", 16), ("m_norm_g", 16), ("a_q_norm", 3), ("a_kv_norm", 2)]
VEC2_SPEC = [("ada_b_2", 96), ("norm1_g_2", 16), ("norm2_g_2", 16), ("conv_a_w_2", 124), ("conv_a_b_2", 4),
             ("ln_a_g_2", 4), ("ln_a_b_2", 4), ("sg_ln_g_2", 4), ("sg_ln_b_2", 4), ("conv_d_w_2", 12),
             ("subln_g_2", 2), ("final_g_2", 8)]
V1, NV1 = columns(VEC1_SPEC)
V2, NV2 = columns(VEC2_SPEC)


def w_span(s):
    return (s * T, s * T + T) if s < 2 else (2 * T + (s - 2) * CTX, 2 * T + (s - 1) * CTX)


def q_span(s):
    return slice(0, T) if s < 2 else LAT



def two_stacks(nc, A, stop_after=None, probe_out=None):
    with ExitStack() as ctx:
        def sb(name, shape, dt=F32, stack=ctx):
            return stack.enter_context(nc.sbuf_tensor(name, shape, dt))

        sems = {}

        def sem(name):
            if name not in sems:
                sems[name] = ctx.enter_context(nc.semaphore(name))
            return sems[name]


        raw = sb("raw", [P, RING, UNIT])
        w_hi = sb("w_hi", [P, RING, UNIT], F32R)
        w_lo = sb("w_lo", [P, RING, UNIT], F32R)
        ada_ring = sb("ada_ring", [P, ADA_RING, 2 * ADA_W])
        ada_acc = sb("ada_acc", [P, 2, 2, ADA_W])
        ones = sb("ones", [P, P])
        ident = sb("ident", [P, P])
        vec1 = sb("vec1", [P, NV1])
        cond = sb("cond", [P, 2, 8, 2])
        mod = sb("mod", [P, 2, 48, 2])
        small = sb("small", [P, 64])
        gcol = small[:, 8:40].rearrange("p (d s h) -> p d s h", d=2, s=4)
        with ExitStack() as st:
            h0_hi = sb("h0_hi", [P, 8, T], F32R, st)
            h0_lo = sb("h0_lo", [P, 8, T], F32R, st)
        xv = sb("xv", [P, 16 * T])
        X = xv[:, 0:8 * T].rearrange("p (t n) -> p t n", n=T)
        TMP = xv[:, 8 * T:16 * T].rearrange("p (t n) -> p t n", n=T)
        V = xv[:, :].rearrange("p (s e) -> p s e", e=4 * T)
        MEAN, RSTD = TMP[:, 6], TMP[:, 7]

        with ExitStack() as st:
            m_hi = sb("m_hi", [P, 16, T], F32R, st)
            qk = sb("qk", [P, 16, T], F32, st)
            wgt = sb("wgt", [P, 8 * T], F32, st)
            rows = sb("rows", [P, T], F32, st)
            with ExitStack() as inner:
                m_lo = sb("m_lo", [P, 16, T], F32R, inner)
            with ExitStack() as inner:
                og = sb("og", [P, 16, T], F32, inner)
        MT = wgt[:, :].rearrange("p (t n) -> p t n", n=T)
        WD = wgt[:, 0:3072].rearrange("p (d n) -> p d n", d=2)
        RD = wgt[:, 3072:4096].rearrange("p (d n) -> p d n", d=2)
        with ExitStack() as st:
            sb("below", [P, 32 * T], F32, st)
            gates = sb("gates", [4, 6, T], F32, st)
            with ExitStack() as inner:
                gate_w = sb("gate_w", [P, 256], F32, inner)
                gate_hi = sb("gate_hi", [P, 256], F32R, inner)
                gate_lo = sb("gate_lo", [P, 256], F32R, inner)
            with ExitStack() as inner:
                gate_all = sb("gate_all", [16, T], F32, inner)

        with ExitStack() as st:
            vec2 = sb("vec2", [P, NV2], F32, st)
            h_hi = sb("h_hi", [P, 8, T], F32R, st)
            h_lo = sb("h_lo", [P, 8, T], F32R, st)
            with ExitStack() as inner:
                hid_hi = sb("hid_hi", [P, 16, T], F32R, inner)
                hid_lo = sb("hid_lo", [P, 16, T], F32R, inner)
            with ExitStack() as inner:
                ckv = sb("ckv", [P, 2, T], F32, inner)
                ckv_hi = sb("ckv_hi", [P, 2, T], F32R, inner)
                ckv_lo = sb("ckv_lo", [P, 2, T], F32R, inner)
                cq = sb("cq", [P, 3, CTX], F32, inner)
                cq_hi = sb("cq_hi", [P, 3, CTX], F32R, inner)
                cq_lo = sb("cq_lo", [P, 3, CTX], F32R, inner)
                qn = sb("qn", [P, 8, CTX], F32, inner)
                qr = sb("qr", [P, 4, CTX], F32, inner)
                kn = sb("kn", [P, 8, T], F32, inner)
                kr = sb("kr", [P, T], F32, inner)
                vm = sb("vm", [P, 4, D], F32, inner)
                arope = sb("arope", [P, 2, CTX], F32, inner)
                arot = sb("arot", [P, P], F32, inner)
            with ExitStack() as inner:
                z = sb("z", [P, 20, T], F32, inner)
                glu = sb("glu", [P, 2, 2, CTX + 30], F32, inner)
                conv = sb("conv", [P, 2, T], F32, inner)
                vtok = sb("vtok", [P, 4, CTX], F32, inner)
                stok = sb("stok", [P, 4, CTX], F32, inner)
                sgw = sb("sgw", [P, 4, P], F32, inner)
                sgb = sb("sgb", [P, 2, P], F32, inner)
                probs = sb("probs", [P, 2, 2, T], F32, inner)
                probs_t = sb("probs_t", [P, 4, T], F32, inner)
                drope = sb("drope", [P, 2, CTX], F32, inner)
                drot = sb("drot", [P, 2, P], F32, inner)
        PS = ctx.enter_context(nc.psum_tensor("PS", [P, 8, T], F32))

        block = ctx.enter_context(nc.Block())

        def w_slot(u):
            return u % RING

        def SQ(n):
            return wgt[:, 3 * T + (n % 2) * T:4 * T + (n % 2) * T] if n < 16 else TMP[:, 4 + n % 2]

        def x_tiles(t, full=True):
            return X[:, t, rng(full)]

        def scale_of(i, j):
            return TMP[:, 4 + i % 2, j * P:(j + 1) * P]

        @block.sync
        def _(sp):
            for name, tile in (("cond", cond[:]), ("ones", ones[:]), ("ident", ident[:]), ("vec1", vec1[:]),
                               ("bg", small[0:4, 0:4]), ("lam", small[0:32, 56:64])):
                sp.dma_start(tile, A[name]).then_inc(sem("consts_in"), 16)
            for i in range(8):
                dst = (xv[:] if i < 4 else qk[:].rearrange("p t n -> p (t n)"))[:, (i % 4) * 2 * UNIT:(i % 4 + 1) * 2 * UNIT]
                sp.dma_start(dst, A["ada0"][i]).then_inc(sem(f"ada0_in{i}"), 16)
            sp.dma_start(MT[:, :, :], A["x0"]).then_inc(sem("x0_in"), 16)
            ada_out = 0
            for u in range(len(UNITS)):
                if u >= RING:
                    sp.wait_ge(sem("w_split"), u - RING + 1)
                n = A["units_width"][u]
                sp.dma_start(raw[:, w_slot(u), 0:n], A["weights"][u, :, 0:n]).then_inc(sem(f"raw_in{w_slot(u)}"), 16)
                while ada_out < len(ADA_MACS) and (ada_out < ADA_RING or ADA_MACS[ada_out - ADA_RING][0] + RING <= u):
                    if ada_out >= ADA_RING:
                        sp.wait_ge(sem("ada_mac"), ada_steps(ada_out - ADA_RING + 1))
                    slot = ada_out % ADA_RING
                    sp.dma_start(ada_ring[:, slot, :], A["ada"][ada_out]).then_inc(sem(f"ada_in{slot}"), 16)
                    ada_out += 1
            sp.wait_ge(sem("out_done"), 16)

        @block.gpsimd
        def _(pool):
            for i in range(4):
                pool.wait_ge(sem("free_act"), LIN["og"].free0 + 4 * (i + 1))
                pool.dma_start(A["og_spill"][:, 4 * i:4 * i + 4, :], qk[:, 4 * i:4 * i + 4, :]).then_inc(sem("og_out"), 16)
            pool.wait_ge(sem("up_c"), 16)
            pool.dma_start(gate_w[:], A["gate_w"]).then_inc(sem("gate_w_in"), 16)
            pool.wait_ge(sem("og_out"), 64)
            pool.wait_ge(sem("tile_done"), LIN["mout"].t0)
            pool.dma_start(og[:, :, :], A["og_spill"]).then_inc(sem("og_in"), 16)
            for h in range(NH):
                for d in range(2):
                    for s in range(4):
                        i = 8 * h + 4 * d + s
                        pool.wait_ge(sem("wraw"), i + 1)
                        lo, hi = w_span(s)
                        if d == 0:
                            ap = WD[:, 0, lo:hi]
                            base, step, cm = (0 if s < 2 else CTX) - s * P, 1, -1
                        else:
                            ap = WD[:, 1, lo:lo + CTX]
                            base, step, cm = s * P - (0 if s < 2 else CTX), -1, 1
                        pool.affine_select(out=ap, in_=ap, compare_op=ALU.is_ge, fill=0.0, base=base,
                                           pattern=[[step, ap.shape[-1]]], channel_multiplier=cm)\
                            .then_inc(sem("wsel"), 1)
            pool.wait_ge(sem("pv"), 4 * NH)
            pool.dma_start(X[:, :, :], A["x0"]).then_inc(sem("x_in"), 16)
            pool.wait_ge(sem("tile_done"), LIN["dkv"].t0)
            pool.dma_start(vec2[:], A["vec2"]).then_inc(sem("vec2_in"), 16)
            pool.dma_start(arope[:], A["arope"]).then_inc(sem("arope_in"), 16)
            pool.dma_start(arot[:], A["arot"]).then_inc(sem("arope_in"), 16)
            pool.wait_ge(sem("h_lo"), 8 * 3)
            pool.dma_start(X[:, :, 0:CTX], A["ctx2"]).then_inc(sem("ctx2_in"), 16)
            for l in range(2):
                pool.wait_ge(sem("tile_done"), LIN[f"kv{l}"].t0)
                for name, dst, src in (("drope", drope, A["drope"]), ("drot", drot, A["drot"]), ("sgw", sgw, A["sgw"][l])):
                    pool.dma_start(dst[:], src).then_inc(sem("mix_in"), 16)
                for g in range(4):
                    pool.dma_start(sgb[64 * (g % 2):64 * (g % 2) + 64, g // 2, :],
                                   A["sgb"][l, g:g + 1, :].broadcast_to([64, P])).then_inc(sem("mix_in"), 16)
            pool.wait_ge(sem("final"), 8)
            pool.dma_start(A["out"], X[:, :, LAT]).then_inc(sem("out_done"), 16)

        @block.tensor
        def _(pe):
            nsq, ncall = [0], [0]

            def first_modulation():
                for m in range(16):
                    src = xv[:] if m < 8 else qk[:].rearrange("p t n -> p (t n)")
                    pe.wait_ge(sem(f"ada0_in{m // 2}"), 16)
                    for k in range(8):
                        at = (m % 8) * UNIT + k * P
                        mm = pe.matmul(PS[:, 7, 2 * m:2 * m + 2], src[:, at:at + P], cond[:, 0, k, :],
                                       start=(k == 0), stop=(k == 7))
                    if m % 2:
                        mm.then_inc(sem("ada_sum"), 1)

            def sum_modulation(a):
                if a in MOD_READ:
                    pe.wait_ge(sem("mod_read"), MOD_READ[a])
                layer, c = divmod(a, ADA_LAYER)
                pe.wait_ge(sem("ada_mac"), ada_steps((a - ADA0 + 1) * ADA_KS))
                for v in range(ada_conds(a)):
                    for m in range(2):
                        col = (layer % 2) * 96 + 2 * (2 * c + m) + v
                        mm = pe.matmul(PS[:, 7, col:col + 1], ada_acc[:, a % 2, v, m * P:(m + 1) * P], ones[:, 0:1],
                                       start=True, stop=True)
                mm.then_inc(sem("ada_sum"), 1)

            def linear(name, hi, lo, ready=(), each=None):
                ph = LIN[name]
                for what, value in ready:
                    pe.wait_ge(sem(what), value)
                r = rng(ph.full)
                for g in range(len(ph.groups)):
                    for c, ks in enumerate(ph.chunks):
                        u = ph.u0 + g * ph.nch + c
                        s = w_slot(u)
                        pe.wait_ge(sem("w_split"), u + 1)
                        for m in range(ph.tpg):
                            t = ph.t0 + g * ph.tpg + m
                            if c == 0 and t >= BANKS:
                                freed, n = TILES[t - BANKS]
                                pe.wait_ge(sem(f"free_{freed}"), n)
                            for kk, k in enumerate(ks):
                                if each and g == 0 and m == 0:
                                    pe.wait_ge(sem(each[0]), each[1] + k + 1)
                                if ph.token_major:
                                    at = slice(kk * ph.width, (kk + 1) * ph.width)
                                    pairs = [(hi(k)[:, m * P:(m + 1) * P], w_hi[:, s, at]),
                                             (hi(k)[:, m * P:(m + 1) * P], w_lo[:, s, at]),
                                             (lo(k)[:, m * P:(m + 1) * P], w_hi[:, s, at])]
                                    out = PS[:, t % BANKS, 0:ph.width]
                                else:
                                    at = slice(kk * ph.width + m * P, kk * ph.width + (m + 1) * P)
                                    pairs = [(w_hi[:, s, at], hi(k)), (w_hi[:, s, at], lo(k)), (w_lo[:, s, at], hi(k))]
                                    out = PS[:, t % BANKS, r]
                                for i, (a, b) in enumerate(pairs):
                                    mm = pe.matmul(out, a, b, start=(k == 0 and i == 0),
                                                   stop=(k == ph.k_tiles - 1 and i == 2))
                            if c == ph.nch - 1:
                                mm.then_inc(sem("tile_done"), 1)
                            elif m == ph.tpg - 1:
                                mm.then_inc(sem("unit_used"), 1)
                        for a in ADA_SUMS.get(u, ()):
                            sum_modulation(a)

            def sum_squares(n, bank, cols, lhs, width):
                if ncall[0] > 0:
                    pe.wait_ge(sem("var"), ncall[0])
                ncall[0] += 1
                for i in range(n):
                    nsq[0] += 1
                    pe.wait_ge(sem("sq_made"), nsq[0])
                    pe.matmul(PS[:, bank, cols], lhs, SQ(nsq[0] - 1)[:, 0:width], start=(i == 0), stop=(i == n - 1))\
                        .then_inc(sem("sq_used"), 1)

            def sums(aps, bank, cols, waits):
                for i, (ap, (what, value)) in enumerate(zip(aps, waits)):
                    pe.wait_ge(sem(what), value)
                    mm = pe.matmul(PS[:, bank, cols], ones[:], ap, start=(i == 0), stop=(i == len(aps) - 1))
                mm.then_inc(sem("xsum"), 1)

            pe.wait_ge(sem("cond"), 1)
            first_modulation()
            h0 = (lambda k: h0_hi[:, k, :], lambda k: h0_lo[:, k, :])
            mx = (lambda k: m_hi[:, k, :], lambda k: m_lo[:, k, :])
            hx = lambda full: (lambda k: h_hi[:, k, rng(full)], lambda k: h_lo[:, k, rng(full)])
            hid = lambda full: (lambda k: hid_hi[:, k, rng(full)], lambda k: hid_lo[:, k, rng(full)])
            linear("og", *h0, each=("h_lo", 0))
            linear("up", *h0)
            linear("v", *mx, each=("up_lo", 0))
            pe.wait_ge(sem("xc_lo"), 16)
            pe.wait_ge(sem("gate_wlo"), 1)
            for k in range(16):
                w = slice(k * 16, (k + 1) * 16)
                for i, (a, b) in enumerate(((gate_hi, m_hi), (gate_hi, m_lo), (gate_lo, m_hi))):
                    mm = pe.matmul(PS[0:16, 4, :], a[:, w], b[:, k, :], start=(k == 0 and i == 0), stop=(k == 15 and i == 2))
            mm.then_inc(sem("gate_mm"), 1)
            pe.wait_ge(sem("gate_all"), 1)
            pe.wait_ge(sem("free_act"), LIN["v"].free0 + 16)
            for q in range(4):
                at = 8 * (q % 2) + 4 * (q // 2)
                pe.matmul(PS[0:4, (4, 5, 6, 3)[q], :], ident[0:16, at:at + 4], gate_all[:], start=True, stop=True)\
                    .then_inc(sem("gate_rows"), 1)
            linear("qk", *mx, ready=[("gate_pre", 4)])
            pe.wait_ge(sem("gate_g"), 1)
            for d in range(2):
                for s in range(4):
                    mm = pe.transpose(PS[:, 4, d * 16 + s * 4:d * 16 + s * 4 + 4], gates[:, d, s * P:(s + 1) * P],
                                      ident[0:4, 0:4])
            mm.then_inc(sem("gcol_t"), 1)
            pe.wait_ge(sem("rows"), 4)
            pe.wait_ge(sem("gcol"), 1)
            pe.wait_ge(sem("free_act"), LIN["qk"].free0 + 16)
            for h in range(NH):
                if h > 0:
                    pe.wait_ge(sem("pv_used"), 4 * h)
                    pe.wait_ge(sem("var"), ncall[0])
                for i in range(4):
                    b = 32 * i
                    pe.matmul(PS[:, 3 + i, :], ident[b:b + 4, b + h:b + h + 1].broadcast_to([4, P]), rows[b:b + 4, :],
                              start=True, stop=True).then_inc(sem("bcast"), 1)
                for s in range(4):
                    out = PS[:, s, :] if s < 2 else PS[:, 2, (s - 2) * CTX:(s - 1) * CTX]
                    for kk in range(2):
                        mm = pe.matmul(out, qk[:, 8 + 2 * h + kk, s * P:(s + 1) * P], qk[:, 2 * h + kk, q_span(s)],
                                       start=(kk == 0), stop=(kk == 1))
                    mm.then_inc(sem("scores"), 1)
                for d in range(2):
                    pe.wait_ge(sem("expw"), 8 * h + 4 * d + 4)
                    for s in range(4):
                        pe.wait_ge(sem("wsel"), 8 * h + 4 * d + s + 1)
                        lo, hi = w_span(s)
                        mm = pe.matmul(PS[:, 3 + d, q_span(s)], ones[:], WD[:, d, lo:hi], start=(s == 0), stop=(s == 3))
                    mm.then_inc(sem("den"), 1)
                for e in range(4):
                    for s in range(4):
                        if e == 0:
                            pe.wait_ge(sem("wsum"), 4 * h + s + 1)
                        if e == 3 and s == 0:
                            pe.wait_ge(sem("wsum"), 4 * (h + 1))
                        lo, hi = w_span(s)
                        at = h * T + e * P
                        mm = pe.matmul(PS[:, (0, 1, 2, 5)[e], q_span(s)], V[:, s, at:at + P], WD[:, 0, lo:hi],
                                       start=(s == 0), stop=(s == 3))
                    mm.then_inc(sem("pv"), 1)
                sum_squares(4, 6, slice(0, T), ones[:], T)
            linear("mout", *mx, each=("hs_lo", 0))

            def norm_sums(full, name, mean):
                ph = LIN[name]
                if mean:
                    n0 = ph.free0 + ph.n_tiles - 8
                    sums([X[:, t, rng(full)] for t in range(8)], 4, rng(full), [("free_dve", n0 + t + 1) for t in range(8)])
                sum_squares(8, 5, rng(full), ones[:], T if full else CTX)

            def feed_forward(tag, full, n_h):
                for half in range(2):
                    linear(f"{tag}in{half}", *hx(full), each=("h_lo", 8 * n_h) if half == 0 else None)
                    n = 11 if tag[0] == "f" else 16
                    linear(f"{tag}out{half}", *hid(full), each=("hid_lo", hid0[tag] + n * half))

            norm_sums(True, "mout", True)
            feed_forward("f0", True, 1)
            norm_sums(True, "f0out1", True)
            hl = (lambda k: h_hi[:, k, LAT], lambda k: h_lo[:, k, LAT])
            linear("dkv", *hx(True), each=("h_lo", 16))
            linear("dkr", *hx(True))
            linear("dq", *hl)
            sum_squares(2, 5, slice(0, T), ones[:], T)
            sum_squares(3, 5, slice(0, CTX), ones[:], CTX)
            ckv_x = (lambda k: ckv_hi[:, k, :], lambda k: ckv_lo[:, k, :])
            linear("uqn", lambda k: cq_hi[:, k, :], lambda k: cq_lo[:, k, :], ready=[("c_lo", 5)])
            linear("uqr", lambda k: cq_hi[:, k, :], lambda k: cq_lo[:, k, :])
            linear("ukn", *ckv_x)
            linear("ukv", *ckv_x)
            pe.wait_ge(sem("free_act"), LIN["ukv"].free0 + 8)
            pe.wait_ge(sem("arope_in"), 32)
            for i in range(5):
                src = kr[:, LAT] if i == 4 else qr[:, i, :]
                pe.matmul(PS[:, 4 + i // 2, (i % 2) * CTX:(i % 2 + 1) * CTX], arot[:], src, start=True, stop=True)\
                    .then_inc(sem("rot"), 1)
            pe.wait_ge(sem("roped"), 5)

            def mla_scores(i):
                h, tt = divmod(i, 2)
                if i - 1 > 0:
                    pe.wait_ge(sem("att_e"), i - 1)
                b = 64 * (h % 2)
                pe.matmul(PS[:, i % 2, :], qn[:, h, tt * P:(tt + 1) * P], kn[:, h, :], start=True, stop=False)
                pe.matmul(PS[:, i % 2, :], qr[b:b + 64, h // 2, tt * P:(tt + 1) * P], kr[b:b + 64, :],
                          start=False, stop=True).then_inc(sem("att_s"), 1)

            def mla_values(h):
                pe.wait_ge(sem("att_pt"), 2 * h + 2)
                if h > 1:
                    pe.wait_ge(sem("o_lo"), h - 1)
                for s in range(4):
                    mm = pe.matmul(PS[:, 2 + h % 2, 0:CTX], vm[:, s, h * P:(h + 1) * P],
                                   TMP[:, 2 + s // 2, (s % 2) * CTX:(s % 2 + 1) * CTX], start=(s == 0), stop=(s == 3))
                mm.then_inc(sem("att_o"), 1)

            mla_scores(0)
            for i in range(16):
                if i < 15:
                    mla_scores(i + 1)
                pe.wait_ge(sem("att_p"), i + 1)
                if i - 1 > 0:
                    pe.wait_ge(sem("att_pt"), i - 1)
                for s in range(4):
                    mm = pe.matmul(PS[:, 4 + i % 2, s * P:(s + 1) * P], TMP[:, i % 2, s * P:(s + 1) * P], scale_of(i, 0),
                                   start=True, stop=True)
                mm.then_inc(sem("att_t"), 1)
                if i and i % 2 == 0:
                    mla_values(i // 2 - 1)
            mla_values(7)
            linear("aout", *hl, ready=[("o_lo", 8)])
            norm_sums(False, "aout", True)
            feed_forward("f1", False, 3)
            norm_sums(False, "f1out1", True)
            item = [16]
            for l in range(2):
                full = l == 0
                sum_squares(8, 5, slice(0, T), ones[:], T)
                linear(f"kv{l}", *hx(True), each=("h_lo", 8 * (4 + 2 * l)))
                linear(f"z{l}", *hx(full))
                r, n = rng(full), (T if full else CTX)
                z0, kv0 = LIN[f"z{l}"].free0, LIN[f"kv{l}"].free0
                pe.wait_ge(sem("mix_in"), 112 * (l + 1))
                pe.wait_ge(sem("free_act"), z0 + 6)
                for i in range(4):
                    pe.matmul(PS[:, 4 + i // 2, (i % 2) * CTX:(i % 2 + 1) * CTX], drot[:, 0, :], z[:, 4 + i, LAT],
                              start=True, stop=True).then_inc(sem("rot"), 1)
                pe.wait_ge(sem("free_act"), z0 + 16)
                for s in range(4):
                    for j in range(2):
                        mm = pe.transpose(PS[:, (6, 0)[s // 2], (s % 2) * CTX + j * P:(s % 2) * CTX + (j + 1) * P],
                                          z[:, 8 + j, s * P:(s + 1) * P], ident[:])
                    if s % 2:
                        mm.then_inc(sem("vt"), 1)
                pe.wait_ge(sem("lam_prod"), l + 1)
                pe.matmul(PS[:, 1, 0:2], ones[0:32, :], small[0:32, 48:50], start=True, stop=True).then_inc(sem("lam_mm"), 1)

                def norm2(first, what):
                    for j in range(2):
                        pe.wait_ge(sem(what), 2 * l + j + 1)
                        mm = pe.matmul(PS[:, 4, r], ones[:], first(j), start=(j == 0), stop=(j == 1))
                    mm.then_inc(sem("xsum"), 1)
                    sum_squares(2, 5, r, ones[:], n)

                pe.wait_ge(sem("roped"), 5 + 4 * (l + 1))
                norm2(lambda j: z[:, 12 + j, r], "sv_in")
                toks = range(4) if full else range(2, 4)
                pe.wait_ge(sem("sv_done"), 2 * (l + 1))
                for s in toks:
                    for j in range(2):
                        mm = pe.transpose(PS[:, (2, 3)[s // 2], (s % 2) * CTX + j * P:(s % 2) * CTX + (j + 1) * P],
                                          z[:, 12 + j, s * P:(s + 1) * P], ident[:])
                mm.then_inc(sem("st_t"), 1)
                pe.wait_ge(sem("stok"), l + 1)
                for j in range(2):
                    for s in toks:
                        for gi in range(2):
                            g = 2 * j + gi
                            mm = pe.matmul(PS[64 * gi:64 * gi + 64, 2 + j, s * P:(s + 1) * P], stok[:, s, g * 64:(g + 1) * 64],
                                           sgw[:, g, :], start=True, stop=True)
                    mm.then_inc(sem("sg_mm"), 1)
                norm2(lambda j: conv[:, j, r], "conv_in")
                pe.wait_ge(sem("sg_used"), 2 * (l + 1))
                pe.wait_ge(sem("lam"), l + 1)
                pe.wait_ge(sem("vtok"), 2 * (l + 1))
                pe.wait_ge(sem("var"), ncall[0])
                items = [(h, s) for h in range(4) for s in toks]
                base = item[0]

                def scores(i):
                    h, s = items[i]
                    pe.wait_ge(sem("att_e"), base + i - 1)
                    nk = CTX if s < 2 else T
                    for j in range(2):
                        b = 64 * (h % 2) + 32 * j
                        mm = pe.matmul(PS[:, 2 * (i % 2) + j, 0:nk], z[b:b + 32, 4 + h // 2, s * P:(s + 1) * P],
                                       z[b:b + 32, 6 + h // 2, 0:nk], start=True, stop=True)
                    mm.then_inc(sem("att_s"), 1)

                def values(h):
                    pe.wait_ge(sem("att_pt"), base + (h + 1) * len(toks))
                    if h == 2:
                        pe.wait_ge(sem("ot"), 2 * l + 1)
                    for c, nks in ([(slice(0, CTX), 2)] if full else []) + [(LAT, 4)]:
                        for ks in range(nks):
                            mm = pe.matmul(PS[64 * (h % 2):64 * (h % 2) + 64, 6, c], vtok[:, ks, h * 64:(h + 1) * 64],
                                           probs_t[:, ks, c], start=(ks == 0), stop=(ks == nks - 1))
                    mm.then_inc(sem("att_o"), 1)

                scores(0)
                for i, (h, s) in enumerate(items):
                    if i + 1 < len(items):
                        scores(i + 1)
                    pe.wait_ge(sem("att_p"), base + i + 1)
                    pe.wait_ge(sem("att_pt"), base + i - 1)
                    for ks in range(2 if s < 2 else 4):
                        for j in range(2):
                            mm = pe.matmul(PS[:, 4 + i % 2, ks * P:(ks + 1) * P], probs[:, i % 2, j, ks * P:(ks + 1) * P],
                                           scale_of(i, j), start=(j == 0), stop=(j == 1))
                    mm.then_inc(sem("att_t"), 1)
                    if h and s == toks[0]:
                        values(h - 1)
                values(3)
                item[0] += len(items)
                for j in range(2):
                    sum_squares(1, 5, r, drot[:, 1, :], n)
                linear(f"wo{l}", *hx(full), ready=[("y_lo", 8 * (l + 1))])
                sum_squares(8, 5, r, ones[:], n)
                feed_forward(f"g{l}", full, 5 + 2 * l)
            sum_squares(8, 5, LAT, ones[:], CTX)

        @block.scalar
        def _(act):
            nsplit, nsq, nsd, chain = [0], [0], [0], [0]

            def split_to(n):
                while nsplit[0] < min(n, len(UNITS)):
                    u = nsplit[0]
                    s, w = w_slot(u), A["units_width"][u]
                    act.wait_ge(sem(f"raw_in{s}"), 16 * (u // RING + 1))
                    if u >= RING:
                        act.wait_ge(sem(UNITS[u - RING][3]), UNITS[u - RING][4])
                    act.activation(w_hi[:, s, 0:w], raw[:, s, 0:w], ACT.Copy).then_inc(sem("w_hi"), 1)
                    nsplit[0] += 1

            def phase(name, evacuate):
                ph = LIN[name]
                for g in range(len(ph.groups)):
                    split_to(ph.u0 + (g + 1) * ph.nch + LEAD)
                    for m in range(ph.tpg):
                        evacuate(g * ph.tpg + m, ph.t0 + g * ph.tpg + m)

            def only_split(name):
                split_to(LIN[name].u0 + len(LIN[name].groups) * LIN[name].nch + LEAD)

            def square(ap, width):
                if nsq[0] >= 2:
                    act.wait_ge(sem("sq_used"), nsq[0] - 1)
                act.activation(SQ(nsq[0])[:, 0:width], ap, ACT.Square).then_inc(sem("sq_made"), 1)
                nsq[0] += 1

            def root(ap):
                nsd[0] += 1
                act.wait_ge(sem("var"), nsd[0])
                act.activation(ap, ap, ACT.Sqrt).then_inc(sem("sd"), 1)

            act.wait_ge(sem("consts_in"), 96)
            act.activation(cond[:].rearrange("p a b c -> p (a b c)"), cond[:].rearrange("p a b c -> p (a b c)"),
                           ACT.Silu).then_inc(sem("cond"), 1)
            split_to(RING)
            for t in range(8):
                act.wait_ge(sem("h_made"), t + 1)
                act.activation(h0_hi[:, t, :], MT[:, t, :], ACT.Copy).then_inc(sem("h_hi"), 1)

            def sigmoid_o(i, t):
                act.wait_ge(sem("tile_done"), t + 1)
                act.activation(qk[:, i, :], PS[:, t % BANKS, :], ACT.Sigmoid).then_inc(sem("free_act"), 1)

            phase("og", sigmoid_o)

            def silu_xc(i):
                act.wait_ge(sem("free_dve"), LIN["up"].free0 + i + 1)
                if i == 0:
                    act.wait_ge(sem("og_out"), 64)
                act.activation(qk[:, i, :], MT[:, i % 4, :], ACT.Silu).then_inc(sem("up_c"), 1)

            def up(i, t):
                act.wait_ge(sem("tile_done"), t + 1)
                act.activation(m_hi[:, i, :], PS[:, t % BANKS, :], ACT.Copy).then_inc(sem("up_hi"), 1)
                if i:
                    silu_xc(i - 1)

            phase("up", up)
            silu_xc(15)

            def values(i, t):
                g, s = divmod(i, 4)
                act.wait_ge(sem("tile_done"), t + 1)
                act.activation(V[:, s, g * T:(g + 1) * T], PS[:, t % BANKS, :], ACT.Copy).then_inc(sem("free_act"), 1)

            phase("v", values)
            act.wait_ge(sem("gate_w_in"), 16)
            act.activation(gate_hi[:], gate_w[:], ACT.Copy).then_inc(sem("gate_whi"), 1)
            for i in range(16):
                act.activation(m_hi[:, i, :], qk[:, i, :], ACT.Copy).then_inc(sem("xc_hi"), 1)
            act.wait_ge(sem("gate_neg"), 1)
            act.activation(gates[:, 4:6, :], gates[:, 4:6, :], ACT.Exp).then_inc(sem("gate_exp"), 1)
            act.wait_ge(sem("gate_exp"), 1)
            act.activation(gates[:, 4:6, :], gates[:, 4:6, :], ACT.Ln, bias=1.0).then_inc(sem("gate_ln"), 1)

            def q_or_k(i, t):
                act.wait_ge(sem("tile_done"), t + 1)
                if i == 0:
                    act.wait_ge(sem("xc_lo"), 16)
                act.activation(qk[:, i, :], PS[:, t % BANKS, :], ACT.Copy, scale=1.0 if i < 8 else 1.0 / 16)\
                    .then_inc(sem("free_act"), 1)

            phase("qk", q_or_k)
            act.wait_ge(sem("gate_m"), 1)
            for i, (src, func, scale) in enumerate(((2, ACT.Copy, 1.0), (3, ACT.Copy, 1.0), (4, ACT.Exp, -1.0),
                                                    (5, ACT.Exp, -1.0))):
                act.activation(rows[32 * i:32 * i + 4, :], gates[:, src, :], func, scale=scale).then_inc(sem("rows"), 1)
            for h in range(NH):
                for i in range(8):
                    d, s = divmod(i, 4)
                    lo, hi = w_span(s)
                    act.wait_ge(sem("bcast"), 4 * h + 1 + d)
                    if i == 0:
                        act.wait_ge(sem("gcol"), 1)
                        if h == 0:
                            act.wait_ge(sem("rows"), 4)
                        else:
                            act.wait_ge(sem("pv"), 4 * h)
                    act.activation(WD[:, d, lo:hi], PS[:, 3 + d, q_span(s)], ACT.Exp, bias=gcol[:, d, s, h:h + 1],
                                   scale=-1.0).then_inc(sem("expw"), 1)
                for d in range(2):
                    act.wait_ge(sem("den"), 2 * h + d + 1)
                    act.activation(RD[:, d, :], PS[:, 3 + d, :], ACT.Abs).then_inc(sem("den_abs"), 1)
                for e in range(4):
                    act.wait_ge(sem("pv_used"), 4 * h + e + 1)
                    square(og[:, 4 * h + e, :], T)
                root(RD[:, 0, :])
                for e in range(4):
                    i = 4 * h + e
                    act.wait_ge(sem("hs"), i + 1)
                    act.activation(m_hi[:, i, :], og[:, i, :], ACT.Copy).then_inc(sem("hs_hi"), 1)
            only_split("mout")

            def ln_squares(full, n):
                r = rng(full)
                for t in range(8):
                    act.wait_ge(sem("xc"), 8 * n + t + 1)
                    square(X[:, t, r], T if full else CTX)
                root(RSTD[:, r])

            def hi_of_h(n, full):
                r = rng(full)
                for t in range(8):
                    act.wait_ge(sem("h_made"), 8 * n + t + 1)
                    act.activation(h_hi[:, t, r], TMP[:, t % 4, r], ACT.Copy).then_inc(sem("h_hi"), 1)

            def layer_norm(n, full, col, n_h, h_full=None):
                ln_squares(full, n)
                r = rng(full)
                for t in range(8):
                    act.wait_ge(sem("xn"), 8 * n + t + 1)
                    act.activation(X[:, t, r], X[:, t, r], ACT.Identity, bias=vec1[:, V1["ln_b"] + col + t:V1["ln_b"] + col + t + 1])\
                        .then_inc(sem("xb"), 1)
                    if n_h is not None and t:
                        hi_tile(n_h, t - 1, h_full if h_full is not None else full)
                if n_h is not None:
                    hi_tile(n_h, 7, h_full if h_full is not None else full)

            def hi_tile(n, t, full):
                r = rng(full)
                act.wait_ge(sem("h_made"), 8 * n + t + 1)
                act.activation(h_hi[:, t, r], TMP[:, t % 4, r], ACT.Copy).then_inc(sem("h_hi"), 1)

            def conv_ffn(tag, full):
                r = rng(full)
                for half in range(2):
                    ph = LIN[f"{tag}in{half}"]
                    base = hid0[tag] + 11 * half
                    for f in range(11):
                        split_to(ph.u0 + (f + 1) * ph.nch + LEAD)
                        act.wait_ge(sem("free_dve"), ph.free0 + 2 * f + 1)
                        act.activation(TMP[:, 2 + f % 2, r], TMP[:, f % 2, r], ACT.Silu).then_inc(sem("sg"), 1)
                        act.wait_ge(sem("free_dve"), ph.free0 + 2 * f + 2)
                        act.activation(hid_hi[:, f, r], TMP[:, 4 + f % 2, r], ACT.Copy).then_inc(sem("hid_hi"), 1)
                    only_split(f"{tag}out{half}")

            def mlp(tag, full):
                r = rng(full)
                for half in range(2):
                    ph = LIN[f"{tag}in{half}"]
                    base = hid0[tag] + 16 * half

                    def hi(i):
                        act.wait_ge(sem("prod"), base - 44 + i + 1)
                        act.activation(hid_hi[:, i, r], TMP[:, 4 + i % 2, r], ACT.Copy).then_inc(sem("hid_hi"), 1)

                    def relu(i, t):
                        act.wait_ge(sem("tile_done"), t + 1)
                        if base - 44 + i >= 2:
                            act.wait_ge(sem("prod"), base - 44 + i - 1)
                        act.activation(TMP[:, i % 2, r], PS[:, t % BANKS, r], ACT.Relu).then_inc(sem("free_act"), 1)
                        if i:
                            hi(i - 1)

                    phase(f"{tag}in{half}", relu)
                    hi(15)
                    only_split(f"{tag}out{half}")

            layer_norm(0, True, 0, 1)
            conv_ffn("f0", True)
            layer_norm(1, True, 8, 2)

            def copy_to(aps, full=True):
                def evacuate(i, t):
                    act.wait_ge(sem("tile_done"), t + 1)
                    act.activation(aps(i), PS[:, t % BANKS, rng(full)], ACT.Copy).then_inc(sem("free_act"), 1)
                return evacuate

            phase("dkv", copy_to(lambda i: ckv[:, i, :]))
            phase("dkr", copy_to(lambda i: kr[:, :]))
            phase("dq", copy_to(lambda i: cq[:, i, :], False))
            for t in range(2):
                act.wait_ge(sem("free_act"), LIN["dkv"].free0 + t + 1)
                square(ckv[:, t, :], T)
            root(RSTD)
            for t in range(3):
                act.wait_ge(sem("free_act"), LIN["dq"].free0 + t + 1)
                square(cq[:, t, :], CTX)
            root(MEAN[:, 0:CTX])
            for i in range(5):
                act.wait_ge(sem("c_made"), i + 1)
                dst, src = (ckv_hi[:, i, :], ckv[:, i, :]) if i < 2 else (cq_hi[:, i - 2, :], cq[:, i - 2, :])
                act.activation(dst, src, ACT.Copy).then_inc(sem("c_hi"), 1)
            phase("uqn", copy_to(lambda i: qn[:, i, :], False))
            phase("uqr", copy_to(lambda i: qr[:, i, :], False))
            phase("ukn", copy_to(lambda i: kn[:, i, :]))
            phase("ukv", copy_to(lambda i: vm[:, i % 4, (i // 4) * T:(i // 4 + 1) * T]))
            natt = [0]

            def att_copy(i):
                act.wait_ge(sem("att_t"), i + 1)
                if i // 2 > 0:
                    act.wait_ge(sem("att_o"), i // 2)
                dst = TMP[:, 2:4, :].rearrange("p a (b q) -> p (a b) q", q=CTX)[:, :, (i % 2) * P:(i % 2 + 1) * P]
                act.activation(dst, PS[:, 4 + i % 2, :].rearrange("p (s q) -> p s q", s=4), ACT.Copy)\
                    .then_inc(sem("att_pt"), 1)

            def o_hi(h):
                act.wait_ge(sem("att_o"), h + 1)
                act.activation(h_hi[:, h, LAT], PS[:, 2 + h % 2, 0:CTX], ACT.Copy).then_inc(sem("o_hi"), 1)

            only_split("ukv")
            for i in range(16):
                act.wait_ge(sem("att_nb"), i + 1)
                c = 8 * (i % 2)
                act.activation(TMP[:, i % 2, :], PS[:, i % 2, :], ACT.Exp, bias=small[:, 8 + c:9 + c], scale=MLA_SCALE,
                               accum_out=small[:, 9 + c:10 + c]).then_inc(sem("att_e"), 1)
                if i:
                    att_copy(i - 1)
                if i >= 3 and i % 2:
                    o_hi((i - 3) // 2)
            att_copy(15)
            o_hi(7)
            only_split("aout")
            layer_norm(2, False, 16, 3)
            conv_ffn("f1", False)
            layer_norm(3, False, 24, None)

            def rms(n_h, full, chunk, par, first):
                r = rng(full)
                for t in range(8):
                    what, value = first(t)
                    act.wait_ge(sem(what), value)
                    square(X[:, t, r], T if full else CTX)
                root(RSTD[:, r])
                for t in range(8):
                    act.wait_ge(sem("h_made"), 8 * n_h + t + 1)
                    for i, (c, v) in enumerate(halves(full)):
                        ins = act.activation(h_hi[:, t, c], TMP[:, t % 4, c], ACT.Identity,
                                             bias=mod[:, par, 8 * chunk + t, v:v + 1])
                    ins.then_inc(sem("h_hi"), 1)

            ny, item = [0], [16]
            for l in range(2):
                full = l == 0
                r, n = rng(full), (T if full else CTX)
                if l == 0:
                    act.wait_ge(sem("ctx2_in"), 16)
                    rms(4, True, 0, 0, lambda t: ("xb", 32))
                else:
                    rms(6, True, 0, 1, lambda t: ("free_dve", LIN["g0out1"].free0 + LIN["g0out1"].n_tiles - 8 + t + 1))
                parts = [0, 1, 2, 5, 6, 7, 8, 9]
                phase(f"kv{l}", copy_to(lambda i: z[:, 6 + i, :]))
                z_out = copy_to(lambda i: z[:, 2 * parts[i // 2] + i % 2, r], full)

                def z_tile(i, t):
                    z_out(i, t)
                    if i == 4:
                        for j in range(2):
                            act.wait_ge(sem("free_act"), LIN[f"z{l}"].free0 + 3 + j)
                            act.activation(z[:, 2 + j, r], z[:, 2 + j, r], ACT.Sigmoid).then_inc(sem("sig"), 1)

                phase(f"z{l}", z_tile)
                only_split(f"z{l}")
                z0 = LIN[f"z{l}"].free0
                act.wait_ge(sem("free_act"), z0 + 16)
                for j in range(2):
                    act.activation(z[:, 12 + j, r], z[:, 12 + j, r], ACT.Gelu_apprx_tanh).then_inc(sem("sv_in"), 1)
                for j in range(2):
                    act.activation(z[:, 10 + j, r], z[:, 10 + j, r], ACT.Gelu_apprx_tanh).then_inc(sem("gelu_u"), 1)
                for i in range(2):
                    act.wait_ge(sem("vt"), 2 * l + i + 1)
                    act.activation(vtok[:, 2 * i:2 * i + 2, :].rearrange("p s e -> p (s e)"), PS[:, (6, 0)[i], :], ACT.Copy)\
                        .then_inc(sem("vtok"), 1)
                act.wait_ge(sem("lam_mm"), l + 1)
                act.activation(small[:, 50:52], PS[:, 1, 0:2], ACT.Exp).then_inc(sem("lam_exp"), 1)
                def y_hi(j):
                    ny[0] += 1
                    act.wait_ge(sem("y_made"), ny[0] - 2 * l - (2 if j in (2, 3) else 0))
                    act.activation(h_hi[:, j, r], TMP[:, (ny[0] - 1) % 4, r], ACT.Copy).then_inc(sem("y_hi"), 1)

                for j in (6, 7):
                    y_hi(j)
                for j in range(2):
                    act.wait_ge(sem("n2_xc"), 4 * l + j + 1)
                    square(z[:, 12 + j, r], n)
                root(RSTD[:, r])
                for j in range(2):
                    act.wait_ge(sem("sv_n"), 2 * l + j + 1)
                    b = V2["sg_ln_b_2"] + 2 * l + j
                    act.activation(z[:, 12 + j, r], z[:, 12 + j, r], ACT.Identity, bias=vec2[:, b:b + 1])\
                        .then_inc(sem("sv_done"), 1)
                act.wait_ge(sem("st_t"), l + 1)
                for i in (range(2) if full else range(1, 2)):
                    ins = act.activation(stok[:, 2 * i:2 * i + 2, :].rearrange("p s e -> p (s e)"), PS[:, 2 + i, :], ACT.Copy)
                ins.then_inc(sem("stok"), 1)

                for j in (4, 5):
                    y_hi(j)
                for j in range(2):
                    act.wait_ge(sem("n2_xc"), 4 * l + 2 + j + 1)
                    square(conv[:, j, r], n)
                root(RSTD[:, r])
                for j in range(2):
                    act.wait_ge(sem("conv_n"), 2 * l + j + 1)
                    g, b = V2["ln_a_g_2"] + 2 * l + j, V2["ln_a_b_2"] + 2 * l + j
                    act.wait_ge(sem("y_lo"), ny[0] - 3)
                    act.activation(TMP[:, ny[0] % 4, r], conv[:, j, r], ACT.Silu, bias=vec2[:, b:b + 1],
                                   scale=vec2[:, g:g + 1]).then_inc(sem("conv_y"), 1)
                    act.wait_ge(sem("conv_y"), 2 * l + j + 1)
                    ny[0] += 1
                    act.activation(h_hi[:, j, r], TMP[:, (ny[0] - 1) % 4, r], ACT.Copy).then_inc(sem("y_hi"), 1)
                toks = range(4) if full else range(2, 4)
                items = [(h, s) for h in range(4) for s in toks]
                base = item[0]

                def probs_copy(i):
                    h, s = items[i]
                    nks = 2 if s < 2 else 4
                    act.wait_ge(sem("att_t"), base + i + 1)
                    if h:
                        act.wait_ge(sem("att_o"), 8 + 4 * l + h)
                    act.activation(probs_t[:, 0:nks, s * P:(s + 1) * P],
                                   PS[:, 4 + i % 2, 0:nks * P].rearrange("p (s q) -> p s q", q=P), ACT.Copy)\
                        .then_inc(sem("att_pt"), 1)

                for i, (h, s) in enumerate(items):
                    nk = CTX if s < 2 else T
                    c = 8 + 8 * (i % 2)
                    act.wait_ge(sem("att_nb"), base + i + 1)
                    for j in range(2):
                        ins = act.activation(probs[:, i % 2, j, 0:nk], PS[:, 2 * (i % 2) + j, 0:nk], ACT.Exp,
                                             bias=small[:, c + j:c + j + 1], scale=DIFF_SCALE,
                                             accum_out=small[:, c + 2 + j:c + 3 + j])
                    ins.then_inc(sem("att_e"), 1)
                    if i:
                        probs_copy(i - 1)
                probs_copy(len(items) - 1)
                item[0] += len(items)
                for j in range(2):
                    act.wait_ge(sem("ot"), 2 * l + j + 1)
                    square(TMP[:, j, r], n)
                    root(RSTD[:, r])
                for j in (2, 3):
                    y_hi(j)
                only_split(f"wo{l}")
                rms(5 + 2 * l, full, 3, l, lambda t: ("free_dve", LIN[f"wo{l}"].free0 + t + 1))
                mlp(f"g{l}", full)
            ph = LIN["g1out1"]
            for t in range(8):
                act.wait_ge(sem("free_dve"), ph.free0 + t + 1)
                square(X[:, t, LAT], CTX)
            root(RSTD[:, LAT])

        @block.vector
        def _(dve):
            nstep = [0]
            nsplit, nvar, chain, nmean, ny, natt, nmod = [0], [0], [0], [0], [0], [0], [0]

            def split_to(n):
                while nsplit[0] < min(n, len(UNITS)):
                    u = nsplit[0]
                    s, w = w_slot(u), A["units_width"][u]
                    dve.wait_ge(sem("w_hi"), u + 1)
                    dve.tensor_tensor(w_lo[:, s, 0:w], raw[:, s, 0:w], w_hi[:, s, 0:w].bitcast(F32), ALU.subtract)\
                        .then_inc(sem("w_split"), 1)
                    nsplit[0] += 1
                    for i, (at, a, k) in enumerate(ADA_MACS):
                        if at == u:
                            modulation_unit(i, a, k)

            def modulation_unit(n, a, k):
                dve.wait_ge(sem(f"ada_in{n % ADA_RING}"), 16 * (n // ADA_RING + 1))
                if k == 0:
                    dve.wait_ge(sem("ada_sum"), a - 1)
                blk, nv = a // (2 * ADA_LAYER), ada_conds(a)
                for kk in range(2):
                    w = ada_ring[:, n % ADA_RING, kk * ADA_W:(kk + 1) * ADA_W]
                    for v in range(nv):
                        acc, c = ada_acc[:, a % 2, v, :], cond[:, blk, 2 * k + kk, v:v + 1]
                        if k == 0 and kk == 0:
                            dve.tensor_scalar(acc, w, c, None, ALU.mult).then_inc(sem("ada_mac"), 1)
                        else:
                            dve.wait_ge(sem("ada_mac"), nstep[0] - nv + 1)
                            dve.scalar_tensor_tensor(out=acc, in0=w, scalar=c, in1=acc, op0=ALU.mult, op1=ALU.add)\
                                .then_inc(sem("ada_mac"), 1)
                        nstep[0] += 1

            def chained():
                chain[0] += 1
                return chain[0]

            def phase(name, evacuate):
                ph = LIN[name]
                for g in range(len(ph.groups)):
                    split_to(ph.u0 + (g + 1) * ph.nch + LEAD)
                    for m in range(ph.tpg):
                        evacuate(g * ph.tpg + m, ph.t0 + g * ph.tpg + m)

            def only_split(name):
                split_to(LIN[name].u0 + len(LIN[name].groups) * LIN[name].nch + LEAD)

            def rstd(bank, count, cols, dst):
                nvar[0] += 1
                dve.wait_ge(sem("sq_used"), nsq_after[nvar[0] - 1])
                dve.tensor_scalar(dst, PS[:, bank, cols], 1.0 / count, EPS, ALU.mult, ALU.add).then_inc(sem("var"), 1)
                dve.wait_ge(sem("sd"), nvar[0])
                dve.reciprocal(dst, dst).then_inc(sem("dve_chain"), 1)
                dve.wait_ge(sem("dve_chain"), chained())

            def mean(count, cols):
                nmean[0] += 1
                dve.wait_ge(sem("xsum"), nmean[0])
                dve.tensor_scalar(MEAN[:, cols], PS[:, 4, cols], 1.0 / count, None, ALU.mult).then_inc(sem("dve_chain"), 1)
                dve.wait_ge(sem("dve_chain"), chained())

            def modulation(layer, lo, hi, nv=2, gains=(), summed=0):
                par = layer % 2
                dve.wait_ge(sem("ada_sum"), max(ADA_LAYER * layer + hi // 2, summed))
                vec, at = (vec1, V1["ada_b"]) if layer < 2 else (vec2, V2["ada_b_2"])
                at += 48 * par
                sums = PS[:, 7, 96 * par + 2 * lo:96 * par + 2 * hi].rearrange("p (m v) -> p m v", v=2)[:, :, 0:nv]
                bias = vec[:, at + lo:at + hi].rearrange("p (m v) -> p m v", v=1).broadcast_to([P, hi - lo, nv])
                dve.tensor_tensor(mod[:, par, lo:hi, 0:nv], sums, bias, ALU.add).then_inc(sem("mod_read"), 1)
                nmod[0] += 1
                dve.wait_ge(sem("mod_read"), nmod[0])
                for chunk in (1, 4):
                    if lo <= 8 * chunk < hi:
                        scale = mod[:, par, 8 * chunk:8 * chunk + 8, 0:nv]
                        dve.tensor_scalar(scale, scale, 1.0, None, ALU.add).then_inc(sem("dve_chain"), 1)
                        dve.wait_ge(sem("dve_chain"), chained())
                        if gains:
                            g = gains[chunk // 3]
                            gain = vec2[:, g:g + 8].rearrange("p (m v) -> p m v", v=1).broadcast_to([P, 8, nv])
                            dve.tensor_tensor(scale, scale, gain, ALU.mult).then_inc(sem("dve_chain"), 1)
                            dve.wait_ge(sem("dve_chain"), chained())

            def scalar(par, chunk, t, v):
                return mod[:, par, 8 * chunk + t, v:v + 1]

            modulation(0, 0, 16)
            split_to(RING)
            dve.wait_ge(sem("x0_in"), 16)
            for t in range(8):
                for c, v in halves(True):
                    ins = dve.tensor_scalar(MT[:, t, c], MT[:, t, c], scalar(0, 1, t, v), scalar(0, 0, t, v), ALU.mult, ALU.add)
                ins.then_inc(sem("h_made"), 1)
            for t in range(8):
                dve.wait_ge(sem("h_hi"), t + 1)
                dve.tensor_tensor(h0_lo[:, t, :], MT[:, t, :], h0_hi[:, t, :].bitcast(F32), ALU.subtract)\
                    .then_inc(sem("h_lo"), 1)
            only_split("og")

            def segments(ap):
                return ap.rearrange("p (s n) -> p s n", n=CTX)

            def conv3(dst, src, taps, bias=None, last=None):
                d, s = segments(dst), segments(src)
                if bias is not None:
                    dve.tensor_scalar(dst, src, taps[1], bias, ALU.mult, ALU.add).then_inc(sem("dve_chain"), 1)
                    dve.wait_ge(sem("dve_chain"), chained())
                else:
                    dve.tensor_scalar(dst, src, taps[1], None, ALU.mult).then_inc(sem("dve_chain"), 1)
                    dve.wait_ge(sem("dve_chain"), chained())
                dve.scalar_tensor_tensor(out=d[:, :, 1:], in0=s[:, :, 0:CTX - 1], scalar=taps[0], in1=d[:, :, 1:],
                                         op0=ALU.mult, op1=ALU.add).then_inc(sem("dve_chain"), 1)
                dve.wait_ge(sem("dve_chain"), chained())
                ins = dve.scalar_tensor_tensor(out=d[:, :, 0:CTX - 1], in0=s[:, :, 1:], scalar=taps[2],
                                               in1=d[:, :, 0:CTX - 1], op0=ALU.mult, op1=ALU.add)
                if last:
                    ins.then_inc(sem(last), 1)
                else:
                    ins.then_inc(sem("dve_chain"), 1)
                    dve.wait_ge(sem("dve_chain"), chained())

            def col(vec, at):
                return vec[:, at:at + 1]

            def up(i, t):
                b = t % BANKS
                dve.wait_ge(sem("up_hi"), i + 1)
                dve.tensor_tensor(m_lo[:, i, :], PS[:, b, :], m_hi[:, i, :].bitcast(F32), ALU.subtract)\
                    .then_inc(sem("up_lo"), 1)
                if i == 0:
                    dve.wait_ge(sem("h_lo"), 8)
                if i - 3 > 0:
                    dve.wait_ge(sem("up_c"), i - 3)
                taps = [col(vec1, V1["m_conv_w"] + 16 * k + i) for k in range(3)]
                conv3(MT[:, i % 4, :], PS[:, b, :], taps, col(vec1, V1["m_conv_b"] + i), last="free_dve")

            phase("up", up)
            only_split("v")
            dve.wait_ge(sem("gate_whi"), 1)
            dve.tensor_tensor(gate_lo[:], gate_w[:], gate_hi[:].bitcast(F32), ALU.subtract).then_inc(sem("gate_wlo"), 1)
            for i in range(16):
                dve.wait_ge(sem("xc_hi"), i + 1)
                dve.tensor_tensor(m_lo[:, i, :], qk[:, i, :], m_hi[:, i, :].bitcast(F32), ALU.subtract)\
                    .then_inc(sem("xc_lo"), 1)
            dve.wait_ge(sem("gate_mm"), 1)
            dve.tensor_copy(gate_all[:], PS[0:16, 4, :]).then_inc(sem("gate_all"), 1)
            for q in range(4):
                dve.wait_ge(sem("gate_rows"), q + 1)
                dve.tensor_scalar(gates[:, q, :], PS[0:4, (4, 5, 6, 3)[q], :], small[0:4, q:q + 1], None, ALU.add)\
                    .then_inc(sem("gate_pre"), 1)
            dve.wait_ge(sem("gate_pre"), 4)
            dve.tensor_scalar(gates[:, 4:6, :], gates[:, 2:4, :], -1.0, None, ALU.mult).then_inc(sem("dve_chain"), 1)
            dve.wait_ge(sem("dve_chain"), chained())
            dve.tensor_tensor(gates[:, 4:6, :], gates[:, 4:6, :], gates[:, 2:4, :], ALU.min).then_inc(sem("gate_neg"), 1)
            dve.wait_ge(sem("gate_ln"), 1)
            dve.tensor_scalar(gates[:, 2:4, :], gates[:, 2:4, :], 0.0, None, ALU.min).then_inc(sem("dve_chain"), 1)
            dve.wait_ge(sem("dve_chain"), chained())
            dve.tensor_tensor(gates[:, 2:4, :], gates[:, 2:4, :], gates[:, 4:6, :], ALU.subtract)\
                .then_inc(sem("dve_chain"), 1)
            dve.wait_ge(sem("dve_chain"), chained())

            def scan(dst, src, op, backward):
                d, s = gates[:, dst, :], gates[:, src, :]
                if not backward:
                    dve.tensor_tensor_scan(d, s, s, 0.0, op, ALU.bypass).then_inc(sem("dve_chain"), 1)
                    dve.wait_ge(sem("dve_chain"), chained())
                    return
                dve.tensor_tensor_scan(d[:, 0:CTX][:, ::-1], s[:, 0:CTX][:, ::-1], s[:, 0:CTX][:, ::-1], 0.0, op, ALU.bypass)\
                    .then_inc(sem("dve_chain"), 1)
                dve.wait_ge(sem("dve_chain"), chained())
                dve.tensor_tensor_scan(d[:, LAT][:, ::-1], s[:, LAT][:, ::-1], s[:, LAT][:, ::-1], d[:, 0:1], op, ALU.bypass)\
                    .then_inc(sem("dve_chain"), 1)
                dve.wait_ge(sem("dve_chain"), chained())

            scan(4, 2, ALU.add, False)
            scan(5, 3, ALU.add, True)
            dve.tensor_tensor(gates[:, 0:2, :], gates[:, 0:2, :], gates[:, 4:6, :], ALU.subtract).then_inc(sem("gate_g"), 1)
            dve.wait_ge(sem("gate_g"), 1)
            scan(2, 0, ALU.max, False)
            scan(3, 1, ALU.max, True)
            dve.tensor_tensor(gates[:, 4:6, :], gates[:, 4:6, :], gates[:, 2:4, :], ALU.add).then_inc(sem("gate_m"), 1)
            only_split("qk")
            modulation(0, 16, 48, summed=summed_before("mout"))
            dve.wait_ge(sem("gcol_t"), 1)
            dve.tensor_copy(small[:, 8:40], PS[:, 4, 0:32]).then_inc(sem("gcol"), 1)
            dve.wait_ge(sem("gcol"), 1)
            dve.wait_ge(sem("rows"), 4)
            def heads_lo(h):
                for e in range(4):
                    i = 4 * h + e
                    dve.wait_ge(sem("hs_hi"), i + 1)
                    dve.tensor_tensor(m_lo[:, i, :], og[:, i, :], m_hi[:, i, :].bitcast(F32), ALU.subtract)\
                        .then_inc(sem("hs_lo"), 1)

            for h in range(NH):
                for d in range(2):
                    for s in range(4):
                        lo, hi = w_span(s)
                        dve.wait_ge(sem("expw"), 8 * h + 4 * d + s + 1)
                        dve.wait_ge(sem("scores"), 4 * h + (s + 1 if s < 2 else 4))
                        score = PS[:, s, :] if s < 2 else PS[:, 2, (s - 2) * CTX:(s - 1) * CTX]
                        dve.scalar_tensor_tensor(out=WD[:, d, lo:hi], in0=WD[:, d, lo:hi], scalar=1.0, in1=score,
                                                 op0=ALU.min, op1=ALU.mult).then_inc(sem("wraw"), 1)
                dve.wait_ge(sem("bcast"), 4 * h + 4)
                for d in range(2):
                    dve.wait_ge(sem("den_abs"), 2 * h + d + 1)
                    dve.tensor_tensor(RD[:, d, :], RD[:, d, :], PS[:, 5 + d, :], ALU.max).then_inc(sem("dve_chain"), 1)
                    dve.wait_ge(sem("dve_chain"), chained())
                    dve.reciprocal(RD[:, d, :], RD[:, d, :]).then_inc(sem("dve_chain"), 1)
                    dve.wait_ge(sem("dve_chain"), chained())
                for s in range(4):
                    lo, hi = w_span(s)
                    dve.tensor_tensor(WD[:, 0, lo:hi], WD[:, 0, lo:hi], RD[:, 0, q_span(s)], ALU.mult)
                    dve.tensor_tensor(WD[:, 1, lo:hi], WD[:, 1, lo:hi], RD[:, 1, q_span(s)], ALU.mult)\
                        .then_inc(sem("dve_chain"), 1)
                    dve.wait_ge(sem("dve_chain"), chained())
                    dve.tensor_tensor(WD[:, 0, lo:hi], WD[:, 0, lo:hi], WD[:, 1, lo:hi], ALU.add).then_inc(sem("wsum"), 1)
                if h:
                    heads_lo(h - 1)
                dve.wait_ge(sem("og_in"), 16)
                for e in range(4):
                    i = 4 * h + e
                    dve.wait_ge(sem("pv"), i + 1)
                    dve.tensor_tensor(og[:, i, :], og[:, i, :], PS[:, (0, 1, 2, 5)[e], :], ALU.mult).then_inc(sem("pv_used"), 1)
                rstd(6, T, slice(0, T), RD[:, 0, :])
                for e in range(4):
                    i = 4 * h + e
                    dve.scalar_tensor_tensor(out=og[:, i, :], in0=og[:, i, :], scalar=col(vec1, V1["m_norm_g"] + i),
                                             in1=RD[:, 0, :], op0=ALU.mult, op1=ALU.mult).then_inc(sem("hs"), 1)
            heads_lo(NH - 1)
            dve.wait_ge(sem("x_in"), 16)
            dve.tensor_scalar(X[:, :, :], X[:, :, :], ALPHA, None, ALU.mult).then_inc(sem("dve_chain"), 1)
            dve.wait_ge(sem("dve_chain"), chained())

            def residual(name, full, par, chunk):
                def evacuate(i, t):
                    dve.wait_ge(sem("tile_done"), t + 1)
                    if LIN[name].free0 + i >= 8:
                        dve.wait_ge(sem("free_dve"), LIN[name].free0 + i)
                    for c, v in halves(full):
                        ins = dve.scalar_tensor_tensor(out=X[:, i, c], in0=PS[:, t % BANKS, c], scalar=scalar(par, chunk, i, v),
                                                       in1=X[:, i, c], op0=ALU.mult, op1=ALU.add)
                    ins.then_inc(sem("free_dve"), 1)
                phase(name, evacuate)

            residual("mout", True, 0, 2)

            def h_tile(n, t, full, par, chunk, first):
                r = rng(full)
                what, value = first
                dve.wait_ge(sem(what), value)
                if t >= 4:
                    dve.wait_ge(sem("h_lo"), 8 * n + t - 3)
                for c, v in halves(full):
                    ins = dve.tensor_scalar(TMP[:, t % 4, c], X[:, t, c], scalar(par, chunk + 1, t, v),
                                            scalar(par, chunk, t, v), ALU.mult, ALU.add)
                ins.then_inc(sem("h_made"), 1)

            def h_lo_tile(n, t, full):
                r = rng(full)
                dve.wait_ge(sem("h_hi"), 8 * n + t + 1)
                dve.tensor_tensor(h_lo[:, t, r], TMP[:, t % 4, r], h_hi[:, t, r].bitcast(F32), ALU.subtract)\
                    .then_inc(sem("h_lo"), 1)

            def layer_norm(n, full, gcol_at, n_h, par=0, chunk=0):
                r = rng(full)
                mean(D, r)
                for t in range(8):
                    dve.tensor_tensor(X[:, t, r], X[:, t, r], MEAN[:, r], ALU.subtract).then_inc(sem("xc"), 1)
                rstd(5, D, r, RSTD[:, r])
                for t in range(8):
                    dve.scalar_tensor_tensor(out=X[:, t, r], in0=X[:, t, r], scalar=col(vec1, V1["ln_g"] + gcol_at + t),
                                             in1=RSTD[:, r], op0=ALU.mult, op1=ALU.mult).then_inc(sem("xn"), 1)
                    if n_h is not None and t:
                        h_tile(n_h, t - 1, full, par, chunk, ("xb", 8 * n + t))
                    if n_h is not None and t > 1:
                        h_lo_tile(n_h, t - 2, full)
                if n_h is not None:
                    h_tile(n_h, 7, full, par, chunk, ("xb", 8 * n + 8))
                    h_lo_tile(n_h, 6, full)
                    h_lo_tile(n_h, 7, full)

            def conv_ffn(tag, layer, full):
                r = rng(full)
                dve.tensor_scalar(X[:, :, r], X[:, :, r], ALPHA, None, ALU.mult).then_inc(sem("dve_chain"), 1)
                dve.wait_ge(sem("dve_chain"), chained())
                for half in range(2):
                    ph = LIN[f"{tag}in{half}"]
                    base = hid0[tag] + 11 * half

                    def lo(f):
                        dve.wait_ge(sem("hid_hi"), base + f + 1)
                        dve.tensor_tensor(hid_lo[:, f, r], TMP[:, 4 + f % 2, r], hid_hi[:, f, r].bitcast(F32), ALU.subtract)\
                            .then_inc(sem("hid_lo"), 1)

                    for f in range(11):
                        split_to(ph.u0 + (f + 1) * ph.nch + LEAD)
                        tile = 11 * half + f
                        t = ph.t0 + 2 * f
                        taps = [col(vec1, V1["ffn_conv_w"] + (3 * layer + k) * FFN_T + tile) for k in range(3)]
                        bias = col(vec1, V1["ffn_conv_b"] + layer * FFN_T + tile)
                        dve.wait_ge(sem("tile_done"), t + 1)
                        if base + f - 1 > 0:
                            dve.wait_ge(sem("sg"), base + f - 1)
                        conv3(TMP[:, f % 2, r], PS[:, t % BANKS, r], taps, bias, last="free_dve")
                        if f:
                            lo(f - 1)
                        dve.wait_ge(sem("tile_done"), t + 2)
                        dve.wait_ge(sem("sg"), base + f + 1)
                        if base + f - 1 > 0:
                            dve.wait_ge(sem("hid_lo"), base + f - 1)
                        dve.tensor_tensor(TMP[:, 4 + f % 2, r], TMP[:, 2 + f % 2, r], PS[:, (t + 1) % BANKS, r], ALU.mult)\
                            .then_inc(sem("free_dve"), 1)
                    lo(10)
                    residual(f"{tag}out{half}", full, layer, 5)

            layer_norm(0, True, 0, 1, 0, 3)
            conv_ffn("f0", 0, True)
            modulation(1, 0, 16, summed=summed_before("dkv"))
            modulation(1, 16, 48, 1, summed=summed_before("dkv"))
            layer_norm(1, True, 8, 2, 1, 0)
            dve.tensor_scalar(X[:, :, LAT], X[:, :, LAT], ALPHA, None, ALU.mult).then_inc(sem("dve_chain"), 1)
            dve.wait_ge(sem("dve_chain"), chained())
            only_split("dkv")
            only_split("dkr")
            only_split("dq")
            rstd(5, CTX, slice(0, T), RSTD)
            for t in range(2):
                dve.scalar_tensor_tensor(out=ckv[:, t, :], in0=ckv[:, t, :], scalar=col(vec1, V1["a_kv_norm"] + t),
                                         in1=RSTD, op0=ALU.mult, op1=ALU.mult).then_inc(sem("c_made"), 1)
            rstd(5, 3 * P, slice(0, CTX), MEAN[:, 0:CTX])
            for t in range(3):
                dve.scalar_tensor_tensor(out=cq[:, t, :], in0=cq[:, t, :], scalar=col(vec1, V1["a_q_norm"] + t),
                                         in1=MEAN[:, 0:CTX], op0=ALU.mult, op1=ALU.mult).then_inc(sem("c_made"), 1)
            for i in range(5):
                dve.wait_ge(sem("c_hi"), i + 1)
                dst, src, hi = ((ckv_lo, ckv, ckv_hi) if i < 2 else (cq_lo, cq, cq_hi))
                j = i if i < 2 else i - 2
                dve.tensor_tensor(dst[:, j, :], src[:, j, :], hi[:, j, :].bitcast(F32), ALU.subtract).then_inc(sem("c_lo"), 1)
            for name in ("uqn", "uqr", "ukn", "ukv"):
                only_split(name)

            def rotate(i, n, n0, ap, table):
                dve.wait_ge(sem("rot"), n0 + min(i // 2 * 2 + 2, n))
                tmp = TMP[:, i, 0:CTX]
                dve.tensor_tensor(tmp, PS[:, 4 + i // 2, (i % 2) * CTX:(i % 2 + 1) * CTX], table[:, 1, :], ALU.mult)
                dve.tensor_tensor(ap, ap, table[:, 0, :], ALU.mult).then_inc(sem("dve_chain"), 1)
                dve.wait_ge(sem("dve_chain"), chained())
                dve.tensor_tensor(ap, ap, tmp, ALU.add).then_inc(sem("roped"), 1)

            for i in range(5):
                rotate(i, 5, 0, kr[:, LAT] if i == 4 else qr[:, i, :], arope)
            dve.wait_ge(sem("roped"), 5)

            def mla_probs(i):
                c = 8 * (i % 2)
                dve.wait_ge(sem("att_e"), i + 1)
                dve.reciprocal(small[:, 11 + c:12 + c], small[:, 9 + c:10 + c]).then_inc(sem("dve_chain"), 1)
                dve.wait_ge(sem("dve_chain"), chained())
                dve.tensor_scalar(scale_of(i, 0), ident[:], small[:, 11 + c:12 + c], None, ALU.mult)\
                    .then_inc(sem("att_p"), 1)

            def o_lo(h):
                dve.wait_ge(sem("o_hi"), h + 1)
                dve.tensor_tensor(h_lo[:, h, LAT], PS[:, 2 + h % 2, 0:CTX], h_hi[:, h, LAT].bitcast(F32), ALU.subtract)\
                    .then_inc(sem("o_lo"), 1)

            for i in range(16):
                c = 8 * (i % 2)
                dve.wait_ge(sem("att_s"), i + 1)
                dve.tensor_reduce(small[:, 10 + c:11 + c], PS[:, i % 2, :], AX_X, ALU.max).then_inc(sem("dve_chain"), 1)
                dve.wait_ge(sem("dve_chain"), chained())
                dve.tensor_scalar(small[:, 8 + c:9 + c], small[:, 10 + c:11 + c], -MLA_SCALE, None, ALU.mult)\
                    .then_inc(sem("att_nb"), 1)
                mla_probs(i)
                if i >= 3 and i % 2:
                    o_lo((i - 3) // 2)
            o_lo(7)
            residual("aout", False, 1, 2)
            layer_norm(2, False, 16, 3, 1, 3)
            conv_ffn("f1", 1, False)
            dve.wait_ge(sem("vec2_in"), 16)
            modulation(2, 0, 48, gains=(V2["norm1_g_2"], V2["norm2_g_2"]), summed=summed_before("kv0"))
            layer_norm(3, False, 24, None)

            def rms(n_h, full, par, chunk):
                r = rng(full)
                rstd(5, D, r, RSTD[:, r])

                def lo(t):
                    dve.wait_ge(sem("h_hi"), 8 * n_h + t + 1)
                    for c, v in halves(full):
                        ins = dve.scalar_tensor_tensor(out=h_lo[:, t, c], in0=TMP[:, t % 4, c], scalar=scalar(par, chunk, t, v),
                                                       in1=h_hi[:, t, c].bitcast(F32), op0=ALU.add, op1=ALU.subtract)
                    ins.then_inc(sem("h_lo"), 1)

                for t in range(8):
                    if t >= 4:
                        dve.wait_ge(sem("h_lo"), 8 * n_h + t - 3)
                    for c, v in halves(full):
                        ins = dve.scalar_tensor_tensor(out=TMP[:, t % 4, c], in0=X[:, t, c], scalar=scalar(par, chunk + 1, t, v),
                                                       in1=RSTD[:, c], op0=ALU.mult, op1=ALU.mult)
                    ins.then_inc(sem("h_made"), 1)
                    if t:
                        lo(t - 1)
                lo(7)

            def mlp(tag, full, par):
                r = rng(full)
                for half in range(2):
                    name = f"{tag}in{half}"
                    base = hid0[tag] + 16 * half

                    def lo(i):
                        dve.wait_ge(sem("hid_hi"), base + i + 1)
                        dve.tensor_tensor(hid_lo[:, i, r], TMP[:, 4 + i % 2, r], hid_hi[:, i, r].bitcast(F32), ALU.subtract)\
                            .then_inc(sem("hid_lo"), 1)

                    def square_relu(i, t):
                        dve.wait_ge(sem("free_act"), LIN[name].free0 + i + 1)
                        dve.wait_ge(sem("hid_lo"), base + i - 1)
                        dve.tensor_tensor(TMP[:, 4 + i % 2, r], TMP[:, i % 2, r], TMP[:, i % 2, r], ALU.mult)\
                            .then_inc(sem("prod"), 1)
                        if i:
                            lo(i - 1)

                    phase(name, square_relu)
                    lo(15)
                    residual(f"{tag}out{half}", full, par, 5)

            natt[0] = 16
            for l in range(2):
                full = l == 0
                r, n = rng(full), (T if full else CTX)
                toks = range(4) if full else range(2, 4)
                if l:
                    gains = (V2["norm1_g_2"] + 8, V2["norm2_g_2"] + 8)
                    modulation(3, 0, 16, gains=gains)
                    modulation(3, 16, 48, 1, gains)
                rms(4 + 2 * l, True, l, 0)
                only_split(f"kv{l}")
                zp = LIN[f"z{l}"]
                z0 = zp.free0
                seqs = slice(0, 2) if full else slice(1, 2)

                def gated_linear_unit():
                    dve.memset(glu[:].rearrange("p j s n -> p (j s n)"), 0.0).then_inc(sem("dve_chain"), 1)
                    dve.wait_ge(sem("dve_chain"), chained())
                    dve.wait_ge(sem("sig"), 2 * (l + 1))
                    for j in range(2):
                        ins = dve.tensor_tensor(glu[:, j, seqs, 15:15 + CTX], segments(z[:, j, r]), segments(z[:, 2 + j, r]),
                                                ALU.mult)
                    ins.then_inc(sem("dve_chain"), 1)
                    dve.wait_ge(sem("dve_chain"), chained())

                def tap(k, j):
                    dst, src = segments(conv[:, j, r]), glu[:, j, seqs, k:k + CTX]
                    w = col(vec2, V2["conv_a_w_2"] + (31 * l + k) * 2 + j)
                    if k == 0:
                        ins = dve.tensor_scalar(dst, src, w, col(vec2, V2["conv_a_b_2"] + 2 * l + j), ALU.mult, ALU.add)
                    else:
                        dve.wait_ge(sem("tap"), 60 * l + 2 * k + j - 1)
                        ins = dve.scalar_tensor_tensor(out=dst, in0=src, scalar=w, in1=dst, op0=ALU.mult, op1=ALU.add)
                    ins.then_inc(sem("tap" if k < 30 else "conv_in"), 1)

                taps = [(k, j) for k in range(31) for j in range(2)]
                for g in range(len(zp.groups)):
                    split_to(zp.u0 + (g + 1) * zp.nch + LEAD)
                    if g == 3:
                        gated_linear_unit()
                    if g >= 3:
                        for k, j in taps[:CONV_TAPS]:
                            tap(k, j)
                        taps = taps[CONV_TAPS:]
                dve.wait_ge(sem("free_act"), z0 + 16)
                for i in range(4):
                    rotate(i, 4, 5 + 4 * l, z[:, 4 + i, LAT], drope)
                lam_init = 0.8 - 0.6 * math.exp(-0.3 * l)
                a = 56 + 4 * l
                dve.tensor_tensor(small[0:32, 48:50], small[0:32, a:a + 2], small[0:32, a + 2:a + 4], ALU.mult)\
                    .then_inc(sem("lam_prod"), 1)

                def y_slot():
                    if ny[0] - 3 > 0:
                        dve.wait_ge(sem("y_lo"), ny[0] - 3)
                    ny[0] += 1
                    return TMP[:, (ny[0] - 1) % 4, r]

                def y_lo(j, at):
                    dve.wait_ge(sem("y_hi"), at)
                    dve.tensor_tensor(h_lo[:, j, r], TMP[:, (at - 1) % 4, r], h_hi[:, j, r].bitcast(F32), ALU.subtract)\
                        .then_inc(sem("y_lo"), 1)

                for k, j in taps:
                    tap(k, j)
                dve.wait_ge(sem("roped"), 5 + 4 * (l + 1))
                for j in range(2):
                    out = y_slot()
                    dve.tensor_tensor(z[:, 16 + j, r], z[:, 16 + j, r], z[:, 18 + j, r], ALU.mult)\
                        .then_inc(sem("dve_chain"), 1)
                    dve.wait_ge(sem("dve_chain"), chained())
                    conv3(out, z[:, 16 + j, r], [col(vec2, V2["conv_d_w_2"] + (3 * l + k) * 2 + j) for k in range(3)])
                    dve.tensor_tensor(out, out, z[:, 14 + j, r], ALU.mult).then_inc(sem("y_made"), 1)
                for j in range(2):
                    y_lo(6 + j, 8 * l + 1 + j)
                dve.wait_ge(sem("lam_exp"), l + 1)
                dve.tensor_tensor(small[:, 52:53], small[:, 51:52], small[:, 50:51], ALU.subtract)\
                    .then_inc(sem("dve_chain"), 1)
                dve.wait_ge(sem("dve_chain"), chained())
                dve.tensor_scalar(small[:, 53:54], small[:, 52:53], -lam_init, None, ALU.add).then_inc(sem("lam"), 1)
                dve.tensor_scalar(small[:, 54:55], col(vec2, V2["subln_g_2"] + l), 1.0 - lam_init, None, ALU.mult)\
                    .then_inc(sem("dve_chain"), 1)
                dve.wait_ge(sem("dve_chain"), chained())
                mean(CTX, r)
                for j in range(2):
                    dve.tensor_tensor(z[:, 12 + j, r], z[:, 12 + j, r], MEAN[:, r], ALU.subtract).then_inc(sem("n2_xc"), 1)
                rstd(5, CTX, r, RSTD[:, r])
                for j in range(2):
                    dve.scalar_tensor_tensor(out=z[:, 12 + j, r], in0=z[:, 12 + j, r], scalar=col(vec2, V2["sg_ln_g_2"] + 2 * l + j),
                                             in1=RSTD[:, r], op0=ALU.mult, op1=ALU.mult).then_inc(sem("sv_n"), 1)
                for j in range(2):
                    dve.wait_ge(sem("sg_mm"), 2 * l + j + 1)
                    dve.wait_ge(sem("gelu_u"), 2 * l + j + 1)
                    out = y_slot()
                    nc_ = n // P
                    bias = sgb[:, j, :].rearrange("p (c q) -> p c q", c=1).broadcast_to([P, nc_, P])
                    dve.tensor_tensor(out.rearrange("p (c q) -> p c q", q=P), PS[:, 2 + j, r].rearrange("p (c q) -> p c q", q=P),
                                      bias, ALU.add).then_inc(sem("sg_used"), 1)
                    dve.wait_ge(sem("sg_used"), 2 * l + j + 1)
                    dve.tensor_tensor(out, out, z[:, 10 + j, r], ALU.mult).then_inc(sem("y_made"), 1)
                for j in range(2):
                    y_lo(4 + j, 8 * l + 3 + j)
                mean(CTX, r)
                for j in range(2):
                    dve.tensor_tensor(conv[:, j, r], conv[:, j, r], MEAN[:, r], ALU.subtract).then_inc(sem("n2_xc"), 1)
                rstd(5, CTX, r, RSTD[:, r])
                for j in range(2):
                    dve.tensor_tensor(conv[:, j, r], conv[:, j, r], RSTD[:, r], ALU.mult).then_inc(sem("conv_n"), 1)
                for j in range(2):
                    ny[0] += 1
                    y_lo(j, 8 * l + 5 + j)
                items = [(h, s) for h in range(4) for s in toks]
                base = natt[0]

                def probabilities(i):
                    h, s = items[i]
                    nk, c = (CTX if s < 2 else T), 8 + 8 * (i % 2)
                    dve.wait_ge(sem("att_e"), base + i + 1)
                    dve.reciprocal(small[:, c + 6:c + 8], small[:, c + 2:c + 4]).then_inc(sem("dve_chain"), 1)
                    dve.wait_ge(sem("dve_chain"), chained())
                    dve.tensor_tensor(small[:, c + 7:c + 8], small[:, c + 7:c + 8], small[:, 53:54], ALU.mult)\
                        .then_inc(sem("dve_chain"), 1)
                    dve.wait_ge(sem("dve_chain"), chained())
                    dve.tensor_scalar(scale_of(i, 0), ident[:], small[:, c + 6:c + 7], None, ALU.mult)
                    dve.tensor_scalar(scale_of(i, 1), ident[:], small[:, c + 7:c + 8], None, ALU.mult)\
                        .then_inc(sem("att_p"), 1)

                def out_tile(j):
                    dve.wait_ge(sem("att_o"), 8 + 4 * l + 2 * j + 2)
                    dve.tensor_copy(TMP[:, j, r], PS[:, 6, r]).then_inc(sem("ot"), 1)

                dve.wait_ge(sem("y_lo"), 8 * l + 6)
                for i, (h, s) in enumerate(items):
                    nk, c = (CTX if s < 2 else T), 8 + 8 * (i % 2)
                    dve.wait_ge(sem("att_s"), base + i + 1)
                    for j in range(2):
                        ins = dve.tensor_reduce(small[:, c + 4 + j:c + 5 + j], PS[:, 2 * (i % 2) + j, 0:nk], AX_X, ALU.max)
                    ins.then_inc(sem("dve_chain"), 1)
                    dve.wait_ge(sem("dve_chain"), chained())
                    dve.tensor_scalar(small[:, c:c + 2], small[:, c + 4:c + 6], -DIFF_SCALE, None, ALU.mult).then_inc(sem("att_nb"), 1)
                    probabilities(i)
                    if h == 2 and i == 2 * len(toks) + 1:
                        out_tile(0)
                out_tile(1)
                natt[0] += len(items)
                for j in range(2):
                    rstd(5, 64, r, RSTD[:, r])
                    out = y_slot()
                    dve.scalar_tensor_tensor(out=out, in0=TMP[:, j, r], scalar=small[:, 54:55], in1=RSTD[:, r],
                                             op0=ALU.mult, op1=ALU.mult).then_inc(sem("y_made"), 1)
                    dve.wait_ge(sem("y_made"), 6 * l + 5 + j)
                for j in range(2):
                    y_lo(2 + j, 8 * l + 7 + j)
                residual(f"wo{l}", full, l, 2)
                rms(5 + 2 * l, full, l, 3)
                mlp(f"g{l}", full, l)
            rstd(5, D, LAT, RSTD[:, LAT])
            for t in range(8):
                dve.scalar_tensor_tensor(out=X[:, t, LAT], in0=X[:, t, LAT], scalar=col(vec2, V2["final_g_2"] + t),
                                         in1=RSTD[:, LAT], op0=ALU.mult, op1=ALU.mult).then_inc(sem("final"), 1)



def tiles_of(a):
    return np.ascontiguousarray(a.T.reshape(-1, P, a.shape[0]).transpose(1, 0, 2))


def columns_of(arrays, spec):
    return np.ascontiguousarray(np.concatenate([arrays[name].reshape(-1, P) for name, _ in spec]).T)


def rope_tables(blocks, freqs):
    n = len(freqs)
    pos = np.arange(CTX)
    out = np.zeros((P, 2, CTX), np.float32)
    for p in range(P):
        j = p % (4 * n)
        at = (pos // 64 if j < 2 * n else pos % 64).astype(np.float32)
        angle = at * np.float32(freqs[j % n])
        out[p, 0], out[p, 1] = np.cos(angle), np.sin(angle)
    return out


def rotation(half):
    r = np.zeros((P, P), np.float32)
    for p in range(P):
        if p % (2 * half) < half:
            r[p + half, p] = -1.0
            r[p, p + half] = 1.0
    return r


def kernel(**inputs):
    import concourse.bacc as bacc
    from concourse.bass_utils import run_bass_kernel_spmd as run

    a = {k: np.asarray(v) for k, v in inputs.items()}
    weights = np.zeros((len(UNITS), P, UNIT), np.float32)
    widths = []
    for u, (ph, g, c, _, _) in enumerate(UNITS):
        src = a[ph.source[0]][ph.source[1]] if isinstance(ph.source, tuple) else a[ph.source][0]
        ks = ph.chunks[c]
        k0 = (ph.row0 + ks[0]) * P
        part = src[k0:k0 + len(ks) * P][:, ph.groups[g]].reshape(len(ks), P, -1).transpose(1, 0, 2)
        widths.append(part.shape[1] * part.shape[2])
        weights[u, :, :widths[-1]] = part.reshape(P, -1)
    ada = np.concatenate([a[n][l].reshape(ADA_KS, 2, P, ADA_LAYER, ADA_W).transpose(3, 0, 2, 1, 4)
                          for n in ("ada_w", "ada_w_2") for l in range(2)])
    ada0 = a["ada_w"][0][:, :ADA0 * ADA_W].reshape(8, P, 8, 2, P).transpose(2, 1, 3, 0, 4)
    sub = a["subln_g_2"]
    vecs = dict(a, subln_g_2=np.concatenate([sub, sub], axis=1))
    cond = np.stack([np.stack([a["c" + s].reshape(8, P), a["c_ctx" + s].reshape(8, P)]) for s in ("", "_2")])
    block_ones = np.zeros((P, P), np.float32)
    block_ones[0:64, 0:64] = block_ones[64:, 64:] = 1.0
    arrays = {
        "weights": weights,
        "ada": np.ascontiguousarray(ada[ADA0:].reshape(-1, P, 2 * ADA_W)),
        "ada0": np.ascontiguousarray(ada0.reshape(8, P, 2 * UNIT)),
        "cond": np.ascontiguousarray(cond.transpose(3, 0, 2, 1)),
        "ones": np.ones((P, P), np.float32),
        "ident": np.eye(P, dtype=np.float32),
        "vec1": columns_of(vecs, VEC1_SPEC),
        "vec2": columns_of(vecs, VEC2_SPEC),
        "bg": np.ascontiguousarray(a["m_b_gates"][0].reshape(2, 2, 4).transpose(2, 1, 0).reshape(4, 4)),
        "lam": np.ascontiguousarray(np.stack([a["lam_q1_2"], a["lam_q2_2"], a["lam_k1_2"], a["lam_k2_2"]], axis=1)
                                    .reshape(8, 32).T),
        "x0": tiles_of(np.concatenate([a["ctx"][0], a["x"][0]])),
        "ctx2": tiles_of(a["ctx_2"][0]),
        "gate_w": np.ascontiguousarray(a["m_w_gates"][0].transpose(1, 0, 2).reshape(16, P, 16).transpose(1, 0, 2)
                                       .reshape(P, 256)),
        "arope": rope_tables(2, np.float32(10000.0) ** (-np.arange(16, dtype=np.float32) / 16)),
        "arot": rotation(16),
        "drope": rope_tables(4, np.float32(10000.0) ** (-np.arange(0, 16, 2, dtype=np.float32) / 16)),
        "drot": np.ascontiguousarray(np.stack([rotation(8), block_ones], axis=1)),
        "sgw": np.ascontiguousarray(a["sg_w_2"].transpose(0, 3, 1, 2)),
        "sgb": a["sg_b_2"],
    }
    nc = bacc.Bacc("TRN2", target_bir_lowering=False, num_devices=1)
    A = {"units_width": widths}
    in_map = {}
    for name, array in arrays.items():
        in_map[f"in_{name}"] = array
        A[name] = nc.dram_tensor(f"in_{name}", array.shape, F32, kind="ExternalInput").ap()
    A["og_spill"] = nc.dram_tensor("og_spill", (P, 16, T), F32, kind="Internal").ap()
    A["out"] = nc.dram_tensor("out_0", (P, 8, CTX), F32, kind="ExternalOutput").ap()
    two_stacks(nc, A)
    out = run(nc, [in_map], core_ids=[0]).results[0]["out_0"]
    return np.ascontiguousarray(out.transpose(2, 1, 0).reshape(1, CTX, D))
```

```python
import math
from contextlib import ExitStack

import numpy as np

import concourse.bass as bass
from concourse import mybir

F32 = mybir.dt.float32
F32R = mybir.dt.float32r
ALU = mybir.AluOpType
ACT = mybir.ActivationFunctionType
AX_X = mybir.AxisListType.X

P = 128
D = 1024
CTX = 256
T = 512
LAT = slice(CTX, T)
EPS = 1e-6
ALPHA = 4 ** 0.25
NH = 4
FFN_T = 22
RING = 4
BANKS = 4
UNIT = 1024
LEAD = 2
CONV_TAPS = 11
ADA_W = 256
ADA_KS = 4
ADA_LAYER = 6 * D // ADA_W
ADA0 = 2 * D // ADA_W
ADA_RING = 3
MLA_SCALE = 192 ** -0.5
DIFF_SCALE = 32 ** -0.5
ADA_PACE = {"og": (2, 1), "up": (0, 1), "v": (2, 1), "qk": (2, 1), "mo": (2, 1), "f1": (0, 1), "z0": (0, 1), "z1": (0, 1)}



def halves(full):
    return [(slice(0, CTX), 1), (LAT, 0)] if full else [(LAT, 0)]


def rng(full):
    return slice(0, T) if full else LAT



def span(*starts, width=P):
    return np.concatenate([np.arange(s, s + width) for s in starts])


class Linear:

    def __init__(self, name, source, k_tiles, groups, full=True, token_major=False, freed_by="act", row0=0,
                 kc=None):
        self.name, self.source, self.k_tiles, self.groups = name, source, k_tiles, groups
        self.full, self.token_major, self.freed_by, self.row0 = full, token_major, freed_by, row0
        self.width = len(groups[0])
        self.kc = kc or UNIT // self.width
        self.chunks = [list(range(k, min(k + self.kc, k_tiles))) for k in range(0, k_tiles, self.kc)]
        self.nch = len(self.chunks)
        self.tpg = 4 if token_major else self.width // P
        self.n_tiles = self.tpg * len(groups)


Z_PARTS = (0, 1, 6, 2, 5, 7, 8, 9)


def plan():
    g256 = lambda n, at=0: [span(at + i * 256, width=256) for i in range(n)]
    out = []
    out += [Linear("og", "m_w_og", 8, g256(8)),
            Linear("up", "m_w_up", 8, g256(8), freed_by="dve"),
            Linear("v", "m_w_v", 16, [span(i * 512, width=512) for i in range(4)], token_major=True, kc=2),
            Linear("qk", "m_w_qk", 16, g256(8)),
            Linear("mout", "m_w_out", 16, g256(4), freed_by="dve")]

    def ffn(tag, layer, full):
        for half in range(2):
            fs = range(11 * half, 11 * half + 11)
            out.append(Linear(f"{tag}in{half}", ("ffn_w_in", layer), 8,
                              [np.concatenate([span(f * P), span(FFN_T * P + f * P)]) for f in fs],
                              full=full, freed_by="dve"))
            out.append(Linear(f"{tag}out{half}", ("ffn_w_out", layer), 11, g256(4), full=full, freed_by="dve",
                              row0=11 * half))

    ffn("f0", 0, True)
    out += [Linear("dkv", "a_w_dkv", 8, [span(0, width=256)]),
            Linear("dkr", "a_w_dkv", 8, [np.concatenate([span(256, width=64)] * 2)]),
            Linear("dq", "a_w_dq", 8, [span(i * P) for i in range(3)], full=False),
            Linear("ukn", "a_w_ukv", 2, [span(*[256 * h for h in range(4 * i, 4 * i + 4)]) for i in range(2)]),
            Linear("ukv", "a_w_ukv", 2, [span(*[256 * h + 128 for h in range(4 * i, 4 * i + 4)]) for i in range(2)],
                   token_major=True),
            Linear("uqn", "a_w_uq", 3, [span(384 * i, 384 * i + 192) for i in range(4)], full=False),
            Linear("uqr", "a_w_uq", 3, [np.concatenate([span(192 * h + 128, width=64) for h in range(4 * i, 4 * i + 4)])
                                        for i in range(2)], full=False),
            Linear("aout", "a_w_out", 8, g256(4), full=False, freed_by="dve")]
    ffn("f1", 1, False)
    for l in range(2):
        full = l == 0
        out.append(Linear(f"kv{l}", ("w_in_2", l), 8, g256(2, at=768)))
        out.append(Linear(f"z{l}", ("w_in_2", l), 8, [span(256 * part, width=256) for part in Z_PARTS], full=full))
        out.append(Linear(f"wo{l}", ("w_out_2", l), 8, g256(4), full=full, freed_by="dve"))
        for half in range(2):
            out.append(Linear(f"g{l}in{half}", ("mlp_w1_2", l), 8, g256(8, at=2048 * half), full=full))
            out.append(Linear(f"g{l}out{half}", ("mlp_w2_2", l), 16, g256(4), full=full, freed_by="dve",
                              row0=16 * half))
    units, tiles, used, done = [], [], 0, 0
    free = {"act": 0, "dve": 0}
    for ph in out:
        ph.u0, ph.t0 = len(units), len(tiles)
        ph.free0 = free[ph.freed_by]
        for g in range(len(ph.groups)):
            for c in range(ph.nch):
                if c < ph.nch - 1:
                    used += 1
                    units.append((ph, g, c, "unit_used", used))
                else:
                    units.append((ph, g, c, "tile_done", done + ph.tpg))
            done += ph.tpg
            for m in range(ph.tpg):
                free[ph.freed_by] += 1
                tiles.append((ph.freed_by, free[ph.freed_by]))
    macs, sums = [], {}
    todo = [(a, k) for a in range(ADA0, 4 * ADA_LAYER) for k in range(ADA_KS)]
    for u, (ph, g, c, _, _) in enumerate(units):
        count, every = ADA_PACE.get(ph.name[:2], (1, 1))
        for _ in range(0 if (u - ph.u0) % every else min(count, len(todo))):
            a, k = todo.pop(0)
            macs.append((u, a, k))
            if k == ADA_KS - 1:
                sums.setdefault(u + 1, []).append(a)
    assert not todo, len(todo)
    return {ph.name: ph for ph in out}, units, tiles, macs, sums


LIN, UNITS, TILES, ADA_MACS, ADA_SUMS = plan()
hid0 = {"f0": 0, "f1": 22, "g0": 44, "g1": 76}


def ada_conds(a):
    layer, c = divmod(a, ADA_LAYER)
    return 1 if layer % 2 and c >= ADA0 else 2


def ada_steps(n):
    return 2 * sum(ada_conds(a) for _, a, _ in ADA_MACS[:n])


def summed_before(name):
    return ADA0 + sum(len(slices) for u, slices in ADA_SUMS.items() if u < LIN[name].u0)


MOD_READ = {ADA0: 1, summed_before("mout"): 2, summed_before("dkv"): 4, summed_before("kv0"): 5}
assert ADA_LAYER <= summed_before("mout") <= 2 * ADA_LAYER and 2 * ADA_LAYER <= summed_before("dkv") <= 3 * ADA_LAYER
assert 3 * ADA_LAYER <= summed_before("kv0") and summed_before("kv1") == 4 * ADA_LAYER
nsq_after = list(np.cumsum([4] * 4 + [8, 8, 2, 3, 8, 8] + [8, 2, 2, 1, 1, 8] * 2 + [8]).tolist())


def columns(spec):
    at, out = 0, {}
    for name, n in spec:
        out[name] = at
        at += n
    return out, at


VEC1_SPEC = [("ada_b", 96), ("ln_g", 32), ("ln_b", 32), ("ffn_conv_w", 132), ("ffn_conv_b", 44), ("m_conv_w", 48),
             ("m_conv_b", 16), ("m_norm_g", 16), ("a_q_norm", 3), ("a_kv_norm", 2)]
VEC2_SPEC = [("ada_b_2", 96), ("norm1_g_2", 16), ("norm2_g_2", 16), ("conv_a_w_2", 124), ("conv_a_b_2", 4),
             ("ln_a_g_2", 4), ("ln_a_b_2", 4), ("sg_ln_g_2", 4), ("sg_ln_b_2", 4), ("conv_d_w_2", 12),
             ("subln_g_2", 2), ("final_g_2", 8)]
V1, NV1 = columns(VEC1_SPEC)
V2, NV2 = columns(VEC2_SPEC)


def w_span(s):
    return (s * T, s * T + T) if s < 2 else (2 * T + (s - 2) * CTX, 2 * T + (s - 1) * CTX)


def q_span(s):
    return slice(0, T) if s < 2 else LAT



def two_stacks(nc, A):
    with ExitStack() as ctx:
        def sb(name, shape, dt=F32, stack=ctx):
            return stack.enter_context(nc.sbuf_tensor(name, shape, dt))

        sems = {}

        def sem(name):
            if name not in sems:
                sems[name] = ctx.enter_context(nc.semaphore(name))
            return sems[name]


        raw = sb("raw", [P, RING, UNIT])
        w_hi = sb("w_hi", [P, RING, UNIT], F32R)
        w_lo = sb("w_lo", [P, RING, UNIT], F32R)
        ada_ring = sb("ada_ring", [P, ADA_RING, 2 * ADA_W])
        ada_acc = sb("ada_acc", [P, 2, 2, ADA_W])
        ones = sb("ones", [P, P])
        ident = sb("ident", [P, P])
        vec1 = sb("vec1", [P, NV1])
        cond = sb("cond", [P, 2, 8, 2])
        mod = sb("mod", [P, 2, 48, 2])
        small = sb("small", [P, 64])
        gcol = small[:, 8:40].rearrange("p (d s h) -> p d s h", d=2, s=4)
        with ExitStack() as st:
            h0_hi = sb("h0_hi", [P, 8, T], F32R, st)
            h0_lo = sb("h0_lo", [P, 8, T], F32R, st)
        xv = sb("xv", [P, 16 * T])
        X = xv[:, 0:8 * T].rearrange("p (t n) -> p t n", n=T)
        TMP = xv[:, 8 * T:16 * T].rearrange("p (t n) -> p t n", n=T)
        V = xv[:, :].rearrange("p (s e) -> p s e", e=4 * T)
        MEAN, RSTD = TMP[:, 6], TMP[:, 7]

        with ExitStack() as st:
            m_hi = sb("m_hi", [P, 16, T], F32R, st)
            qk = sb("qk", [P, 16, T], F32, st)
            wgt = sb("wgt", [P, 8 * T], F32, st)
            rows = sb("rows", [P, T], F32, st)
            with ExitStack() as inner:
                m_lo = sb("m_lo", [P, 16, T], F32R, inner)
            with ExitStack() as inner:
                og = sb("og", [P, 16, T], F32, inner)
        first_acc = og[:].rearrange("p t n -> p (t n)")
        MT = wgt[:, :].rearrange("p (t n) -> p t n", n=T)
        WD = wgt[:, 0:3072].rearrange("p (d n) -> p d n", d=2)
        RD = wgt[:, 3072:4096].rearrange("p (d n) -> p d n", d=2)
        with ExitStack() as st:
            sb("below", [P, 32 * T], F32, st)
            gates = sb("gates", [4, 6, T], F32, st)
            with ExitStack() as inner:
                gate_w = sb("gate_w", [P, 256], F32, inner)
                gate_hi = sb("gate_hi", [P, 256], F32R, inner)
                gate_lo = sb("gate_lo", [P, 256], F32R, inner)
            with ExitStack() as inner:
                gate_all = sb("gate_all", [16, T], F32, inner)

        with ExitStack() as st:
            vec2 = sb("vec2", [P, NV2], F32, st)
            h_hi = sb("h_hi", [P, 8, T], F32R, st)
            h_lo = sb("h_lo", [P, 8, T], F32R, st)
            with ExitStack() as inner:
                hid_hi = sb("hid_hi", [P, 16, T], F32R, inner)
                hid_lo = sb("hid_lo", [P, 16, T], F32R, inner)
            with ExitStack() as inner:
                ckv = sb("ckv", [P, 2, T], F32, inner)
                ckv_hi = sb("ckv_hi", [P, 2, T], F32R, inner)
                ckv_lo = sb("ckv_lo", [P, 2, T], F32R, inner)
                cq = sb("cq", [P, 3, CTX], F32, inner)
                cq_hi = sb("cq_hi", [P, 3, CTX], F32R, inner)
                cq_lo = sb("cq_lo", [P, 3, CTX], F32R, inner)
                qn = sb("qn", [P, 8, CTX], F32, inner)
                qr = sb("qr", [P, 4, CTX], F32, inner)
                kn = sb("kn", [P, 8, T], F32, inner)
                kr = sb("kr", [P, T], F32, inner)
                vm = sb("vm", [P, 4, D], F32, inner)
                arope = sb("arope", [P, 2, CTX], F32, inner)
                arot = sb("arot", [P, P], F32, inner)
            with ExitStack() as inner:
                z = sb("z", [P, 20, T], F32, inner)
                glu = sb("glu", [P, 2, 2, CTX + 30], F32, inner)
                conv = sb("conv", [P, 2, T], F32, inner)
                vtok = sb("vtok", [P, 4, CTX], F32, inner)
                stok = sb("stok", [P, 4, CTX], F32, inner)
                sgw = sb("sgw", [P, 4, P], F32, inner)
                sgb = sb("sgb", [P, 2, P], F32, inner)
                probs = sb("probs", [P, 2, 2, T], F32, inner)
                probs_t = sb("probs_t", [P, 4, T], F32, inner)
                drope = sb("drope", [P, 2, CTX], F32, inner)
                drot = sb("drot", [P, 2, P], F32, inner)
        PS = ctx.enter_context(nc.psum_tensor("PS", [P, 8, T], F32))

        block = ctx.enter_context(nc.Block())

        def w_slot(u):
            return u % RING

        def SQ(n):
            return wgt[:, 3 * T + (n % 2) * T:4 * T + (n % 2) * T] if n < 16 else TMP[:, 4 + n % 2]

        def scale_of(i, j):
            return TMP[:, 4 + i % 2, j * P:(j + 1) * P]

        @block.sync
        def _(sp):
            for name, tile in (("cond", cond[:]), ("ones", ones[:]), ("ident", ident[:]), ("vec1", vec1[:]),
                               ("bg", small[0:4, 0:4]), ("lam", small[0:32, 56:64])):
                sp.dma_start(tile, A[name]).then_inc(sem("consts_in"), 16)
            for i in (0, 4, 1, 5, 2, 6, 3, 7):
                dst = (xv[:] if i < 4 else qk[:].rearrange("p t n -> p (t n)"))[:, (i % 4) * 2 * UNIT:(i % 4 + 1) * 2 * UNIT]
                sp.dma_start(dst, A["ada0"][i]).then_inc(sem(f"ada0_in{i}"), 16)
            sp.dma_start(MT[:, :, :], A["x0"]).then_inc(sem("x0_in"), 16)
            ada_out = 0
            for u in range(len(UNITS)):
                if u >= RING:
                    sp.wait_ge(sem("w_split"), u - RING + 1)
                n = A["units_width"][u]
                sp.dma_start(raw[:, w_slot(u), 0:n], A["weights"][u, :, 0:n]).then_inc(sem(f"raw_in{w_slot(u)}"), 16)
                while ada_out < len(ADA_MACS) and (ada_out < ADA_RING or ADA_MACS[ada_out - ADA_RING][0] + RING <= u):
                    if ada_out >= ADA_RING:
                        sp.wait_ge(sem("ada_mac"), ada_steps(ada_out - ADA_RING + 1))
                    slot = ada_out % ADA_RING
                    sp.dma_start(ada_ring[:, slot, :], A["ada"][ada_out]).then_inc(sem(f"ada_in{slot}"), 16)
                    ada_out += 1
            sp.wait_ge(sem("out_done"), 16)

        @block.gpsimd
        def _(pool):
            def modulated(n, first, full, par, chunk):
                for t in range(8):
                    pool.wait_ge(sem("xb"), first + t + 1)
                    if t >= 4:
                        pool.wait_ge(sem("h_lo"), 8 * n + t - 3)
                    for c, v in halves(full):
                        ins = pool.tensor_scalar(TMP[:, t % 4, c], X[:, t, c],
                                                 mod[:, par, 8 * (chunk + 1) + t, v:v + 1], mod[:, par, 8 * chunk + t, v:v + 1],
                                                 ALU.mult, ALU.add)
                    ins.then_inc(sem("h_made"), 1)

            for i in range(4):
                pool.wait_ge(sem("free_act"), LIN["og"].free0 + 4 * (i + 1))
                pool.dma_start(A["og_spill"][:, 4 * i:4 * i + 4, :], qk[:, 4 * i:4 * i + 4, :]).then_inc(sem("og_out"), 16)
            pool.wait_ge(sem("up_c"), 16)
            pool.dma_start(gate_w[:], A["gate_w"]).then_inc(sem("gate_w_in"), 16)
            pool.wait_ge(sem("og_out"), 64)
            pool.wait_ge(sem("tile_done"), LIN["mout"].t0)
            pool.dma_start(og[:, :, :], A["og_spill"]).then_inc(sem("og_in"), 16)
            for h in range(NH):
                for d in range(2):
                    for s in range(4):
                        i = 8 * h + 4 * d + s
                        pool.wait_ge(sem("wraw"), i + 1)
                        lo, hi = w_span(s)
                        if d == 0:
                            ap = WD[:, 0, lo:hi]
                            base, step, cm = (0 if s < 2 else CTX) - s * P, 1, -1
                        else:
                            ap = WD[:, 1, lo:lo + CTX]
                            base, step, cm = s * P - (0 if s < 2 else CTX), -1, 1
                        pool.affine_select(out=ap, in_=ap, compare_op=ALU.is_ge, fill=0.0, base=base,
                                           pattern=[[step, ap.shape[-1]]], channel_multiplier=cm)\
                            .then_inc(sem("wsel"), 1)
            pool.wait_ge(sem("pv"), 4 * NH)
            pool.dma_start(X[:, :, :], A["x0"]).then_inc(sem("x_in"), 16)
            modulated(1, 0, True, 0, 3)
            modulated(2, 8, True, 1, 0)
            pool.wait_ge(sem("tile_done"), LIN["dkv"].t0)
            pool.dma_start(vec2[:], A["vec2"]).then_inc(sem("vec2_in"), 16)
            pool.dma_start(arope[:], A["arope"]).then_inc(sem("arope_in"), 16)
            pool.dma_start(arot[:], A["arot"]).then_inc(sem("arope_in"), 16)
            pool.wait_ge(sem("h_lo"), 8 * 3)
            pool.dma_start(X[:, :, 0:CTX], A["ctx2"]).then_inc(sem("ctx2_in"), 16)
            modulated(3, 16, False, 1, 3)
            for l in range(2):
                pool.wait_ge(sem("tile_done"), LIN[f"kv{l}"].t0)
                for name, dst, src in (("drope", drope, A["drope"]), ("drot", drot, A["drot"]), ("sgw", sgw, A["sgw"][l])):
                    pool.dma_start(dst[:], src).then_inc(sem("mix_in"), 16)
                for g in range(4):
                    pool.dma_start(sgb[64 * (g % 2):64 * (g % 2) + 64, g // 2, :],
                                   A["sgb"][l, g:g + 1, :].broadcast_to([64, P])).then_inc(sem("mix_in"), 16)
            pool.wait_ge(sem("final"), 8)
            pool.dma_start(A["out"], X[:, :, LAT]).then_inc(sem("out_done"), 16)

        @block.tensor
        def _(pe):
            nsq, ncall, nacc = [0], [0], [0]

            def first_modulation():
                for m in range(8):
                    pe.wait_ge(sem(f"ada0_in{m // 2}"), 16)
                    for k in range(8):
                        at = m * UNIT + k * P
                        mm = pe.matmul(PS[:, 7, 2 * m:2 * m + 2], xv[:, at:at + P], cond[:, 0, k, :],
                                       start=(k == 0), stop=(k == 7))
                    if m % 2:
                        mm.then_inc(sem("ada_sum"), 1)
                pe.wait_ge(sem("first_scale"), 16)
                for m in range(8, 16):
                    for v in range(2):
                        at = v * UNIT + (m - 8) * P
                        mm = pe.matmul(PS[:, 7, 2 * m + v:2 * m + v + 1], first_acc[:, at:at + P], ones[:, 0:1],
                                       start=True, stop=True)
                    if m % 2:
                        mm.then_inc(sem("ada_sum"), 1)

            def sum_modulation(a):
                if a in MOD_READ:
                    pe.wait_ge(sem("mod_read"), MOD_READ[a])
                layer, c = divmod(a, ADA_LAYER)
                pe.wait_ge(sem("ada_mac"), ada_steps((a - ADA0 + 1) * ADA_KS))
                for v in range(ada_conds(a)):
                    for m in range(2):
                        col = (layer % 2) * 96 + 2 * (2 * c + m) + v
                        mm = pe.matmul(PS[:, 7, col:col + 1], ada_acc[:, a % 2, v, m * P:(m + 1) * P], ones[:, 0:1],
                                       start=True, stop=True)
                mm.then_inc(sem("ada_sum"), 1)

            def linear(name, hi, lo, ready=(), each=None, behind=None):
                ph = LIN[name]
                for what, value in ready:
                    pe.wait_ge(sem(what), value)
                r = rng(ph.full)
                for g in range(len(ph.groups)):
                    for c, ks in enumerate(ph.chunks):
                        u = ph.u0 + g * ph.nch + c
                        s = w_slot(u)
                        pe.wait_ge(sem("w_split"), u + 1)
                        for m in range(ph.tpg):
                            t = ph.t0 + g * ph.tpg + m
                            if c == 0 and t >= BANKS:
                                freed, n = TILES[t - BANKS]
                                pe.wait_ge(sem(f"free_{freed}"), n)
                            for kk, k in enumerate(ks):
                                if each and g == 0 and m == 0:
                                    pe.wait_ge(sem(each[0]), each[1] + k + 1)
                                if ph.token_major:
                                    at = slice(kk * ph.width, (kk + 1) * ph.width)
                                    pairs = [(hi(k)[:, m * P:(m + 1) * P], w_hi[:, s, at]),
                                             (hi(k)[:, m * P:(m + 1) * P], w_lo[:, s, at]),
                                             (lo(k)[:, m * P:(m + 1) * P], w_hi[:, s, at])]
                                    out = PS[:, t % BANKS, 0:ph.width]
                                else:
                                    at = slice(kk * ph.width + m * P, kk * ph.width + (m + 1) * P)
                                    pairs = [(w_hi[:, s, at], hi(k)), (w_hi[:, s, at], lo(k)), (w_lo[:, s, at], hi(k))]
                                    out = PS[:, t % BANKS, r]
                                for i, (a, b) in enumerate(pairs):
                                    mm = pe.matmul(out, a, b, start=(k == 0 and i == 0),
                                                   stop=(k == ph.k_tiles - 1 and i == 2))
                            if c == ph.nch - 1:
                                mm.then_inc(sem("tile_done"), 1)
                            elif m == ph.tpg - 1:
                                mm.then_inc(sem("unit_used"), 1)
                        for a in ADA_SUMS.get(u, ()):
                            sum_modulation(a)
                    if behind:
                        behind(g)

            def sum_squares(n, bank, cols, lhs, width):
                for i in range(n):
                    if i == 0:
                        if ncall[0] > 0:
                            pe.wait_ge(sem("var"), ncall[0])
                        ncall[0] += 1
                    nsq[0] += 1
                    pe.wait_ge(sem("sq_made"), nsq[0])
                    pe.matmul(PS[:, bank, cols], lhs, SQ(nsq[0] - 1)[:, 0:width], start=(i == 0), stop=(i == n - 1))\
                        .then_inc(sem("sq_used"), 1)

            def residual_product(name, hi, lo, full, mean, **more):
                r = rng(full)
                linear(name, hi, lo, **more)
                if mean:
                    nacc[0] += 7
                    pe.wait_ge(sem("tiles_added"), nacc[0])
                    pe.matmul(PS[:, 4, r], ones[:], MEAN[:, r], start=True, stop=True).then_inc(sem("xsum"), 1)
                    sum_squares(8, 5, r, ones[:], T if full else CTX)
                else:
                    pe.wait_ge(sem("var"), ncall[0])
                    ncall[0] += 1
                    nsq[0] += 8
                    pe.wait_ge(sem("sq_used"), nsq[0])
                    pe.matmul(PS[:, 5, r], ones[:], RSTD[:, r], start=True, stop=True).then_inc(sem("xsum"), 1)

            pe.wait_ge(sem("cond"), 1)
            first_modulation()
            h0 = (lambda k: h0_hi[:, k, :], lambda k: h0_lo[:, k, :])
            mx = (lambda k: m_hi[:, k, :], lambda k: m_lo[:, k, :])
            hx = lambda full: (lambda k: h_hi[:, k, rng(full)], lambda k: h_lo[:, k, rng(full)])
            hid = lambda full: (lambda k: hid_hi[:, k, rng(full)], lambda k: hid_lo[:, k, rng(full)])
            linear("og", *h0, each=("h_lo", 0))
            linear("up", *h0)
            linear("v", *mx, each=("up_lo", 0))
            pe.wait_ge(sem("gate_wlo"), 1)
            for k in range(16):
                pe.wait_ge(sem("xc_lo"), k + 1)
                w = slice(k * 16, (k + 1) * 16)
                for i, (a, b) in enumerate(((gate_hi, m_hi), (gate_hi, m_lo), (gate_lo, m_hi))):
                    mm = pe.matmul(PS[0:16, 4, :], a[:, w], b[:, k, :], start=(k == 0 and i == 0), stop=(k == 15 and i == 2))
            mm.then_inc(sem("gate_mm"), 1)
            pe.wait_ge(sem("gate_all"), 1)
            pe.wait_ge(sem("free_act"), LIN["v"].free0 + 16)
            for q in range(4):
                at = 8 * (q % 2) + 4 * (q // 2)
                pe.matmul(PS[0:4, (4, 5, 6, 3)[q], :], ident[0:16, at:at + 4], gate_all[:], start=True, stop=True)\
                    .then_inc(sem("gate_rows"), 1)
            linear("qk", *mx, ready=[("gate_pre", 4)])
            pe.wait_ge(sem("gate_g"), 1)
            for d in range(2):
                for s in range(4):
                    mm = pe.transpose(PS[:, 4, d * 16 + s * 4:d * 16 + s * 4 + 4], gates[:, d, s * P:(s + 1) * P],
                                      ident[0:4, 0:4])
            mm.then_inc(sem("gcol_t"), 1)
            pe.wait_ge(sem("rows"), 4)
            pe.wait_ge(sem("gcol"), 1)
            pe.wait_ge(sem("free_act"), LIN["qk"].free0 + 16)
            for h in range(NH):
                if h > 0:
                    pe.wait_ge(sem("pv_used"), 4 * h)
                    pe.wait_ge(sem("var"), ncall[0])
                for i in range(4):
                    b = 32 * i
                    pe.matmul(PS[:, 3 + i, :], ident[b:b + 4, b + h:b + h + 1].broadcast_to([4, P]), rows[b:b + 4, :],
                              start=True, stop=True).then_inc(sem("bcast"), 1)
                for s in range(4):
                    out = PS[:, s, :] if s < 2 else PS[:, 2, (s - 2) * CTX:(s - 1) * CTX]
                    for kk in range(2):
                        mm = pe.matmul(out, qk[:, 8 + 2 * h + kk, s * P:(s + 1) * P], qk[:, 2 * h + kk, q_span(s)],
                                       start=(kk == 0), stop=(kk == 1))
                    mm.then_inc(sem("scores"), 1)
                for d in range(2):
                    pe.wait_ge(sem("expw"), 8 * h + 4 * d + 4)
                    for s in range(4):
                        pe.wait_ge(sem("wsel"), 8 * h + 4 * d + s + 1)
                        lo, hi = w_span(s)
                        mm = pe.matmul(PS[:, 3 + d, q_span(s)], ones[:], WD[:, d, lo:hi], start=(s == 0), stop=(s == 3))
                    mm.then_inc(sem("den"), 1)
                for e in range(4):
                    for s in range(4):
                        if e == 0:
                            pe.wait_ge(sem("wsum"), 4 * h + s + 1)
                        if e == 3 and s == 0:
                            pe.wait_ge(sem("wsum"), 4 * (h + 1))
                        lo, hi = w_span(s)
                        at = h * T + e * P
                        mm = pe.matmul(PS[:, (0, 1, 2, 5)[e], q_span(s)], V[:, s, at:at + P], WD[:, 0, lo:hi],
                                       start=(s == 0), stop=(s == 3))
                    mm.then_inc(sem("pv"), 1)
                sum_squares(4, 6, slice(0, T), ones[:], T)
            residual_product("mout", *mx, True, True, each=("hs_lo", 0))

            def feed_forward(tag, full, n_h):
                mean, n = tag[0] == "f", 11 if tag[0] == "f" else 16
                linear(f"{tag}in0", *hx(full), each=("h_lo", 8 * n_h))
                linear(f"{tag}out0", *hid(full), each=("hid_lo", hid0[tag]))
                linear(f"{tag}in1", *hx(full))
                residual_product(f"{tag}out1", *hid(full), full, mean, each=("hid_lo", hid0[tag] + n))

            feed_forward("f0", True, 1)
            hl = (lambda k: h_hi[:, k, LAT], lambda k: h_lo[:, k, LAT])
            linear("dkv", *hx(True), each=("h_lo", 16))
            linear("dkr", *hx(True))
            sum_squares(2, 5, slice(0, T), ones[:], T)
            linear("dq", *hl)
            ckv_x = (lambda k: ckv_hi[:, k, :], lambda k: ckv_lo[:, k, :])
            sum_squares(3, 5, slice(0, CTX), ones[:], CTX)
            linear("ukn", *ckv_x, ready=[("c_lo", 2)])
            linear("ukv", *ckv_x)
            linear("uqn", lambda k: cq_hi[:, k, :], lambda k: cq_lo[:, k, :], ready=[("c_lo", 5)])
            linear("uqr", lambda k: cq_hi[:, k, :], lambda k: cq_lo[:, k, :])
            pe.wait_ge(sem("free_act"), LIN["uqr"].free0 + LIN["uqr"].n_tiles)
            pe.wait_ge(sem("arope_in"), 32)
            for i in range(5):
                src = kr[:, LAT] if i == 4 else qr[:, i, :]
                pe.matmul(PS[:, 4 + i // 2, (i % 2) * CTX:(i % 2 + 1) * CTX], arot[:], src, start=True, stop=True)\
                    .then_inc(sem("rot"), 1)
            pe.wait_ge(sem("roped"), 5)

            def mla_scores(i):
                h, tt = divmod(i, 2)
                if i - 1 > 0:
                    pe.wait_ge(sem("att_e"), i - 1)
                b = 64 * (h % 2)
                pe.matmul(PS[:, i % 2, :], qn[:, h, tt * P:(tt + 1) * P], kn[:, h, :], start=True, stop=False)
                pe.matmul(PS[:, i % 2, :], qr[b:b + 64, h // 2, tt * P:(tt + 1) * P], kr[b:b + 64, :],
                          start=False, stop=True).then_inc(sem("att_s"), 1)

            def mla_values(h):
                pe.wait_ge(sem("att_pt"), 2 * h + 2)
                if h > 1:
                    pe.wait_ge(sem("o_lo"), h - 1)
                for s in range(4):
                    mm = pe.matmul(PS[:, 2 + h % 2, 0:CTX], vm[:, s, h * P:(h + 1) * P],
                                   TMP[:, 2 + s // 2, (s % 2) * CTX:(s % 2 + 1) * CTX], start=(s == 0), stop=(s == 3))
                mm.then_inc(sem("att_o"), 1)

            mla_scores(0)
            for i in range(16):
                if i < 15:
                    mla_scores(i + 1)
                pe.wait_ge(sem("att_p"), i + 1)
                if i - 1 > 0:
                    pe.wait_ge(sem("att_pt"), i - 1)
                for s in range(4):
                    mm = pe.matmul(PS[:, 4 + i % 2, s * P:(s + 1) * P], TMP[:, i % 2, s * P:(s + 1) * P], scale_of(i, 0),
                                   start=True, stop=True)
                mm.then_inc(sem("att_t"), 1)
                if i and i % 2 == 0:
                    mla_values(i // 2 - 1)
            mla_values(7)
            residual_product("aout", *hl, False, True, ready=[("o_lo", 8)])
            feed_forward("f1", False, 3)
            item = [16]
            for l in range(2):
                full = l == 0
                if l == 0:
                    sum_squares(8, 5, slice(0, T), ones[:], T)
                linear(f"kv{l}", *hx(True), each=("h_lo", 8 * (4 + 2 * l)))
                r, n = rng(full), (T if full else CTX)
                z0 = LIN[f"z{l}"].free0
                toks = range(4) if full else range(2, 4)

                def sum_two(first, what):
                    for j in range(2):
                        pe.wait_ge(sem(what), 2 * l + j + 1)
                        mm = pe.matmul(PS[:, 4, r], ones[:], first(j), start=(j == 0), stop=(j == 1))
                    mm.then_inc(sem("xsum"), 1)

                def spatial_gate(g):
                    if g == 3:
                        sum_two(lambda j: z[:, 12 + j, r], "sv_in")
                        pe.wait_ge(sem("lam_prod"), l + 1)
                        pe.matmul(PS[:, 6, 0:2], ones[0:32, :], small[0:32, 48:50], start=True, stop=True)\
                            .then_inc(sem("lam_mm"), 1)
                    if g == 5:
                        sum_squares(2, 5, r, ones[:], n)
                    if g == 6:
                        pe.wait_ge(sem("sv_done"), 2 * (l + 1))
                        pe.wait_ge(sem("lam_exp"), l + 1)
                        for s in toks:
                            for j in range(2):
                                at = (s % 2) * CTX + j * P
                                mm = pe.transpose(PS[:, (6, 4)[s // 2], at:at + P], z[:, 12 + j, s * P:(s + 1) * P], ident[:])
                        mm.then_inc(sem("st_t"), 1)
                    if g == 7:
                        pe.wait_ge(sem("mix_in"), 112 * (l + 1))
                        pe.wait_ge(sem("stok"), l + 1)
                        for j in range(2):
                            for s in toks:
                                for gi in range(2):
                                    c = 2 * j + gi
                                    mm = pe.matmul(PS[64 * gi:64 * gi + 64, 5 + j, s * P:(s + 1) * P],
                                                   stok[:, s, c * 64:(c + 1) * 64], sgw[:, c, :], start=True, stop=True)
                            mm.then_inc(sem("sg_mm"), 1)

                linear(f"z{l}", *hx(full), behind=spatial_gate)
                pe.wait_ge(sem("free_act"), z0 + 16)
                for i in range(4):
                    pe.matmul(PS[:, i // 2, (i % 2) * CTX:(i % 2 + 1) * CTX], drot[:, 0, :], z[:, 4 + i, LAT],
                              start=True, stop=True).then_inc(sem("rot"), 1)
                for s in range(4):
                    for j in range(2):
                        mm = pe.transpose(PS[:, 2 + s // 2, (s % 2) * CTX + j * P:(s % 2) * CTX + (j + 1) * P],
                                          z[:, 8 + j, s * P:(s + 1) * P], ident[:])
                    if s % 2:
                        mm.then_inc(sem("vt"), 1)
                sum_two(lambda j: conv[:, j, r], "conv_in")
                pe.wait_ge(sem("sg_used"), 2 * (l + 1))
                sum_squares(2, 5, r, ones[:], n)
                pe.wait_ge(sem("roped"), 5 + 4 * (l + 1))
                pe.wait_ge(sem("vtok"), 2 * (l + 1))
                pe.wait_ge(sem("var"), ncall[0])
                items = [(h, s) for h in range(4) for s in toks]
                base = item[0]

                def scores(i):
                    h, s = items[i]
                    pe.wait_ge(sem("att_e"), base + i - 1)
                    nk = CTX if s < 2 else T
                    for j in range(2):
                        b = 64 * (h % 2) + 32 * j
                        mm = pe.matmul(PS[:, 2 * (i % 2) + j, 0:nk], z[b:b + 32, 4 + h // 2, s * P:(s + 1) * P],
                                       z[b:b + 32, 6 + h // 2, 0:nk], start=True, stop=True)
                    mm.then_inc(sem("att_s"), 1)

                def values(h):
                    pe.wait_ge(sem("att_pt"), base + (h + 1) * len(toks))
                    if h == 2:
                        pe.wait_ge(sem("ot"), 2 * l + 1)
                    for c, nks in ([(slice(0, CTX), 2)] if full else []) + [(LAT, 4)]:
                        for ks in range(nks):
                            mm = pe.matmul(PS[64 * (h % 2):64 * (h % 2) + 64, 6, c], vtok[:, ks, h * 64:(h + 1) * 64],
                                           probs_t[:, ks, c], start=(ks == 0), stop=(ks == nks - 1))
                    mm.then_inc(sem("att_o"), 1)

                scores(0)
                for i, (h, s) in enumerate(items):
                    if i + 1 < len(items):
                        scores(i + 1)
                    pe.wait_ge(sem("att_p"), base + i + 1)
                    pe.wait_ge(sem("att_pt"), base + i - 1)
                    for ks in range(2 if s < 2 else 4):
                        for j in range(2):
                            mm = pe.matmul(PS[:, 4 + i % 2, ks * P:(ks + 1) * P], probs[:, i % 2, j, ks * P:(ks + 1) * P],
                                           scale_of(i, j), start=(j == 0), stop=(j == 1))
                    mm.then_inc(sem("att_t"), 1)
                    if h and s == toks[0]:
                        values(h - 1)
                values(3)
                item[0] += len(items)
                for j in range(2):
                    sum_squares(1, 5, r, drot[:, 1, :], n)
                residual_product(f"wo{l}", *hx(full), full, False, ready=[("y_lo", 8 * (l + 1))])
                feed_forward(f"g{l}", full, 5 + 2 * l)

        @block.scalar
        def _(act):
            nsplit, nsq, nsd, chain = [0], [0], [0], [0]

            def split_to(n):
                while nsplit[0] < min(n, len(UNITS)):
                    u = nsplit[0]
                    s, w = w_slot(u), A["units_width"][u]
                    act.wait_ge(sem(f"raw_in{s}"), 16 * (u // RING + 1))
                    if u >= RING:
                        act.wait_ge(sem(UNITS[u - RING][3]), UNITS[u - RING][4])
                    act.activation(w_hi[:, s, 0:w], raw[:, s, 0:w], ACT.Copy).then_inc(sem("w_hi"), 1)
                    nsplit[0] += 1

            def phase(name, evacuate):
                ph = LIN[name]
                for g in range(len(ph.groups)):
                    split_to(ph.u0 + (g + 1) * ph.nch + LEAD)
                    for m in range(ph.tpg):
                        evacuate(g * ph.tpg + m, ph.t0 + g * ph.tpg + m)

            def only_split(name):
                split_to(LIN[name].u0 + len(LIN[name].groups) * LIN[name].nch + LEAD)

            def square(ap, width):
                if nsq[0] >= 2:
                    act.wait_ge(sem("sq_used"), nsq[0] - 1)
                act.activation(SQ(nsq[0])[:, 0:width], ap, ACT.Square).then_inc(sem("sq_made"), 1)
                nsq[0] += 1

            def root(ap):
                nsd[0] += 1
                act.wait_ge(sem("var"), nsd[0])
                act.activation(ap, ap, ACT.Sqrt).then_inc(sem("sd"), 1)

            act.wait_ge(sem("consts_in"), 96)
            act.activation(cond[:].rearrange("p a b c -> p (a b c)"), cond[:].rearrange("p a b c -> p (a b c)"),
                           ACT.Silu).then_inc(sem("cond"), 1)
            split_to(RING)
            for t in range(8):
                act.wait_ge(sem("h_made"), t + 1)
                act.activation(h0_hi[:, t, :], MT[:, t, :], ACT.Copy).then_inc(sem("h_hi"), 1)

            def sigmoid_o(i, t):
                act.wait_ge(sem("tile_done"), t + 1)
                act.activation(qk[:, i, :], PS[:, t % BANKS, :], ACT.Sigmoid).then_inc(sem("free_act"), 1)

            phase("og", sigmoid_o)

            def silu_xc(i):
                act.wait_ge(sem("free_dve"), LIN["up"].free0 + i + 1)
                if i == 0:
                    act.wait_ge(sem("og_out"), 64)
                act.activation(qk[:, i, :], MT[:, i % 4, :], ACT.Silu).then_inc(sem("up_c"), 1)

            def up(i, t):
                act.wait_ge(sem("tile_done"), t + 1)
                act.activation(m_hi[:, i, :], PS[:, t % BANKS, :], ACT.Copy).then_inc(sem("up_hi"), 1)
                if i:
                    silu_xc(i - 1)

            phase("up", up)
            silu_xc(15)

            def values(i, t):
                g, s = divmod(i, 4)
                act.wait_ge(sem("tile_done"), t + 1)
                act.activation(V[:, s, g * T:(g + 1) * T], PS[:, t % BANKS, :], ACT.Copy).then_inc(sem("free_act"), 1)

            phase("v", values)
            act.wait_ge(sem("gate_w_in"), 16)
            act.activation(gate_hi[:], gate_w[:], ACT.Copy).then_inc(sem("gate_whi"), 1)
            for i in range(16):
                act.activation(m_hi[:, i, :], qk[:, i, :], ACT.Copy).then_inc(sem("xc_hi"), 1)
            act.wait_ge(sem("gate_neg"), 1)
            act.activation(gates[:, 4:6, :], gates[:, 4:6, :], ACT.Exp).then_inc(sem("gate_exp"), 1)
            act.wait_ge(sem("gate_exp"), 1)
            act.activation(gates[:, 4:6, :], gates[:, 4:6, :], ACT.Ln, bias=1.0).then_inc(sem("gate_ln"), 1)

            def q_or_k(i, t):
                act.wait_ge(sem("tile_done"), t + 1)
                if i == 0:
                    act.wait_ge(sem("xc_lo"), 16)
                act.activation(qk[:, i, :], PS[:, t % BANKS, :], ACT.Copy, scale=1.0 if i < 8 else 1.0 / 16)\
                    .then_inc(sem("free_act"), 1)

            phase("qk", q_or_k)
            act.wait_ge(sem("gate_m"), 1)
            for i, (src, func, scale) in enumerate(((2, ACT.Copy, 1.0), (3, ACT.Copy, 1.0), (4, ACT.Exp, -1.0),
                                                    (5, ACT.Exp, -1.0))):
                act.activation(rows[32 * i:32 * i + 4, :], gates[:, src, :], func, scale=scale).then_inc(sem("rows"), 1)
            for h in range(NH):
                for i in range(8):
                    d, s = divmod(i, 4)
                    lo, hi = w_span(s)
                    act.wait_ge(sem("bcast"), 4 * h + 1 + d)
                    if i == 0:
                        act.wait_ge(sem("gcol"), 1)
                        if h == 0:
                            act.wait_ge(sem("rows"), 4)
                        else:
                            act.wait_ge(sem("pv"), 4 * h)
                    act.activation(WD[:, d, lo:hi], PS[:, 3 + d, q_span(s)], ACT.Exp, bias=gcol[:, d, s, h:h + 1],
                                   scale=-1.0).then_inc(sem("expw"), 1)
                for d in range(2):
                    act.wait_ge(sem("den"), 2 * h + d + 1)
                    act.activation(RD[:, d, :], PS[:, 3 + d, :], ACT.Abs).then_inc(sem("den_abs"), 1)
                for e in range(4):
                    act.wait_ge(sem("pv_used"), 4 * h + e + 1)
                    square(og[:, 4 * h + e, :], T)
                root(RD[:, 0, :])
                for e in range(4):
                    i = 4 * h + e
                    act.wait_ge(sem("hs"), i + 1)
                    act.activation(m_hi[:, i, :], og[:, i, :], ACT.Copy).then_inc(sem("hs_hi"), 1)
            only_split("mout")

            def ln_squares(full, n):
                r = rng(full)
                for t in range(8):
                    act.wait_ge(sem("xc"), 8 * n + t + 1)
                    square(X[:, t, r], T if full else CTX)
                root(RSTD[:, r])

            def layer_norm(n, full, col, n_h):
                ln_squares(full, n)
                r = rng(full)
                for t in range(8):
                    act.wait_ge(sem("xn"), 8 * n + t + 1)
                    act.activation(X[:, t, r], X[:, t, r], ACT.Identity, bias=vec1[:, V1["ln_b"] + col + t:V1["ln_b"] + col + t + 1])\
                        .then_inc(sem("xb"), 1)
                    if n_h is not None and t:
                        hi_tile(n_h, t - 1, full)
                if n_h is not None:
                    hi_tile(n_h, 7, full)

            def hi_tile(n, t, full):
                r = rng(full)
                act.wait_ge(sem("h_made"), 8 * n + t + 1)
                act.activation(h_hi[:, t, r], TMP[:, t % 4, r], ACT.Copy).then_inc(sem("h_hi"), 1)

            def conv_ffn(tag, full):
                r = rng(full)
                for half in range(2):
                    ph = LIN[f"{tag}in{half}"]
                    split_to(ph.u0 + ph.nch + LEAD)
                    for f in range(11):
                        act.wait_ge(sem("free_dve"), ph.free0 + 2 * f + 1)
                        act.activation(TMP[:, 2 + f % 2, r], TMP[:, f % 2, r], ACT.Silu).then_inc(sem("sg"), 1)
                        split_to(ph.u0 + (f + 2) * ph.nch + LEAD)
                        act.wait_ge(sem("free_dve"), ph.free0 + 2 * f + 2)
                        act.activation(hid_hi[:, f, r], TMP[:, 4 + f % 2, r], ACT.Copy).then_inc(sem("hid_hi"), 1)
                    only_split(f"{tag}out{half}")

            def mlp(tag, full):
                r = rng(full)
                for half in range(2):
                    ph = LIN[f"{tag}in{half}"]
                    base = hid0[tag] + 16 * half

                    def hi(i):
                        act.wait_ge(sem("prod"), base - 44 + i + 1)
                        act.activation(hid_hi[:, i, r], TMP[:, 4 + i % 2, r], ACT.Copy).then_inc(sem("hid_hi"), 1)

                    def relu(i, t):
                        act.wait_ge(sem("tile_done"), t + 1)
                        if base - 44 + i >= 2:
                            act.wait_ge(sem("prod"), base - 44 + i - 1)
                        act.activation(TMP[:, i % 2, r], PS[:, t % BANKS, r], ACT.Relu).then_inc(sem("free_act"), 1)
                        if i:
                            hi(i - 1)

                    phase(f"{tag}in{half}", relu)
                    hi(15)
                    if half == 0:
                        only_split(f"{tag}out0")
                    else:
                        squares_behind(f"{tag}out1", full)

            layer_norm(0, True, 0, 1)
            conv_ffn("f0", True)
            layer_norm(1, True, 8, 2)

            def copy_to(aps, full=True):
                def evacuate(i, t):
                    act.wait_ge(sem("tile_done"), t + 1)
                    act.activation(aps(i), PS[:, t % BANKS, rng(full)], ACT.Copy).then_inc(sem("free_act"), 1)
                return evacuate

            phase("dkv", copy_to(lambda i: ckv[:, i, :]))
            for t in range(2):
                act.wait_ge(sem("free_act"), LIN["dkv"].free0 + t + 1)
                square(ckv[:, t, :], T)

            def c_hi(i):
                act.wait_ge(sem("c_made"), i + 1)
                dst, src = (ckv_hi[:, i, :], ckv[:, i, :]) if i < 2 else (cq_hi[:, i - 2, :], cq[:, i - 2, :])
                act.activation(dst, src, ACT.Copy).then_inc(sem("c_hi"), 1)

            phase("dkr", copy_to(lambda i: kr[:, :]))
            root(RSTD)
            c_hi(0)
            c_hi(1)
            phase("dq", copy_to(lambda i: cq[:, i, :], False))
            for t in range(3):
                act.wait_ge(sem("free_act"), LIN["dq"].free0 + t + 1)
                square(cq[:, t, :], CTX)
            phase("ukn", copy_to(lambda i: kn[:, i, :]))
            root(MEAN[:, 0:CTX])
            for i in (2, 3, 4):
                c_hi(i)
            phase("ukv", copy_to(lambda i: vm[:, i % 4, (i // 4) * T:(i // 4 + 1) * T]))
            phase("uqn", copy_to(lambda i: qn[:, i, :], False))
            phase("uqr", copy_to(lambda i: qr[:, i, :], False))

            def att_copy(i):
                act.wait_ge(sem("att_t"), i + 1)
                if i // 2 > 0:
                    act.wait_ge(sem("att_o"), i // 2)
                dst = TMP[:, 2:4, :].rearrange("p a (b q) -> p (a b) q", q=CTX)[:, :, (i % 2) * P:(i % 2 + 1) * P]
                act.activation(dst, PS[:, 4 + i % 2, :].rearrange("p (s q) -> p s q", s=4), ACT.Copy)\
                    .then_inc(sem("att_pt"), 1)

            def o_hi(h):
                act.wait_ge(sem("att_o"), h + 1)
                act.activation(h_hi[:, h, LAT], PS[:, 2 + h % 2, 0:CTX], ACT.Copy).then_inc(sem("o_hi"), 1)

            only_split("uqr")
            for i in range(16):
                act.wait_ge(sem("att_nb"), i + 1)
                c = 8 * (i % 2)
                act.activation(TMP[:, i % 2, :], PS[:, i % 2, :], ACT.Exp, bias=small[:, 8 + c:9 + c], scale=MLA_SCALE,
                               accum_out=small[:, 9 + c:10 + c]).then_inc(sem("att_e"), 1)
                if i:
                    att_copy(i - 1)
                if i >= 3 and i % 2:
                    o_hi((i - 3) // 2)
            att_copy(15)
            o_hi(7)
            only_split("aout")
            layer_norm(2, False, 16, 3)
            conv_ffn("f1", False)
            layer_norm(3, False, 24, None)

            def squares_behind(name, full):
                ph, r = LIN[name], rng(full)
                for g in range(5):
                    split_to(ph.u0 + min(g + 1, 4) * ph.nch + LEAD)
                    for t in (2 * g - 2, 2 * g - 1) if g else ():
                        act.wait_ge(sem("free_dve"), ph.free0 + t + 1)
                        square(X[:, t, r], T if full else CTX)

            def rms(n_h, full, chunk, par):
                r = rng(full)
                root(RSTD[:, r])
                for t in range(8):
                    act.wait_ge(sem("h_made"), 8 * n_h + t + 1)
                    for i, (c, v) in enumerate(halves(full)):
                        ins = act.activation(h_hi[:, t, c], TMP[:, t % 4, c], ACT.Identity,
                                             bias=mod[:, par, 8 * chunk + t, v:v + 1])
                    ins.then_inc(sem("h_hi"), 1)

            ny, item = [0], [16]
            for l in range(2):
                full = l == 0
                r, n = rng(full), (T if full else CTX)
                if l == 0:
                    act.wait_ge(sem("ctx2_in"), 16)
                    act.wait_ge(sem("xb"), 32)
                    for t in range(8):
                        square(X[:, t, :], T)
                rms(4 + 2 * l, True, 0, l)
                phase(f"kv{l}", copy_to(lambda i: z[:, 6 + i, :]))
                z_out = copy_to(lambda i: z[:, 2 * Z_PARTS[i // 2] + i % 2, r], full)
                z0 = LIN[f"z{l}"].free0

                def z_tile(i, t):
                    z_out(i, t)
                    if i == 4:
                        act.wait_ge(sem("free_act"), z0 + 4)
                        for j in range(2):
                            act.activation(z[:, 2 + j, r], z[:, 2 + j, r], ACT.Sigmoid).then_inc(sem("sig"), 1)
                    if i == 7:
                        act.wait_ge(sem("free_act"), z0 + 6)
                        for j in range(2):
                            act.activation(z[:, 12 + j, r], z[:, 12 + j, r], ACT.Gelu_apprx_tanh).then_inc(sem("sv_in"), 1)
                    if i == 9:
                        for j in range(2):
                            act.wait_ge(sem("n2_xc"), 4 * l + j + 1)
                            square(z[:, 12 + j, r], n)
                    if i == 10:
                        act.wait_ge(sem("lam_mm"), l + 1)
                        act.activation(small[:, 50:52], PS[:, 6, 0:2], ACT.Exp).then_inc(sem("lam_exp"), 1)
                    if i == 12:
                        root(RSTD[:, r])
                    if i == 13:
                        for j in range(2):
                            act.wait_ge(sem("sv_n"), 2 * l + j + 1)
                            b = V2["sg_ln_b_2"] + 2 * l + j
                            act.activation(z[:, 12 + j, r], z[:, 12 + j, r], ACT.Identity, bias=vec2[:, b:b + 1])\
                                .then_inc(sem("sv_done"), 1)
                    if i == 14:
                        act.wait_ge(sem("st_t"), l + 1)
                        for k in (range(2) if full else range(1, 2)):
                            ins = act.activation(stok[:, 2 * k:2 * k + 2, :].rearrange("p s e -> p (s e)"),
                                                 PS[:, (6, 4)[k], :], ACT.Copy)
                        ins.then_inc(sem("stok"), 1)
                    if i == 15:
                        act.wait_ge(sem("free_act"), z0 + 10)
                        for j in range(2):
                            act.activation(z[:, 10 + j, r], z[:, 10 + j, r], ACT.Gelu_apprx_tanh).then_inc(sem("gelu_u"), 1)

                phase(f"z{l}", z_tile)
                only_split(f"z{l}")
                for i in range(2):
                    act.wait_ge(sem("vt"), 2 * l + i + 1)
                    act.activation(vtok[:, 2 * i:2 * i + 2, :].rearrange("p s e -> p (s e)"), PS[:, 2 + i, :], ACT.Copy)\
                        .then_inc(sem("vtok"), 1)

                def y_hi(j):
                    ny[0] += 1
                    act.wait_ge(sem("y_made"), ny[0] - 2 * l - (0 if j in (4, 5) else 2))
                    act.activation(h_hi[:, j, r], TMP[:, (ny[0] - 1) % 4, r], ACT.Copy).then_inc(sem("y_hi"), 1)

                for j in range(2):
                    act.wait_ge(sem("n2_xc"), 4 * l + 2 + j + 1)
                    square(conv[:, j, r], n)
                for j in (4, 5):
                    y_hi(j)
                root(RSTD[:, r])
                for j in range(2):
                    act.wait_ge(sem("conv_n"), 2 * l + j + 1)
                    g, b = V2["ln_a_g_2"] + 2 * l + j, V2["ln_a_b_2"] + 2 * l + j
                    if ny[0] > 3:
                        act.wait_ge(sem("y_lo"), ny[0] - 3)
                    act.activation(TMP[:, ny[0] % 4, r], conv[:, j, r], ACT.Silu, bias=vec2[:, b:b + 1],
                                   scale=vec2[:, g:g + 1]).then_inc(sem("conv_y"), 1)
                    act.wait_ge(sem("conv_y"), 2 * l + j + 1)
                    ny[0] += 1
                    act.activation(h_hi[:, j, r], TMP[:, (ny[0] - 1) % 4, r], ACT.Copy).then_inc(sem("y_hi"), 1)
                toks = range(4) if full else range(2, 4)
                items = [(h, s) for h in range(4) for s in toks]
                base = item[0]

                def probs_copy(i):
                    h, s = items[i]
                    nks = 2 if s < 2 else 4
                    act.wait_ge(sem("att_t"), base + i + 1)
                    if h:
                        act.wait_ge(sem("att_o"), 8 + 4 * l + h)
                    act.activation(probs_t[:, 0:nks, s * P:(s + 1) * P],
                                   PS[:, 4 + i % 2, 0:nks * P].rearrange("p (s q) -> p s q", q=P), ACT.Copy)\
                        .then_inc(sem("att_pt"), 1)

                for i, (h, s) in enumerate(items):
                    nk = CTX if s < 2 else T
                    c = 8 + 8 * (i % 2)
                    act.wait_ge(sem("att_nb"), base + i + 1)
                    for j in range(2):
                        ins = act.activation(probs[:, i % 2, j, 0:nk], PS[:, 2 * (i % 2) + j, 0:nk], ACT.Exp,
                                             bias=small[:, c + j:c + j + 1], scale=DIFF_SCALE,
                                             accum_out=small[:, c + 2 + j:c + 3 + j])
                    ins.then_inc(sem("att_e"), 1)
                    if i:
                        probs_copy(i - 1)
                    for k in ((i,) if full else (2 * i, 2 * i + 1)):
                        if k in (3, 4):
                            y_hi(6 + k - 3)
                probs_copy(len(items) - 1)
                item[0] += len(items)
                for j in range(2):
                    act.wait_ge(sem("ot"), 2 * l + j + 1)
                    square(TMP[:, j, r], n)
                    root(RSTD[:, r])
                for j in (2, 3):
                    y_hi(j)
                squares_behind(f"wo{l}", full)
                rms(5 + 2 * l, full, 3, l)
                mlp(f"g{l}", full)
            root(RSTD[:, LAT])

        @block.vector
        def _(dve):
            nstep = [0]
            nsplit, nvar, chain, nmean, ny, natt, nmod = [0], [0], [0], [0], [0], [0], [0]

            def split_to(n):
                while nsplit[0] < min(n, len(UNITS)):
                    u = nsplit[0]
                    s, w = w_slot(u), A["units_width"][u]
                    dve.wait_ge(sem("w_hi"), u + 1)
                    dve.tensor_tensor(w_lo[:, s, 0:w], raw[:, s, 0:w], w_hi[:, s, 0:w].bitcast(F32), ALU.subtract)\
                        .then_inc(sem("w_split"), 1)
                    nsplit[0] += 1
                    for i, (at, a, k) in enumerate(ADA_MACS):
                        if at == u:
                            modulation_unit(i, a, k)

            def modulation_unit(n, a, k):
                dve.wait_ge(sem(f"ada_in{n % ADA_RING}"), 16 * (n // ADA_RING + 1))
                if k == 0:
                    dve.wait_ge(sem("ada_sum"), a - 1)
                blk, nv = a // (2 * ADA_LAYER), ada_conds(a)
                for kk in range(2):
                    w = ada_ring[:, n % ADA_RING, kk * ADA_W:(kk + 1) * ADA_W]
                    for v in range(nv):
                        acc, c = ada_acc[:, a % 2, v, :], cond[:, blk, 2 * k + kk, v:v + 1]
                        if k == 0 and kk == 0:
                            dve.tensor_scalar(acc, w, c, None, ALU.mult).then_inc(sem("ada_mac"), 1)
                        else:
                            dve.wait_ge(sem("ada_mac"), nstep[0] - nv + 1)
                            dve.scalar_tensor_tensor(out=acc, in0=w, scalar=c, in1=acc, op0=ALU.mult, op1=ALU.add)\
                                .then_inc(sem("ada_mac"), 1)
                        nstep[0] += 1

            def chained():
                chain[0] += 1
                return chain[0]

            def phase(name, evacuate):
                ph = LIN[name]
                for g in range(len(ph.groups)):
                    split_to(ph.u0 + (g + 1) * ph.nch + LEAD)
                    for m in range(ph.tpg):
                        evacuate(g * ph.tpg + m, ph.t0 + g * ph.tpg + m)

            def only_split(name):
                split_to(LIN[name].u0 + len(LIN[name].groups) * LIN[name].nch + LEAD)

            def rstd(bank, count, cols, dst, added=False):
                nvar[0] += 1
                if added:
                    nmean[0] += 1
                    dve.wait_ge(sem("xsum"), nmean[0])
                else:
                    dve.wait_ge(sem("sq_used"), nsq_after[nvar[0] - 1])
                dve.tensor_scalar(dst, PS[:, bank, cols], 1.0 / count, EPS, ALU.mult, ALU.add).then_inc(sem("var"), 1)
                dve.wait_ge(sem("sd"), nvar[0])
                dve.reciprocal(dst, dst).then_inc(sem("dve_chain"), 1)
                dve.wait_ge(sem("dve_chain"), chained())

            def mean(count, cols):
                nmean[0] += 1
                dve.wait_ge(sem("xsum"), nmean[0])
                dve.tensor_scalar(MEAN[:, cols], PS[:, 4, cols], 1.0 / count, None, ALU.mult).then_inc(sem("dve_chain"), 1)
                dve.wait_ge(sem("dve_chain"), chained())

            def modulation(layer, lo, hi, nv=2, gains=(), summed=0):
                par = layer % 2
                dve.wait_ge(sem("ada_sum"), max(ADA_LAYER * layer + hi // 2, summed))
                vec, at = (vec1, V1["ada_b"]) if layer < 2 else (vec2, V2["ada_b_2"])
                at += 48 * par
                sums = PS[:, 7, 96 * par + 2 * lo:96 * par + 2 * hi].rearrange("p (m v) -> p m v", v=2)[:, :, 0:nv]
                bias = vec[:, at + lo:at + hi].rearrange("p (m v) -> p m v", v=1).broadcast_to([P, hi - lo, nv])
                dve.tensor_tensor(mod[:, par, lo:hi, 0:nv], sums, bias, ALU.add).then_inc(sem("mod_read"), 1)
                nmod[0] += 1
                dve.wait_ge(sem("mod_read"), nmod[0])
                for chunk in (1, 4):
                    if lo <= 8 * chunk < hi:
                        scale = mod[:, par, 8 * chunk:8 * chunk + 8, 0:nv]
                        dve.tensor_scalar(scale, scale, 1.0, None, ALU.add).then_inc(sem("dve_chain"), 1)
                        dve.wait_ge(sem("dve_chain"), chained())
                        if gains:
                            g = gains[chunk // 3]
                            gain = vec2[:, g:g + 8].rearrange("p (m v) -> p m v", v=1).broadcast_to([P, 8, nv])
                            dve.tensor_tensor(scale, scale, gain, ALU.mult).then_inc(sem("dve_chain"), 1)
                            dve.wait_ge(sem("dve_chain"), chained())

            def scalar(par, chunk, t, v):
                return mod[:, par, 8 * chunk + t, v:v + 1]

            dve.wait_ge(sem("cond"), 1)
            for k in range(8):
                dve.wait_ge(sem(f"ada0_in{4 + k // 2}"), 16)
                w = qk[:].rearrange("p t n -> p (t n)")[:, k * UNIT:(k + 1) * UNIT]
                for v in range(2):
                    acc, c = first_acc[:, v * UNIT:(v + 1) * UNIT], cond[:, 0, k, v:v + 1]
                    if k == 0:
                        dve.tensor_scalar(acc, w, c, None, ALU.mult).then_inc(sem("first_scale"), 1)
                    else:
                        dve.wait_ge(sem("first_scale"), 2 * k + v - 1)
                        dve.scalar_tensor_tensor(out=acc, in0=w, scalar=c, in1=acc, op0=ALU.mult, op1=ALU.add)\
                            .then_inc(sem("first_scale"), 1)

            def first_lo(t):
                dve.wait_ge(sem("h_hi"), t + 1)
                dve.tensor_tensor(h0_lo[:, t, :], MT[:, t, :], h0_hi[:, t, :].bitcast(F32), ALU.subtract)\
                    .then_inc(sem("h_lo"), 1)

            modulation(0, 0, 16)
            split_to(1)
            dve.wait_ge(sem("x0_in"), 16)
            for t in range(8):
                for c, v in halves(True):
                    ins = dve.tensor_scalar(MT[:, t, c], MT[:, t, c], scalar(0, 1, t, v), scalar(0, 0, t, v), ALU.mult, ALU.add)
                ins.then_inc(sem("h_made"), 1)
                if t:
                    first_lo(t - 1)
            first_lo(7)
            split_to(RING)
            only_split("og")

            def segments(ap):
                return ap.rearrange("p (s n) -> p s n", n=CTX)

            def conv3(dst, src, taps, bias=None, last=None):
                d, s = segments(dst), segments(src)
                if bias is not None:
                    dve.tensor_scalar(dst, src, taps[1], bias, ALU.mult, ALU.add).then_inc(sem("dve_chain"), 1)
                    dve.wait_ge(sem("dve_chain"), chained())
                else:
                    dve.tensor_scalar(dst, src, taps[1], None, ALU.mult).then_inc(sem("dve_chain"), 1)
                    dve.wait_ge(sem("dve_chain"), chained())
                dve.scalar_tensor_tensor(out=d[:, :, 1:], in0=s[:, :, 0:CTX - 1], scalar=taps[0], in1=d[:, :, 1:],
                                         op0=ALU.mult, op1=ALU.add).then_inc(sem("dve_chain"), 1)
                dve.wait_ge(sem("dve_chain"), chained())
                ins = dve.scalar_tensor_tensor(out=d[:, :, 0:CTX - 1], in0=s[:, :, 1:], scalar=taps[2],
                                               in1=d[:, :, 0:CTX - 1], op0=ALU.mult, op1=ALU.add)
                if last:
                    ins.then_inc(sem(last), 1)
                else:
                    ins.then_inc(sem("dve_chain"), 1)
                    dve.wait_ge(sem("dve_chain"), chained())

            def col(vec, at):
                return vec[:, at:at + 1]

            def up(i, t):
                b = t % BANKS
                dve.wait_ge(sem("up_hi"), i + 1)
                dve.tensor_tensor(m_lo[:, i, :], PS[:, b, :], m_hi[:, i, :].bitcast(F32), ALU.subtract)\
                    .then_inc(sem("up_lo"), 1)
                if i == 0:
                    dve.wait_ge(sem("h_lo"), 8)
                if i - 3 > 0:
                    dve.wait_ge(sem("up_c"), i - 3)
                taps = [col(vec1, V1["m_conv_w"] + 16 * k + i) for k in range(3)]
                conv3(MT[:, i % 4, :], PS[:, b, :], taps, col(vec1, V1["m_conv_b"] + i), last="free_dve")

            phase("up", up)
            only_split("v")
            dve.wait_ge(sem("gate_whi"), 1)
            dve.tensor_tensor(gate_lo[:], gate_w[:], gate_hi[:].bitcast(F32), ALU.subtract).then_inc(sem("gate_wlo"), 1)
            for i in range(16):
                dve.wait_ge(sem("xc_hi"), i + 1)
                dve.tensor_tensor(m_lo[:, i, :], qk[:, i, :], m_hi[:, i, :].bitcast(F32), ALU.subtract)\
                    .then_inc(sem("xc_lo"), 1)
            dve.wait_ge(sem("gate_mm"), 1)
            dve.tensor_copy(gate_all[:], PS[0:16, 4, :]).then_inc(sem("gate_all"), 1)
            for q in range(4):
                dve.wait_ge(sem("gate_rows"), q + 1)
                dve.tensor_scalar(gates[:, q, :], PS[0:4, (4, 5, 6, 3)[q], :], small[0:4, q:q + 1], None, ALU.add)\
                    .then_inc(sem("gate_pre"), 1)
            dve.wait_ge(sem("gate_pre"), 4)
            dve.tensor_scalar(gates[:, 4:6, :], gates[:, 2:4, :], -1.0, None, ALU.mult).then_inc(sem("dve_chain"), 1)
            dve.wait_ge(sem("dve_chain"), chained())
            dve.tensor_tensor(gates[:, 4:6, :], gates[:, 4:6, :], gates[:, 2:4, :], ALU.min).then_inc(sem("gate_neg"), 1)
            dve.wait_ge(sem("gate_ln"), 1)
            dve.tensor_scalar(gates[:, 2:4, :], gates[:, 2:4, :], 0.0, None, ALU.min).then_inc(sem("dve_chain"), 1)
            dve.wait_ge(sem("dve_chain"), chained())
            dve.tensor_tensor(gates[:, 2:4, :], gates[:, 2:4, :], gates[:, 4:6, :], ALU.subtract)\
                .then_inc(sem("dve_chain"), 1)
            dve.wait_ge(sem("dve_chain"), chained())

            def scan(dst, src, op, backward):
                d, s = gates[:, dst, :], gates[:, src, :]
                if not backward:
                    dve.tensor_tensor_scan(d, s, s, 0.0, op, ALU.bypass).then_inc(sem("dve_chain"), 1)
                    dve.wait_ge(sem("dve_chain"), chained())
                    return
                dve.tensor_tensor_scan(d[:, 0:CTX][:, ::-1], s[:, 0:CTX][:, ::-1], s[:, 0:CTX][:, ::-1], 0.0, op, ALU.bypass)\
                    .then_inc(sem("dve_chain"), 1)
                dve.wait_ge(sem("dve_chain"), chained())
                dve.tensor_tensor_scan(d[:, LAT][:, ::-1], s[:, LAT][:, ::-1], s[:, LAT][:, ::-1], d[:, 0:1], op, ALU.bypass)\
                    .then_inc(sem("dve_chain"), 1)
                dve.wait_ge(sem("dve_chain"), chained())

            scan(4, 2, ALU.add, False)
            scan(5, 3, ALU.add, True)
            dve.tensor_tensor(gates[:, 0:2, :], gates[:, 0:2, :], gates[:, 4:6, :], ALU.subtract).then_inc(sem("gate_g"), 1)
            dve.wait_ge(sem("gate_g"), 1)
            scan(2, 0, ALU.max, False)
            scan(3, 1, ALU.max, True)
            dve.tensor_tensor(gates[:, 4:6, :], gates[:, 4:6, :], gates[:, 2:4, :], ALU.add).then_inc(sem("gate_m"), 1)
            only_split("qk")
            modulation(0, 16, 48, summed=summed_before("mout"))
            dve.wait_ge(sem("gcol_t"), 1)
            dve.tensor_copy(small[:, 8:40], PS[:, 4, 0:32]).then_inc(sem("gcol"), 1)
            dve.wait_ge(sem("gcol"), 1)
            dve.wait_ge(sem("rows"), 4)
            def heads_lo(h):
                for e in range(4):
                    i = 4 * h + e
                    dve.wait_ge(sem("hs_hi"), i + 1)
                    dve.tensor_tensor(m_lo[:, i, :], og[:, i, :], m_hi[:, i, :].bitcast(F32), ALU.subtract)\
                        .then_inc(sem("hs_lo"), 1)

            for h in range(NH):
                for d in range(2):
                    for s in range(4):
                        lo, hi = w_span(s)
                        dve.wait_ge(sem("expw"), 8 * h + 4 * d + s + 1)
                        dve.wait_ge(sem("scores"), 4 * h + (s + 1 if s < 2 else 4))
                        score = PS[:, s, :] if s < 2 else PS[:, 2, (s - 2) * CTX:(s - 1) * CTX]
                        dve.scalar_tensor_tensor(out=WD[:, d, lo:hi], in0=WD[:, d, lo:hi], scalar=1.0, in1=score,
                                                 op0=ALU.min, op1=ALU.mult).then_inc(sem("wraw"), 1)
                dve.wait_ge(sem("bcast"), 4 * h + 4)
                for d in range(2):
                    dve.wait_ge(sem("den_abs"), 2 * h + d + 1)
                    dve.tensor_tensor(RD[:, d, :], RD[:, d, :], PS[:, 5 + d, :], ALU.max).then_inc(sem("dve_chain"), 1)
                    dve.wait_ge(sem("dve_chain"), chained())
                    dve.reciprocal(RD[:, d, :], RD[:, d, :]).then_inc(sem("dve_chain"), 1)
                    dve.wait_ge(sem("dve_chain"), chained())
                for s in range(4):
                    lo, hi = w_span(s)
                    dve.tensor_tensor(WD[:, 0, lo:hi], WD[:, 0, lo:hi], RD[:, 0, q_span(s)], ALU.mult)
                    dve.tensor_tensor(WD[:, 1, lo:hi], WD[:, 1, lo:hi], RD[:, 1, q_span(s)], ALU.mult)\
                        .then_inc(sem("dve_chain"), 1)
                    dve.wait_ge(sem("dve_chain"), chained())
                    dve.tensor_tensor(WD[:, 0, lo:hi], WD[:, 0, lo:hi], WD[:, 1, lo:hi], ALU.add).then_inc(sem("wsum"), 1)
                if h:
                    heads_lo(h - 1)
                dve.wait_ge(sem("og_in"), 16)
                for e in range(4):
                    i = 4 * h + e
                    dve.wait_ge(sem("pv"), i + 1)
                    dve.tensor_tensor(og[:, i, :], og[:, i, :], PS[:, (0, 1, 2, 5)[e], :], ALU.mult).then_inc(sem("pv_used"), 1)
                rstd(6, T, slice(0, T), RD[:, 0, :])
                for e in range(4):
                    i = 4 * h + e
                    dve.scalar_tensor_tensor(out=og[:, i, :], in0=og[:, i, :], scalar=col(vec1, V1["m_norm_g"] + i),
                                             in1=RD[:, 0, :], op0=ALU.mult, op1=ALU.mult).then_inc(sem("hs"), 1)
            heads_lo(NH - 1)
            dve.wait_ge(sem("x_in"), 16)
            dve.tensor_scalar(X[:, :, :], X[:, :, :], ALPHA, None, ALU.mult).then_inc(sem("dve_chain"), 1)
            dve.wait_ge(sem("dve_chain"), chained())

            nacc = [0]

            def residual(name, full, par, chunk, adds=None):
                r = rng(full)
                sq0 = nsq_after[nvar[0]] - 8

                def add_tile(i):
                    dve.wait_ge(sem("free_dve"), LIN[name].free0 + i + 1)
                    if i > 1:
                        dve.wait_ge(sem("tiles_added"), nacc[0])
                    first = X[:, 0, r] if i == 1 else MEAN[:, r]
                    dve.tensor_tensor(MEAN[:, r], first, X[:, i, r], ALU.add).then_inc(sem("tiles_added"), 1)
                    nacc[0] += 1

                def add_square(i):
                    dve.wait_ge(sem("sq_made"), sq0 + i + 1)
                    if i > 1:
                        dve.wait_ge(sem("sq_used"), sq0 + i)
                    n = r.stop - r.start
                    first = SQ(sq0)[:, 0:n] if i == 1 else RSTD[:, r]
                    dve.tensor_tensor(RSTD[:, r], first, SQ(sq0 + i)[:, 0:n], ALU.add)\
                        .then_inc(sem("sq_used"), 2 if i == 1 else 1)

                def evacuate(i, t):
                    dve.wait_ge(sem("tile_done"), t + 1)
                    if LIN[name].free0 + i >= 8:
                        dve.wait_ge(sem("free_dve"), LIN[name].free0 + i)
                    for c, v in halves(full):
                        ins = dve.scalar_tensor_tensor(out=X[:, i, c], in0=PS[:, t % BANKS, c], scalar=scalar(par, chunk, i, v),
                                                       in1=X[:, i, c], op0=ALU.mult, op1=ALU.add)
                    ins.then_inc(sem("free_dve"), 1)
                    if adds == "tiles" and i:
                        add_tile(i)
                    if adds == "squares" and i > 2:
                        add_square(i - 2)

                phase(name, evacuate)
                if adds == "squares":
                    add_square(6)
                    add_square(7)

            residual("mout", True, 0, 2, "tiles")

            def h_lo_tile(n, t, full):
                r = rng(full)
                dve.wait_ge(sem("h_hi"), 8 * n + t + 1)
                dve.tensor_tensor(h_lo[:, t, r], TMP[:, t % 4, r], h_hi[:, t, r].bitcast(F32), ALU.subtract)\
                    .then_inc(sem("h_lo"), 1)

            def layer_norm(n, full, gcol_at, n_h):
                r = rng(full)
                mean(D, r)
                for t in range(8):
                    dve.tensor_tensor(X[:, t, r], X[:, t, r], MEAN[:, r], ALU.subtract).then_inc(sem("xc"), 1)
                rstd(5, D, r, RSTD[:, r])
                for t in range(8):
                    dve.scalar_tensor_tensor(out=X[:, t, r], in0=X[:, t, r], scalar=col(vec1, V1["ln_g"] + gcol_at + t),
                                             in1=RSTD[:, r], op0=ALU.mult, op1=ALU.mult).then_inc(sem("xn"), 1)
                    if n_h is not None and t > 1:
                        h_lo_tile(n_h, t - 2, full)
                if n_h is not None:
                    h_lo_tile(n_h, 6, full)
                    h_lo_tile(n_h, 7, full)

            def conv_ffn(tag, layer, full):
                r = rng(full)
                dve.wait_ge(sem("h_made"), 16 if full else 32)
                dve.tensor_scalar(X[:, :, r], X[:, :, r], ALPHA, None, ALU.mult).then_inc(sem("dve_chain"), 1)
                dve.wait_ge(sem("dve_chain"), chained())
                for half in range(2):
                    ph = LIN[f"{tag}in{half}"]
                    base = hid0[tag] + 11 * half

                    def lo(f):
                        dve.wait_ge(sem("hid_hi"), base + f + 1)
                        dve.tensor_tensor(hid_lo[:, f, r], TMP[:, 4 + f % 2, r], hid_hi[:, f, r].bitcast(F32), ALU.subtract)\
                            .then_inc(sem("hid_lo"), 1)

                    split_to(ph.u0 + ph.nch + LEAD)
                    for f in range(11):
                        tile = 11 * half + f
                        t = ph.t0 + 2 * f
                        taps = [col(vec1, V1["ffn_conv_w"] + (3 * layer + k) * FFN_T + tile) for k in range(3)]
                        bias = col(vec1, V1["ffn_conv_b"] + layer * FFN_T + tile)
                        dve.wait_ge(sem("tile_done"), t + 1)
                        if base + f - 1 > 0:
                            dve.wait_ge(sem("sg"), base + f - 1)
                        conv3(TMP[:, f % 2, r], PS[:, t % BANKS, r], taps, bias, last="free_dve")
                        if f:
                            lo(f - 1)
                        split_to(ph.u0 + (f + 2) * ph.nch + LEAD)
                        dve.wait_ge(sem("tile_done"), t + 2)
                        dve.wait_ge(sem("sg"), base + f + 1)
                        if base + f - 1 > 0:
                            dve.wait_ge(sem("hid_lo"), base + f - 1)
                        dve.tensor_tensor(TMP[:, 4 + f % 2, r], TMP[:, 2 + f % 2, r], PS[:, (t + 1) % BANKS, r], ALU.mult)\
                            .then_inc(sem("free_dve"), 1)
                    lo(10)
                    residual(f"{tag}out{half}", full, layer, 5, "tiles" if half else None)

            layer_norm(0, True, 0, 1)
            conv_ffn("f0", 0, True)
            modulation(1, 0, 16, summed=summed_before("dkv"))
            modulation(1, 16, 48, 1, summed=summed_before("dkv"))
            layer_norm(1, True, 8, 2)
            dve.tensor_scalar(X[:, :, LAT], X[:, :, LAT], ALPHA, None, ALU.mult).then_inc(sem("dve_chain"), 1)
            dve.wait_ge(sem("dve_chain"), chained())
            only_split("dkv")
            only_split("dkr")
            rstd(5, CTX, slice(0, T), RSTD)

            def c_lo(i):
                dve.wait_ge(sem("c_hi"), i + 1)
                dst, src, hi = (ckv_lo, ckv, ckv_hi) if i < 2 else (cq_lo, cq, cq_hi)
                j = i if i < 2 else i - 2
                dve.tensor_tensor(dst[:, j, :], src[:, j, :], hi[:, j, :].bitcast(F32), ALU.subtract).then_inc(sem("c_lo"), 1)

            for t in range(2):
                dve.scalar_tensor_tensor(out=ckv[:, t, :], in0=ckv[:, t, :], scalar=col(vec1, V1["a_kv_norm"] + t),
                                         in1=RSTD, op0=ALU.mult, op1=ALU.mult).then_inc(sem("c_made"), 1)
            c_lo(0)
            c_lo(1)
            only_split("dq")
            only_split("ukn")
            rstd(5, 3 * P, slice(0, CTX), MEAN[:, 0:CTX])
            for t in range(3):
                dve.scalar_tensor_tensor(out=cq[:, t, :], in0=cq[:, t, :], scalar=col(vec1, V1["a_q_norm"] + t),
                                         in1=MEAN[:, 0:CTX], op0=ALU.mult, op1=ALU.mult).then_inc(sem("c_made"), 1)
            for i in (2, 3, 4):
                c_lo(i)
            for name in ("ukv", "uqn", "uqr"):
                only_split(name)

            def rotate(i, n, n0, ap, table, bank):
                dve.wait_ge(sem("rot"), n0 + min(i // 2 * 2 + 2, n))
                tmp = TMP[:, i, 0:CTX]
                dve.tensor_tensor(tmp, PS[:, bank + i // 2, (i % 2) * CTX:(i % 2 + 1) * CTX], table[:, 1, :], ALU.mult)
                dve.tensor_tensor(ap, ap, table[:, 0, :], ALU.mult).then_inc(sem("dve_chain"), 1)
                dve.wait_ge(sem("dve_chain"), chained())
                dve.tensor_tensor(ap, ap, tmp, ALU.add).then_inc(sem("roped"), 1)

            for i in range(5):
                rotate(i, 5, 0, kr[:, LAT] if i == 4 else qr[:, i, :], arope, 4)
            dve.wait_ge(sem("roped"), 5)

            def mla_probs(i):
                c = 8 * (i % 2)
                dve.wait_ge(sem("att_e"), i + 1)
                dve.reciprocal(small[:, 11 + c:12 + c], small[:, 9 + c:10 + c]).then_inc(sem("dve_chain"), 1)
                dve.wait_ge(sem("dve_chain"), chained())
                dve.tensor_scalar(scale_of(i, 0), ident[:], small[:, 11 + c:12 + c], None, ALU.mult)\
                    .then_inc(sem("att_p"), 1)

            def o_lo(h):
                dve.wait_ge(sem("o_hi"), h + 1)
                dve.tensor_tensor(h_lo[:, h, LAT], PS[:, 2 + h % 2, 0:CTX], h_hi[:, h, LAT].bitcast(F32), ALU.subtract)\
                    .then_inc(sem("o_lo"), 1)

            for i in range(16):
                c = 8 * (i % 2)
                dve.wait_ge(sem("att_s"), i + 1)
                dve.tensor_reduce(small[:, 10 + c:11 + c], PS[:, i % 2, :], AX_X, ALU.max).then_inc(sem("dve_chain"), 1)
                dve.wait_ge(sem("dve_chain"), chained())
                dve.tensor_scalar(small[:, 8 + c:9 + c], small[:, 10 + c:11 + c], -MLA_SCALE, None, ALU.mult)\
                    .then_inc(sem("att_nb"), 1)
                mla_probs(i)
                if i >= 3 and i % 2:
                    o_lo((i - 3) // 2)
            o_lo(7)
            residual("aout", False, 1, 2, "tiles")
            layer_norm(2, False, 16, 3)
            conv_ffn("f1", 1, False)
            dve.wait_ge(sem("vec2_in"), 16)
            modulation(2, 0, 48, gains=(V2["norm1_g_2"], V2["norm2_g_2"]), summed=summed_before("kv0"))
            layer_norm(3, False, 24, None)

            def rms(n_h, full, par, chunk):
                r = rng(full)
                rstd(5, D, r, RSTD[:, r], added=n_h > 4)

                def lo(t):
                    dve.wait_ge(sem("h_hi"), 8 * n_h + t + 1)
                    for c, v in halves(full):
                        ins = dve.scalar_tensor_tensor(out=h_lo[:, t, c], in0=TMP[:, t % 4, c], scalar=scalar(par, chunk, t, v),
                                                       in1=h_hi[:, t, c].bitcast(F32), op0=ALU.add, op1=ALU.subtract)
                    ins.then_inc(sem("h_lo"), 1)

                for t in range(8):
                    if t >= 4:
                        dve.wait_ge(sem("h_lo"), 8 * n_h + t - 3)
                    for c, v in halves(full):
                        ins = dve.scalar_tensor_tensor(out=TMP[:, t % 4, c], in0=X[:, t, c], scalar=scalar(par, chunk + 1, t, v),
                                                       in1=RSTD[:, c], op0=ALU.mult, op1=ALU.mult)
                    ins.then_inc(sem("h_made"), 1)
                    if t:
                        lo(t - 1)
                lo(7)

            def mlp(tag, full, par):
                r = rng(full)
                for half in range(2):
                    name = f"{tag}in{half}"
                    base = hid0[tag] + 16 * half

                    def lo(i):
                        dve.wait_ge(sem("hid_hi"), base + i + 1)
                        dve.tensor_tensor(hid_lo[:, i, r], TMP[:, 4 + i % 2, r], hid_hi[:, i, r].bitcast(F32), ALU.subtract)\
                            .then_inc(sem("hid_lo"), 1)

                    def square_relu(i, t):
                        dve.wait_ge(sem("free_act"), LIN[name].free0 + i + 1)
                        dve.wait_ge(sem("hid_lo"), base + i - 1)
                        dve.tensor_tensor(TMP[:, 4 + i % 2, r], TMP[:, i % 2, r], TMP[:, i % 2, r], ALU.mult)\
                            .then_inc(sem("prod"), 1)
                        if i:
                            lo(i - 1)

                    phase(name, square_relu)
                    lo(15)
                    residual(f"{tag}out{half}", full, par, 5, "squares" if half else None)

            natt[0] = 16
            for l in range(2):
                full = l == 0
                r, n = rng(full), (T if full else CTX)
                toks = range(4) if full else range(2, 4)
                if l:
                    gains = (V2["norm1_g_2"] + 8, V2["norm2_g_2"] + 8)
                    modulation(3, 0, 16, gains=gains)
                    modulation(3, 16, 48, 1, gains)
                rms(4 + 2 * l, True, l, 0)
                only_split(f"kv{l}")
                zp = LIN[f"z{l}"]
                z0 = zp.free0
                seqs = slice(0, 2) if full else slice(1, 2)

                def gated_linear_unit():
                    dve.memset(glu[:].rearrange("p j s n -> p (j s n)"), 0.0).then_inc(sem("dve_chain"), 1)
                    dve.wait_ge(sem("dve_chain"), chained())
                    dve.wait_ge(sem("sig"), 2 * (l + 1))
                    for j in range(2):
                        ins = dve.tensor_tensor(glu[:, j, seqs, 15:15 + CTX], segments(z[:, j, r]), segments(z[:, 2 + j, r]),
                                                ALU.mult)
                    ins.then_inc(sem("dve_chain"), 1)
                    dve.wait_ge(sem("dve_chain"), chained())

                def tap(k, j):
                    dst, src = segments(conv[:, j, r]), glu[:, j, seqs, k:k + CTX]
                    w = col(vec2, V2["conv_a_w_2"] + (31 * l + k) * 2 + j)
                    if k == 0:
                        ins = dve.tensor_scalar(dst, src, w, col(vec2, V2["conv_a_b_2"] + 2 * l + j), ALU.mult, ALU.add)
                    else:
                        dve.wait_ge(sem("tap"), 60 * l + 2 * k + j - 1)
                        ins = dve.scalar_tensor_tensor(out=dst, in0=src, scalar=w, in1=dst, op0=ALU.mult, op1=ALU.add)
                    ins.then_inc(sem("tap" if k < 30 else "conv_in"), 1)

                lam_init = 0.8 - 0.6 * math.exp(-0.3 * l)
                taps = [(k, j) for k in range(31) for j in range(2)]
                for g in range(len(zp.groups)):
                    split_to(zp.u0 + (g + 1) * zp.nch + LEAD)
                    if g == 2:
                        gated_linear_unit()
                        a = 56 + 4 * l
                        dve.tensor_tensor(small[0:32, 48:50], small[0:32, a:a + 2], small[0:32, a + 2:a + 4], ALU.mult)\
                            .then_inc(sem("lam_prod"), 1)
                    if g == 4:
                        mean(CTX, r)
                        for j in range(2):
                            dve.tensor_tensor(z[:, 12 + j, r], z[:, 12 + j, r], MEAN[:, r], ALU.subtract)\
                                .then_inc(sem("n2_xc"), 1)
                    if g == 5:
                        dve.wait_ge(sem("lam_exp"), l + 1)
                        dve.tensor_tensor(small[:, 52:53], small[:, 51:52], small[:, 50:51], ALU.subtract)\
                            .then_inc(sem("dve_chain"), 1)
                        dve.wait_ge(sem("dve_chain"), chained())
                        dve.tensor_scalar(small[:, 53:54], small[:, 52:53], -lam_init, None, ALU.add).then_inc(sem("lam"), 1)
                        dve.tensor_scalar(small[:, 54:55], col(vec2, V2["subln_g_2"] + l), 1.0 - lam_init, None, ALU.mult)\
                            .then_inc(sem("dve_chain"), 1)
                        dve.wait_ge(sem("dve_chain"), chained())
                    if g == 6:
                        rstd(5, CTX, r, RSTD[:, r])
                        for j in range(2):
                            gain = col(vec2, V2["sg_ln_g_2"] + 2 * l + j)
                            dve.scalar_tensor_tensor(out=z[:, 12 + j, r], in0=z[:, 12 + j, r], scalar=gain, in1=RSTD[:, r],
                                                     op0=ALU.mult, op1=ALU.mult).then_inc(sem("sv_n"), 1)
                    if g >= 2:
                        for k, j in taps[:CONV_TAPS]:
                            tap(k, j)
                        taps = taps[CONV_TAPS:]
                for k, j in taps:
                    tap(k, j)
                dve.wait_ge(sem("free_act"), z0 + 16)
                for i in range(4):
                    rotate(i, 4, 5 + 4 * l, z[:, 4 + i, LAT], drope, 0)
                mean(CTX, r)
                for j in range(2):
                    dve.tensor_tensor(conv[:, j, r], conv[:, j, r], MEAN[:, r], ALU.subtract).then_inc(sem("n2_xc"), 1)

                def y_slot():
                    if ny[0] - 3 > 0:
                        dve.wait_ge(sem("y_lo"), ny[0] - 3)
                    ny[0] += 1
                    return TMP[:, (ny[0] - 1) % 4, r]

                def y_lo(j, at):
                    dve.wait_ge(sem("y_hi"), at)
                    dve.tensor_tensor(h_lo[:, j, r], TMP[:, (at - 1) % 4, r], h_hi[:, j, r].bitcast(F32), ALU.subtract)\
                        .then_inc(sem("y_lo"), 1)

                dve.wait_ge(sem("roped"), 5 + 4 * (l + 1))
                for j in range(2):
                    dve.wait_ge(sem("sg_mm"), 2 * l + j + 1)
                    dve.wait_ge(sem("gelu_u"), 2 * l + j + 1)
                    out = y_slot()
                    bias = sgb[:, j, :].rearrange("p (c q) -> p c q", c=1).broadcast_to([P, n // P, P])
                    dve.tensor_tensor(out.rearrange("p (c q) -> p c q", q=P), PS[:, 5 + j, r].rearrange("p (c q) -> p c q", q=P),
                                      bias, ALU.add).then_inc(sem("sg_used"), 1)
                    dve.wait_ge(sem("sg_used"), 2 * l + j + 1)
                    dve.tensor_tensor(out, out, z[:, 10 + j, r], ALU.mult).then_inc(sem("y_made"), 1)
                rstd(5, CTX, r, RSTD[:, r])
                for j in range(2):
                    dve.tensor_tensor(conv[:, j, r], conv[:, j, r], RSTD[:, r], ALU.mult).then_inc(sem("conv_n"), 1)
                for j in range(2):
                    y_lo(4 + j, 8 * l + 1 + j)
                    ny[0] += 1

                def short_conv(j):
                    out = y_slot()
                    dve.tensor_tensor(z[:, 16 + j, r], z[:, 16 + j, r], z[:, 18 + j, r], ALU.mult)\
                        .then_inc(sem("dve_chain"), 1)
                    dve.wait_ge(sem("dve_chain"), chained())
                    conv3(out, z[:, 16 + j, r], [col(vec2, V2["conv_d_w_2"] + (3 * l + k) * 2 + j) for k in range(3)])
                    dve.tensor_tensor(out, out, z[:, 14 + j, r], ALU.mult).then_inc(sem("y_made"), 1)

                def between_items(k):
                    if k in (0, 1):
                        y_lo(k, 8 * l + 3 + k)
                    if k in (2, 3):
                        short_conv(k - 2)
                    if k in (5, 6):
                        y_lo(6 + k - 5, 8 * l + k)

                items = [(h, s) for h in range(4) for s in toks]
                base = natt[0]

                def probabilities(i):
                    h, s = items[i]
                    nk, c = (CTX if s < 2 else T), 8 + 8 * (i % 2)
                    dve.wait_ge(sem("att_e"), base + i + 1)
                    dve.reciprocal(small[:, c + 6:c + 8], small[:, c + 2:c + 4]).then_inc(sem("dve_chain"), 1)
                    dve.wait_ge(sem("dve_chain"), chained())
                    dve.tensor_tensor(small[:, c + 7:c + 8], small[:, c + 7:c + 8], small[:, 53:54], ALU.mult)\
                        .then_inc(sem("dve_chain"), 1)
                    dve.wait_ge(sem("dve_chain"), chained())
                    dve.tensor_scalar(scale_of(i, 0), ident[:], small[:, c + 6:c + 7], None, ALU.mult)
                    dve.tensor_scalar(scale_of(i, 1), ident[:], small[:, c + 7:c + 8], None, ALU.mult)\
                        .then_inc(sem("att_p"), 1)

                def out_tile(j):
                    dve.wait_ge(sem("att_o"), 8 + 4 * l + 2 * j + 2)
                    dve.tensor_copy(TMP[:, j, r], PS[:, 6, r]).then_inc(sem("ot"), 1)

                for i, (h, s) in enumerate(items):
                    nk, c = (CTX if s < 2 else T), 8 + 8 * (i % 2)
                    dve.wait_ge(sem("att_s"), base + i + 1)
                    for j in range(2):
                        ins = dve.tensor_reduce(small[:, c + 4 + j:c + 5 + j], PS[:, 2 * (i % 2) + j, 0:nk], AX_X, ALU.max)
                    ins.then_inc(sem("dve_chain"), 1)
                    dve.wait_ge(sem("dve_chain"), chained())
                    dve.tensor_scalar(small[:, c:c + 2], small[:, c + 4:c + 6], -DIFF_SCALE, None, ALU.mult).then_inc(sem("att_nb"), 1)
                    probabilities(i)
                    for k in ((i,) if full else (2 * i, 2 * i + 1)):
                        between_items(k)
                    if h == 2 and i == 2 * len(toks) + 1:
                        dve.wait_ge(sem("y_lo"), 8 * l + 6)
                        out_tile(0)
                out_tile(1)
                natt[0] += len(items)
                for j in range(2):
                    rstd(5, 64, r, RSTD[:, r])
                    out = y_slot()
                    dve.scalar_tensor_tensor(out=out, in0=TMP[:, j, r], scalar=small[:, 54:55], in1=RSTD[:, r],
                                             op0=ALU.mult, op1=ALU.mult).then_inc(sem("y_made"), 1)
                    dve.wait_ge(sem("y_made"), 6 * l + 5 + j)
                for j in range(2):
                    y_lo(2 + j, 8 * l + 7 + j)
                residual(f"wo{l}", full, l, 2, "squares")
                rms(5 + 2 * l, full, l, 3)
                mlp(f"g{l}", full, l)
            rstd(5, D, LAT, RSTD[:, LAT], added=True)
            for t in range(8):
                dve.scalar_tensor_tensor(out=X[:, t, LAT], in0=X[:, t, LAT], scalar=col(vec2, V2["final_g_2"] + t),
                                         in1=RSTD[:, LAT], op0=ALU.mult, op1=ALU.mult).then_inc(sem("final"), 1)



def tiles_of(a):
    return np.ascontiguousarray(a.T.reshape(-1, P, a.shape[0]).transpose(1, 0, 2))


def columns_of(arrays, spec):
    return np.ascontiguousarray(np.concatenate([arrays[name].reshape(-1, P) for name, _ in spec]).T)


def rope_tables(blocks, freqs):
    n = len(freqs)
    pos = np.arange(CTX)
    out = np.zeros((P, 2, CTX), np.float32)
    for p in range(P):
        j = p % (4 * n)
        at = (pos // 64 if j < 2 * n else pos % 64).astype(np.float32)
        angle = at * np.float32(freqs[j % n])
        out[p, 0], out[p, 1] = np.cos(angle), np.sin(angle)
    return out


def rotation(half):
    r = np.zeros((P, P), np.float32)
    for p in range(P):
        if p % (2 * half) < half:
            r[p + half, p] = -1.0
            r[p, p + half] = 1.0
    return r


def kernel(**inputs):
    import concourse.bacc as bacc
    from concourse.bass_utils import run_bass_kernel_spmd as run

    a = {k: np.asarray(v) for k, v in inputs.items()}
    weights = np.zeros((len(UNITS), P, UNIT), np.float32)
    widths = []
    for u, (ph, g, c, _, _) in enumerate(UNITS):
        src = a[ph.source[0]][ph.source[1]] if isinstance(ph.source, tuple) else a[ph.source][0]
        ks = ph.chunks[c]
        k0 = (ph.row0 + ks[0]) * P
        part = src[k0:k0 + len(ks) * P][:, ph.groups[g]].reshape(len(ks), P, -1).transpose(1, 0, 2)
        widths.append(part.shape[1] * part.shape[2])
        weights[u, :, :widths[-1]] = part.reshape(P, -1)
    ada = np.concatenate([a[n][l].reshape(ADA_KS, 2, P, ADA_LAYER, ADA_W).transpose(3, 0, 2, 1, 4)
                          for n in ("ada_w", "ada_w_2") for l in range(2)])
    shift, scale = a["ada_w"][0][:, :D], a["ada_w"][0][:, D:2 * D]
    ada0 = np.concatenate([shift.reshape(8, P, 4, 2, P).transpose(2, 1, 3, 0, 4).reshape(4, P, 2 * UNIT),
                           scale.reshape(4, 2, P, UNIT).transpose(0, 2, 1, 3).reshape(4, P, 2 * UNIT)])
    sub = a["subln_g_2"]
    vecs = dict(a, subln_g_2=np.concatenate([sub, sub], axis=1))
    cond = np.stack([np.stack([a["c" + s].reshape(8, P), a["c_ctx" + s].reshape(8, P)]) for s in ("", "_2")])
    block_ones = np.zeros((P, P), np.float32)
    block_ones[0:64, 0:64] = block_ones[64:, 64:] = 1.0
    arrays = {
        "weights": weights,
        "ada": np.ascontiguousarray(ada[ADA0:].reshape(-1, P, 2 * ADA_W)),
        "ada0": np.ascontiguousarray(ada0),
        "cond": np.ascontiguousarray(cond.transpose(3, 0, 2, 1)),
        "ones": np.ones((P, P), np.float32),
        "ident": np.eye(P, dtype=np.float32),
        "vec1": columns_of(vecs, VEC1_SPEC),
        "vec2": columns_of(vecs, VEC2_SPEC),
        "bg": np.ascontiguousarray(a["m_b_gates"][0].reshape(2, 2, 4).transpose(2, 1, 0).reshape(4, 4)),
        "lam": np.ascontiguousarray(np.stack([a["lam_q1_2"], a["lam_q2_2"], a["lam_k1_2"], a["lam_k2_2"]], axis=1)
                                    .reshape(8, 32).T),
        "x0": tiles_of(np.concatenate([a["ctx"][0], a["x"][0]])),
        "ctx2": tiles_of(a["ctx_2"][0]),
        "gate_w": np.ascontiguousarray(a["m_w_gates"][0].transpose(1, 0, 2).reshape(16, P, 16).transpose(1, 0, 2)
                                       .reshape(P, 256)),
        "arope": rope_tables(2, np.float32(10000.0) ** (-np.arange(16, dtype=np.float32) / 16)),
        "arot": rotation(16),
        "drope": rope_tables(4, np.float32(10000.0) ** (-np.arange(0, 16, 2, dtype=np.float32) / 16)),
        "drot": np.ascontiguousarray(np.stack([rotation(8), block_ones], axis=1)),
        "sgw": np.ascontiguousarray(a["sg_w_2"].transpose(0, 3, 1, 2)),
        "sgb": a["sg_b_2"],
    }
    nc = bacc.Bacc("TRN2", target_bir_lowering=False, num_devices=1)
    A = {"units_width": widths}
    in_map = {}
    for name, array in arrays.items():
        in_map[f"in_{name}"] = array
        A[name] = nc.dram_tensor(f"in_{name}", array.shape, F32, kind="ExternalInput").ap()
    A["og_spill"] = nc.dram_tensor("og_spill", (P, 16, T), F32, kind="Internal").ap()
    A["out"] = nc.dram_tensor("out_0", (P, 8, CTX), F32, kind="ExternalOutput").ap()
    two_stacks(nc, A)
    out = run(nc, [in_map], core_ids=[0]).results[0]["out_0"]
    return np.ascontiguousarray(out.transpose(2, 1, 0).reshape(1, CTX, D))
```
